# Optimizing a Trainium2 kernel written in Bass

```python
import jax, jax.numpy as jnp
from jax import lax
import numpy as np

D_MODEL = 2048
BATCH = 1
SEQ = 1024
DEPTH = 1
DEC_BATCH = 8
DEC_SEQ = 16
PAST_LEN = 256

CHUNK = 64
EPS = 1e-6
HEADS_A = 8
KV_HEADS_A = 2
GROUP_A = HEADS_A // KV_HEADS_A
HEAD_DIM_A = 128
IDX_HEADS = 16
IDX_DIM = 64
TOPK_MAX = 256
Q_BLOCK = 128
HEADS_B = 8
DK_B = 128
DV_B = 128
CONV_W = 4
WIDTH_A = HEADS_A * HEAD_DIM_A
KV_WIDTH_A = KV_HEADS_A * HEAD_DIM_A
WIDTH_B = HEADS_B * DV_B
QKV_B = HEADS_B * (2 * DK_B + DV_B)
D_MIX = WIDTH_A + WIDTH_B
PROJ_SIZES = (WIDTH_A, KV_WIDTH_A, KV_WIDTH_A, WIDTH_A, IDX_HEADS * IDX_DIM, IDX_DIM, IDX_HEADS,
              QKV_B, WIDTH_B, HEADS_B, HEADS_B)
PROJ_TOTAL = sum(PROJ_SIZES)
IDX_SCALE = (IDX_HEADS * IDX_DIM) ** -0.5

kernel_name = 'dsa_gated_deltanet_parallel_stream'

def _rmsnorm(x, w):
    xf = x.astype(jnp.float32)
    xf = xf * lax.rsqrt(jnp.mean(xf * xf, axis=-1, keepdims=True) + EPS)
    return (xf * w.astype(jnp.float32)).astype(x.dtype)

def _l2norm(x):
    xf = x.astype(jnp.float32)
    return xf * lax.rsqrt(jnp.sum(xf * xf, axis=-1, keepdims=True) + EPS)

def _alibi_slopes():
    s = [2.0 ** (-8.0 * (i + 1) / HEADS_A) for i in range(HEADS_A)]
    return jnp.asarray(s, dtype=jnp.float32).reshape(KV_HEADS_A, GROUP_A)

def _split_proj(p):
    offs = np.cumsum(PROJ_SIZES)[:-1].tolist()
    return jnp.split(p, offs, axis=-1)

def _dsa_block(qb, qib, wb, posb, k_all, v_all, ki_all, topk, slopes):
    B = qb.shape[0]
    L = k_all.shape[1]
    kpos = jnp.arange(L, dtype=jnp.int32)
    allowed = (kpos[None, :] // CHUNK) <= (posb[:, None] // CHUNK)
    rel = jnp.einsum('bqhd,bsd->bqhs', qib.astype(jnp.float32), ki_all.astype(jnp.float32))
    score = jnp.einsum('bqhs,bqh->bqs', jax.nn.relu(rel), wb.astype(jnp.float32))
    score = jnp.where(allowed[None], score, -jnp.inf)
    top_val, top_idx = lax.top_k(score, topk)
    valid = jnp.isfinite(top_val)
    bidx = jnp.arange(B)[:, None, None]
    k_sel = k_all[bidx, top_idx]
    v_sel = v_all[bidx, top_idx]
    logits = jnp.einsum('bqhgd,bqshd->bqhgs', qb, k_sel).astype(jnp.float32) * (HEAD_DIM_A ** -0.5)
    dist = jnp.abs(posb[None, :, None] - top_idx).astype(jnp.float32)
    logits = logits - slopes[None, None, :, :, None] * dist[:, :, None, None, :]
    logits = jnp.where(valid[:, :, None, None, :], logits, -jnp.inf)
    p = jax.nn.softmax(logits, axis=-1).astype(v_sel.dtype)
    return jnp.einsum('bqhgs,bqshd->bqhgd', p, v_sel)

def _dsa_attention(q, qi, wi, k_all, v_all, ki_all, past):
    B, T = q.shape[:2]
    L = k_all.shape[1]
    topk = min(TOPK_MAX, L // 4)
    qblk = min(Q_BLOCK, T)
    nb = T // qblk
    pos = past + jnp.arange(T, dtype=jnp.int32)
    slopes = _alibi_slopes()

    def to_blocks(a):
        return jnp.moveaxis(a.reshape((B, nb, qblk) + a.shape[2:]), 1, 0)

    def one_block(args):
        qb, qib, wb, posb = args
        return _dsa_block(qb, qib, wb, posb, k_all, v_all, ki_all, topk, slopes)

    out = lax.map(one_block, (to_blocks(q), to_blocks(qi), to_blocks(wi), pos.reshape(nb, qblk)))
    return jnp.moveaxis(out, 0, 1).reshape(B, T, WIDTH_A)

def _causal_conv(xc, conv_state, conv_w):
    T = xc.shape[1]
    xcat = jnp.concatenate([conv_state.astype(xc.dtype), xc], axis=1)
    y = xcat[:, 0:T] * conv_w[0]
    for j in range(1, CONV_W):
        y = y + xcat[:, j:j + T] * conv_w[j]
    return y, xcat[:, T:]

def _gated_delta(q, k, v, g, beta, s0, chunk):
    f32 = jnp.float32
    B, T, H, DK = q.shape
    DV = v.shape[-1]
    N = T // chunk

    def blk(a):
        return jnp.moveaxis(a.astype(f32).reshape((B, N, chunk, H) + a.shape[3:]), 3, 2)

    q, k, v, g, beta = blk(q), blk(k), blk(v), blk(g), blk(beta)
    gc = jnp.cumsum(g, axis=-1)
    causal = jnp.tril(jnp.ones((chunk, chunk), dtype=bool))
    strict = jnp.tril(jnp.ones((chunk, chunk), dtype=bool), -1)
    decay = jnp.exp(jnp.where(causal, gc[..., :, None] - gc[..., None, :], -jnp.inf))
    kb = k * beta[..., None]
    a_mat = jnp.where(strict, jnp.einsum('bnhid,bnhjd->bnhij', kb, k) * decay, 0.0)
    m_mat = a_mat + jnp.eye(chunk, dtype=f32)
    rhs = jnp.concatenate([v * beta[..., None], kb * jnp.exp(gc)[..., None]], axis=-1)
    sol = lax.linalg.triangular_solve(m_mat, rhs, left_side=True, lower=True, unit_diagonal=True)
    u, w = sol[..., :DV], sol[..., DV:]
    qk = jnp.einsum('bnhid,bnhjd->bnhij', q, k) * decay
    qg = q * jnp.exp(gc)[..., None]
    glast = gc[..., -1]
    kd = k * jnp.exp(glast[..., None] - gc)[..., None]

    def step(s, inp):
        u_n, w_n, qg_n, qk_n, kd_n, gl_n = inp
        v_new = u_n - jnp.einsum('bhcd,bhde->bhce', w_n, s)
        o = jnp.einsum('bhcd,bhde->bhce', qg_n, s) + jnp.einsum('bhij,bhje->bhie', qk_n, v_new)
        s = s * jnp.exp(gl_n)[..., None, None] + jnp.einsum('bhcd,bhce->bhde', kd_n, v_new)
        return s, o

    xs = tuple(jnp.moveaxis(a, 1, 0) for a in (u, w, qg, qk, kd, glast))
    s_fin, o = lax.scan(step, s0.astype(f32), xs)
    o = jnp.moveaxis(jnp.moveaxis(o, 0, 1), 2, 3).reshape(B, T, H, DV)
    return o, s_fin

def _layer(x, conv_state, delta_state, past_k, past_v, past_ki,
           norm_w, w_in, conv_w, a_log, dt_bias, gnorm_w, w_out):
    B, T, _ = x.shape
    P = past_k.shape[1]
    h = _rmsnorm(x, norm_w)
    q_a, k_a, v_a, z_a, q_i, k_i, w_i, qkv_b, z_b, a_b, b_b = _split_proj(h @ w_in)
    k_a = k_a.reshape(B, T, KV_HEADS_A, HEAD_DIM_A)
    v_a = v_a.reshape(B, T, KV_HEADS_A, HEAD_DIM_A)
    k_all = jnp.concatenate([past_k.astype(x.dtype), k_a], axis=1)
    v_all = jnp.concatenate([past_v.astype(x.dtype), v_a], axis=1)
    ki_all = jnp.concatenate([past_ki.astype(x.dtype), k_i], axis=1)
    o_a = _dsa_attention(q_a.reshape(B, T, KV_HEADS_A, GROUP_A, HEAD_DIM_A),
                         q_i.reshape(B, T, IDX_HEADS, IDX_DIM), w_i * IDX_SCALE,
                         k_all, v_all, ki_all, P)
    o_a = o_a * jax.nn.silu(z_a)
    conv_out, new_conv = _causal_conv(qkv_b, conv_state, conv_w)
    conv_out = jax.nn.silu(conv_out)
    q_b, k_b, v_b = jnp.split(conv_out, [HEADS_B * DK_B, 2 * HEADS_B * DK_B], axis=-1)
    q_b = _l2norm(q_b.reshape(B, T, HEADS_B, DK_B)) * (DK_B ** -0.5)
    k_b = _l2norm(k_b.reshape(B, T, HEADS_B, DK_B))
    v_b = v_b.reshape(B, T, HEADS_B, DV_B)
    g = -jnp.exp(a_log.astype(jnp.float32)) * jax.nn.softplus(a_b.astype(jnp.float32) + dt_bias.astype(jnp.float32))
    beta = jax.nn.sigmoid(b_b.astype(jnp.float32))
    o_b, s_new = _gated_delta(q_b, k_b, v_b, g, beta, delta_state, min(CHUNK, T))
    o_b = _rmsnorm(o_b, gnorm_w) * jax.nn.silu(z_b.reshape(B, T, HEADS_B, DV_B).astype(jnp.float32))
    o_b = o_b.reshape(B, T, WIDTH_B).astype(x.dtype)
    y = x + jnp.concatenate([o_a, o_b], axis=-1) @ w_out
    return y, k_a, v_a, k_i, new_conv, s_new.astype(delta_state.dtype)

def setup_inputs(seed: int = 0) -> dict:
    key = jax.random.key(seed)
    ks = jax.random.split(key, 16)
    f32 = jnp.float32
    x_prompt = jax.random.normal(ks[0], (BATCH, SEQ, D_MODEL), f32)
    x_sample = jax.random.normal(ks[1], (DEC_BATCH, DEC_SEQ, D_MODEL), f32)
    cache_k = jax.random.normal(ks[2], (DEPTH, DEC_BATCH, PAST_LEN, KV_HEADS_A, HEAD_DIM_A), f32)
    cache_v = jax.random.normal(ks[3], (DEPTH, DEC_BATCH, PAST_LEN, KV_HEADS_A, HEAD_DIM_A), f32)
    cache_idx_k = jax.random.normal(ks[4], (DEPTH, DEC_BATCH, PAST_LEN, IDX_DIM), f32)
    state_conv = jax.random.normal(ks[5], (DEPTH, DEC_BATCH, CONV_W - 1, QKV_B), f32)
    state_delta = 0.1 * jax.random.normal(ks[6], (DEPTH, DEC_BATCH, HEADS_B, DK_B, DV_B), f32)
    norm_w = 1.0 + 0.01 * jax.random.normal(ks[7], (DEPTH, D_MODEL), f32)
    w_in = jax.random.normal(ks[8], (DEPTH, D_MODEL, PROJ_TOTAL), f32) * (D_MODEL ** -0.5)
    conv_w = jax.random.normal(ks[9], (DEPTH, CONV_W, QKV_B), f32) * (CONV_W ** -0.5)
    a_log = jnp.log(jax.random.uniform(ks[10], (DEPTH, HEADS_B), f32, 1.0, 16.0))
    dt = jnp.exp(jax.random.uniform(ks[11], (DEPTH, HEADS_B), f32, jnp.log(1e-3), jnp.log(1e-1)))
    dt_bias = dt + jnp.log(-jnp.expm1(-dt))
    gnorm_w = 1.0 + 0.01 * jax.random.normal(ks[12], (DEPTH, DV_B), f32)
    w_out = jax.random.normal(ks[13], (DEPTH, D_MIX, D_MODEL), f32) * (D_MIX ** -0.5)
    final_norm_w = 1.0 + 0.01 * jax.random.normal(ks[14], (D_MODEL,), f32)
    return {'x_prompt': x_prompt, 'x_sample': x_sample, 'cache_k': cache_k, 'cache_v': cache_v,
            'cache_idx_k': cache_idx_k, 'state_conv': state_conv, 'state_delta': state_delta,
            'norm_w': norm_w, 'w_in': w_in, 'conv_w': conv_w, 'a_log': a_log, 'dt_bias': dt_bias,
            'gnorm_w': gnorm_w, 'w_out': w_out, 'final_norm_w': final_norm_w}

def reference(x_prompt, x_sample, cache_k, cache_v, cache_idx_k, state_conv, state_delta,
              norm_w, w_in, conv_w, a_log, dt_bias, gnorm_w, w_out, final_norm_w):
    B = x_prompt.shape[0]
    dt = x_prompt.dtype
    hp, hs = x_prompt, x_sample
    pk, pv, pki, pc, ps = [], [], [], [], []
    sk, sv, ski, sc, ss = [], [], [], [], []
    for l in range(DEPTH):
        w_l = (norm_w[l], w_in[l], conv_w[l], a_log[l], dt_bias[l], gnorm_w[l], w_out[l])
        hp, k_, v_, ki_, c_, s_ = _layer(
            hp, jnp.zeros((B, CONV_W - 1, QKV_B), dt), jnp.zeros((B, HEADS_B, DK_B, DV_B), state_delta.dtype),
            jnp.zeros((B, 0, KV_HEADS_A, HEAD_DIM_A), dt), jnp.zeros((B, 0, KV_HEADS_A, HEAD_DIM_A), dt),
            jnp.zeros((B, 0, IDX_DIM), dt), *w_l)
        pk.append(k_); pv.append(v_); pki.append(ki_); pc.append(c_); ps.append(s_)
        hs, k_, v_, ki_, c_, s_ = _layer(
            hs, state_conv[l], state_delta[l], cache_k[l], cache_v[l], cache_idx_k[l], *w_l)
        sk.append(k_); sv.append(v_); ski.append(ki_); sc.append(c_); ss.append(s_)
    y_prompt = _rmsnorm(hp, final_norm_w)
    y_sample = _rmsnorm(hs, final_norm_w)
    return (y_prompt, y_sample,
            jnp.stack(pk), jnp.stack(pv), jnp.stack(pki), jnp.stack(pc), jnp.stack(ps),
            jnp.stack(sk), jnp.stack(sv), jnp.stack(ski), jnp.stack(sc), jnp.stack(ss))


_drawn_inputs = setup_inputs


def setup_inputs(seed=0):
    import zlib

    import numpy as np

    out = dict(_drawn_inputs(seed))
    spreads = {}
    factors = {'norm_w': 3.025, 'gnorm_w': 8.0, 'final_norm_w': 5.557}
    for name, (base, spread) in spreads.items():
        noise = np.random.default_rng([zlib.crc32(name.encode()), seed]).standard_normal(out[name].shape)
        drawn = base * np.exp(spread * noise) if base else spread * noise
        out[name] = __import__('jax').numpy.asarray(drawn.astype(out[name].dtype))
    for name, factor in factors.items():
        out[name] = (out[name] * factor).astype(out[name].dtype)
    return out
```

```python
from contextlib import ExitStack

import concourse.bass as bass
from concourse import mybir

F32 = mybir.dt.float32
F32R = mybir.dt.float32r
BF16 = mybir.dt.bfloat16
ACT = mybir.ActivationFunctionType
ALU = mybir.AluOpType
AX_X = mybir.AxisListType.X

P = 128
D = 2048
KT = D // P
SEQ = 1024
DEC_B, DEC_T, PAST = 8, 16, 256
NT = SEQ // P
TILES = NT + 1
TOK = TILES * P
CHUNK = 64
EPS = 1e-6
H = 8
KV = 2
GROUP = H // KV
HD = 128
IH, ID = 16, 64
PROMPT_TOP = 256
LS = PAST + DEC_T
SAMPLE_TOP = LS // 4
CONV = 4
C_Q, C_K, C_V, C_Z = 0, 1024, 1280, 1536
C_QI, C_KI, C_WI, C_B, C_ZB, C_AB = 2560, 3584, 3648, 3664, 6736, 7760
PROJ = 7776
IDX_SCALE = (IH * ID) ** -0.5
SCALE = HD ** -0.5
OUT_MASK = -1e30
NOT_ALLOWED = -3.2e38
TAKEN = -3.4e38

FULL_BLOCKS = PROJ // P
LAST_COLS = PROJ - FULL_BLOCKS * P
NCH = 4
CK = KT // NCH
G3 = TOK // 3
FIRST = (C_QI // P, 30)
SEGMENTS = [(0, 7), (7, 14), (14, 20), (30, 37), (37, 44), (44, 51), (51, FULL_BLOCKS)]
INDEX_TILES = [7, 6, 5, 4, 3, 2]


def normalise_inputs(nc, io, hH, hL, ident):
    with ExitStack() as ctx:
        def sbt(name, shape, dt=F32):
            return ctx.enter_context(nc.sbuf_tensor(name, shape, dt))

        used = []

        def sem(name):
            used.append(ctx.enter_context(nc.semaphore(name)))
            return used[-1]

        SLOTS = 3
        x = [sbt(f"x{i}", [P, D]) for i in range(SLOTS)]
        squares = sbt("squares", [P, D])
        normw_rows = sbt("normw_rows", [KT, P])
        normw = sbt("normw", [P, KT])
        stat = sbt("stat", [P, SLOTS, 4])
        hf = [sbt(f"hf{i}", [P, 4, P]) for i in range(2)]
        turned = [ctx.enter_context(nc.psum_tensor(f"turned{i}", [P, 4, P], F32)) for i in range(4)]
        pw = ctx.enter_context(nc.psum_tensor("pw", [P, KT], F32))

        ident_ready, normw_loaded, normw_turned, normw_ready = map(
            sem, ["ident_ready", "normw_loaded", "normw_turned", "normw_ready"])
        x_loaded = [sem(f"x_loaded{i}") for i in range(SLOTS)]
        x_free, squared, meaned, rooted, scaled = map(sem, ["x_free", "squared", "meaned", "rooted", "scaled"])
        quad_turned, weighted, high_ready, low_ready = map(
            sem, ["quad_turned", "weighted", "high_ready", "low_ready"])
        xp = io["x_prompt"].rearrange("b (t p) d -> (b t) p d", p=P)
        xs = io["x_sample"].rearrange("b t d -> (b t) d")

        with nc.Block() as block:
            @block.sync
            def _(sp):
                sp.dma_start(normw_rows[:, :], io["norm_w"].rearrange("a (k p) -> (a k) p", p=P)).then_inc(normw_loaded, 16)
                for t in range(TILES):
                    if t >= SLOTS:
                        sp.wait_ge(quad_turned, 4 * (t - SLOTS + 1))
                    sp.dma_start(x[t % SLOTS][:, :], xp[t] if t < NT else xs).then_inc(x_loaded[t % SLOTS], 16)

            @block.gpsimd
            def _(pool):
                pool.memset(ident[:, :], 0.0).then_inc(ident_ready, 1)
                pool.wait_ge(ident_ready, 1)
                pool.affine_select(out=ident[:, :], in_=ident[:, :], compare_op=ALU.not_equal, fill=1.0,
                                   base=0, pattern=[[-1, P]], channel_multiplier=1).then_inc(ident_ready, 1)
                for q in range(4 * TILES):
                    t, j = divmod(q, 4)
                    pool.wait_ge(high_ready, q + 1)
                    cols = slice(t * P, (t + 1) * P)
                    pool.tensor_tensor(hL[:, 4 * j:4 * j + 4, cols], hf[q % 2][:, :, :],
                                       hH[:, 4 * j:4 * j + 4, cols].bitcast(F32), ALU.subtract).then_inc(low_ready, 1)

            @block.scalar
            def _(act):
                for t in range(TILES):
                    s = t % SLOTS
                    act.wait_ge(x_loaded[s], 16 * (t // SLOTS + 1))
                    if t:
                        act.wait_ge(squared, t)
                    nc.scalar.activation(squares[:, :], x[s][:, :], ACT.Square,
                                         accum_out=stat[:, s, 0:1]).then_inc(squared, 1)
                    act.wait_ge(meaned, 2 * (t + 1))
                    nc.scalar.activation(stat[:, s, 3:4], stat[:, s, 2:3], ACT.Sqrt).then_inc(rooted, 1)
                    act.wait_ge(rooted, t + 1)
                    nc.scalar.activation(x[s][:, :], x[s][:, :], ACT.Copy, scale=stat[:, s, 3:4]).then_inc(scaled, 1)

            @block.tensor
            def _(pe):
                pe.wait_ge(ident_ready, 2)
                pe.wait_ge(normw_loaded, 16)
                pe.transpose(pw[:, :], normw_rows[:, :], ident[0:KT, 0:KT]).then_inc(normw_turned, 1)
                for q in range(4 * TILES):
                    t, j = divmod(q, 4)
                    pe.wait_ge(scaled, t + 1)
                    if q >= 4:
                        pe.wait_ge(weighted, q - 3)
                    for k in range(4):
                        kk = 4 * j + k
                        last = pe.transpose(turned[q % 4][:, k, :], x[t % SLOTS][:, kk * P:(kk + 1) * P], ident[:, :])
                    last.then_inc(quad_turned, 1)

            @block.vector
            def _(dve):
                dve.wait_ge(normw_turned, 1)
                nc.vector.tensor_copy(normw[:, :], pw[:, :]).then_inc(normw_ready, 1)
                dve.wait_ge(normw_ready, 1)

                def statistics(t):
                    s = t % SLOTS
                    dve.wait_ge(squared, t + 1)
                    nc.vector.tensor_scalar(stat[:, s, 1:2], stat[:, s, 0:1], 1.0 / D, EPS, ALU.mult, ALU.add).then_inc(meaned, 1)
                    dve.wait_ge(meaned, 2 * t + 1)
                    nc.vector.reciprocal(stat[:, s, 2:3], stat[:, s, 1:2]).then_inc(meaned, 1)

                statistics(0)
                for q in range(4 * TILES):
                    t, j = divmod(q, 4)
                    if j == 0 and t + 1 < TILES:
                        statistics(t + 1)
                    dve.wait_ge(quad_turned, q + 1)
                    if q >= 2:
                        dve.wait_ge(low_ready, q - 1)
                    nc.vector.tensor_tensor(hf[q % 2][:, :, :], turned[q % 4][:, :, :],
                                            normw[:, 4 * j:4 * j + 4].unsqueeze(2).to_broadcast([P, 4, P]),
                                            ALU.mult).then_inc(weighted, 1)
                    dve.wait_ge(weighted, q + 1)
                    nc.vector.tensor_copy(hH[:, 4 * j:4 * j + 4, t * P:(t + 1) * P], hf[q % 2][:, :, :]).then_inc(high_ready, 1)
                dve.wait_ge(low_ready, 4 * TILES)
        return used


def project_and_select(nc, io, scratch, hH, hL, ident, done_with):
    with ExitStack() as ctx:
        def sbt(name, shape, dt=F32):
            return ctx.enter_context(nc.sbuf_tensor(name, shape, dt))

        used = []

        def sem(name):
            used.append(ctx.enter_context(nc.semaphore(name)))
            return used[-1]

        proj, masks, smask = scratch["proj"], scratch["mask"], scratch["sample_mask"]
        raw = [sbt(f"raw{c}", [P, CK, P]) for c in range(NCH)]
        wH = [sbt(f"wH{i}", [P, CK, P], F32R) for i in range(2)]
        wL = [sbt(f"wL{i}", [P, CK, P], F32R) for i in range(2)]
        ptbuf = sbt("ptbuf", [P, TOK])
        score = sbt("score", [P, SEQ])
        relued = [sbt(f"relued{i}", [P, 512]) for i in range(2)]
        top8 = sbt("top8", [P, 8])
        mask = sbt("mask", [P, SEQ], BF16)
        kiN = sbt("kiN", [P, TILES, 80])
        w_idx = sbt("w_idx", [P, TILES, IH])
        diag = sbt("diag", [P, 2 * P - DEC_T])
        spread = sbt("spread", [IH, IH, DEC_T])
        wbc = sbt("wbc", [P, 2, P])
        pick = [sbt(f"pick{i}", [P, P]) for i in range(2)]
        wT = sbt("wT", [IH, P])
        region = sbt("region", [P, 5248])
        qs = region[0:ID, 0:2048].rearrange("d (b h t) -> d b h t", b=DEC_B, h=IH)
        kcT = region[0:ID, 2048:2048 + DEC_B * LS].rearrange("d (b s) -> d b s", b=DEC_B)
        kc_nat = region[:, 4224:5248].rearrange("p (n d) -> p n d", d=ID)
        qi = [region[:, i * 1024:(i + 1) * 1024].rearrange("p (j t) -> p j t", j=H) for i in range(2)]
        kiT = region[:, 2048:2048 + SEQ]
        kiw = ptbuf[0:80, :]

        bank = [ctx.enter_context(nc.psum_tensor(f"bank{i}", [P, 512], F32)) for i in range(8)]
        BANKS_REL = 4
        rel = bank[3:7]

        w_loaded = [sem(f"w_loaded{c}") for c in range(NCH)]
        high_ready = sem("high_ready")
        low_ready = sem("low_ready")
        products = sem("products")
        evacuated, pt_stored = map(sem, ["evacuated", "pt_stored"])
        idx_loaded, q_loaded, tables = map(sem, ["idx_loaded", "q_loaded", "tables"])
        turned, turned_out, new_k_stored = map(sem, ["turned", "turned_out", "new_k_stored"])
        rel_done, relu_done, acc_done, picked, summed = map(
            sem, ["rel_done", "relu_done", "acc_done", "picked", "summed"])
        dve_step, mask_ready, mask_stored, kiw_loaded = map(sem, ["dve_step", "mask_ready", "mask_stored", "kiw_loaded"])

        w_view = io["w_in"].rearrange("a (k p) n -> (a p) k n", p=P)
        segs = [FIRST] + SEGMENTS
        base, n = [], 0
        for lo, hi in segs:
            base.append(n)
            n += hi - lo
        assert n == FULL_BLOCKS
        RELS = {t: [(hd, c) for hd in range(IH) for c in range(0, (t + 1) * P, 512)] for t in INDEX_TILES}
        rel_base, n = {}, 2 * DEC_B
        for t in INDEX_TILES:
            rel_base[t] = n
            n += len(RELS[t])
        CREDIT = 1
        STEPS = 6

        with nc.Block() as block:
            @block.sync
            def _(sp):
                def load_block(s, cols):
                    for c in range(NCH):
                        sp.wait_ge(low_ready, s * NCH + c + 1)
                        width = LAST_COLS if cols is None else P
                        src = (w_view[:, c * CK:(c + 1) * CK, FULL_BLOCKS * P:PROJ] if cols is None
                               else w_view[:, c * CK:(c + 1) * CK, bass.ds(cols, P)])
                        sp.dma_start(raw[c][:, :, 0:width], src).then_inc(w_loaded[c], 16)

                lo, hi = segs[0]
                with sp.Fori(lo, hi) as b:
                    load_block(b - lo, b * P)
                for i, t in enumerate([None] + INDEX_TILES):
                    lo, hi = segs[i + 1]
                    load_block(base[i + 1], lo * P)
                    sp.wait_ge(pt_stored, 16 * (base[1] + CREDIT))
                    if t is None:
                        sp.dma_start(kiw, proj[C_KI:C_KI + 80, :]).then_inc(kiw_loaded, 16)
                        sp.dma_start(wT[:, :], proj[C_WI:C_WI + IH, SEQ:TOK]).then_inc(idx_loaded, 16)
                        for b in range(DEC_B):
                            at = SEQ + b * DEC_T
                            sp.dma_start(qs[:, b, :, :], proj[C_QI:C_KI, at:at + DEC_T].rearrange("(h d) t -> d h t", d=ID)).then_inc(idx_loaded, 16)
                        sp.dma_start(kc_nat, io["cache_idx_k"].rearrange("a b (n p) d -> p (a b n) d", p=P)).then_inc(idx_loaded, 16)
                        sp.dma_start(kcT[:, :, PAST:LS], proj[C_KI:C_WI, SEQ:TOK].rearrange("d (b t) -> d b t", b=DEC_B)).then_inc(idx_loaded, 16)
                        sp.wait_ge(turned_out, 2)
                        sp.dma_start(io["new_idx_k_prompt"].rearrange("a b (t p) d -> p (a b t) d", p=P), kiN[:, 0:NT, 0:ID]).then_inc(new_k_stored, 16)
                        sp.dma_start(io["new_idx_k_sample"].rearrange("a b t d -> (a b t) d"), kiN[:, NT, 0:ID]).then_inc(new_k_stored, 16)
                    else:
                        if t == INDEX_TILES[0]:
                            sp.wait_ge(rel_done, 2 * DEC_B)
                            for half in range(2):
                                sp.dma_start(kiT[half * ID:(half + 1) * ID, :], proj[C_KI:C_WI, 0:SEQ]).then_inc(idx_loaded, 16)
                        else:
                            n = rel_base[INDEX_TILES[i - 2]] + len(RELS[INDEX_TILES[i - 2]])
                            sp.wait_ge(rel_done, n)
                        sp.dma_start(qi[i % 2], proj[C_QI:C_KI, t * P:(t + 1) * P].rearrange("(j p) t -> p j t", p=P)).then_inc(q_loaded, 16)
                    if hi - lo > 1:
                        with sp.Fori(lo + 1, hi) as b:
                            load_block(b - lo + base[i + 1], b * P)
                    sp.wait_ge(mask_ready, i + 1)
                    if t is None:
                        sp.dma_start(smask, mask[:, 0:LS]).then_inc(mask_stored, 16)
                    else:
                        sp.dma_start(masks[t, :, 0:(t + 1) * P], mask[:, 0:(t + 1) * P]).then_inc(mask_stored, 16)
                load_block(FULL_BLOCKS, None)
                sp.wait_ge(pt_stored, 16 * (FULL_BLOCKS + 1 + CREDIT))
                sp.wait_ge(mask_stored, 16 * len(segs[1:]))
                sp.wait_ge(new_k_stored, 32)

            @block.gpsimd
            def _(pool):
                for old in done_with:
                    pool.sem_clear(old)
                pool.sem_inc(low_ready, CREDIT * NCH)
                pool.memset(diag[:, :], 0.0).then_inc(tables, 1)
                pool.memset(spread[:, :, :], 1.0).then_inc(tables, 1)
                pool.wait_ge(tables, 2)
                for hd in range(H):
                    ones = diag[:, P - DEC_T:P]
                    pool.affine_select(out=ones, in_=ones, compare_op=ALU.not_equal, fill=1.0, base=DEC_T * hd,
                                       pattern=[[1, DEC_T]], channel_multiplier=-1).then_inc(tables, 1)
                    pool.wait_ge(tables, 3 + hd)
                pool.affine_select(out=spread[:, :, :], in_=spread[:, :, :], compare_op=ALU.is_equal, fill=0.0,
                                   base=0, pattern=[[-1, IH], [0, DEC_T]], channel_multiplier=1).then_inc(tables, 1)

                def low_parts(s):
                    for c in range(NCH):
                        pool.wait_ge(high_ready, s * NCH + c + 1)
                        pool.tensor_tensor(wL[c % 2][:, :, :], raw[c][:, :, :], wH[c % 2][:, :, :].bitcast(F32),
                                           ALU.subtract).then_inc(low_ready, 1)

                for (lo, hi), b0 in zip(segs, base):
                    with pool.Fori(lo, hi) as b:
                        low_parts(b - lo + b0)
                low_parts(FULL_BLOCKS)

            @block.scalar
            def _(act):
                act.sem_inc(pt_stored, 16 * CREDIT)
                act.sem_inc(evacuated, 3 * CREDIT)

                def high_part(s, c):
                    act.wait_ge(w_loaded[c], s * 16 + 16)
                    act.wait_ge(products, s * STEPS + (3, 6, 7, 8)[c])
                    nc.scalar.activation(wH[c % 2][:, :, :], raw[c][:, :, :], ACT.Copy).then_inc(high_ready, 1)

                def block_steps(s, rows, cols, more=True):
                    high_part(s, 2)
                    high_part(s, 3)
                    if more:
                        high_part(s + 1, 0)
                    act.wait_ge(pt_stored, s * 16 + 16 * CREDIT)
                    for g in range(3):
                        act.wait_ge(products, s * STEPS + 4 + g + STEPS * CREDIT)
                        nc.scalar.activation(ptbuf[0:rows, g * G3:(g + 1) * G3], bank[g][0:rows, 0:G3], ACT.Copy).then_inc(evacuated, 1)
                    act.wait_ge(evacuated, s * 3 + 3 + 3 * CREDIT)
                    act.dma_start(proj[cols, :], ptbuf[0:rows, :]).then_inc(pt_stored, 16)
                    if more:
                        high_part(s + 1, 1)

                def index_units(first, widths):
                    for u, width in enumerate(widths, first):
                        act.wait_ge(rel_done, u + 1)
                        if 2 <= u < 2 * DEC_B + 2:
                            act.wait_ge(summed, min(u - 1, 2 * DEC_B))
                        if u >= 2 * DEC_B + 2:
                            act.wait_ge(acc_done, u - 2 * DEC_B - 1)
                        nc.scalar.activation(relued[u % 2][:, 0:width], rel[u % BANKS_REL][:, 0:width], ACT.Relu).then_inc(relu_done, 1)

                high_part(0, 0)
                high_part(0, 1)
                for i, ((lo, hi), b0) in enumerate(zip(segs, base)):
                    if i == 1:
                        for half in range(2):
                            act.wait_ge(turned, half + 1)
                            n0, n1 = (0, 5) if half == 0 else (5, 9)
                            nc.scalar.activation(kiN[:, n0:n1, :], bank[3 + half][:, 0:(n1 - n0) * 80].rearrange("p (t c) -> p t c", c=80), ACT.Copy).then_inc(turned_out, 1)
                        for n in range(4):
                            act.wait_ge(turned, 3 + n)
                            nc.scalar.activation(kcT[:, 2 * n:2 * n + 2, 0:PAST], bank[(5, 6, 3, 4)[n]][0:ID, 0:512].rearrange("d (b s) -> d b s", b=2), ACT.Copy).then_inc(turned_out, 1)
                        act.wait_ge(turned, 7)
                        nc.scalar.activation(wbc[:, :, :], bank[7][:, 0:256].rearrange("p (a t) -> p a t", a=2), ACT.Copy, scale=IDX_SCALE).then_inc(turned_out, 1)
                        index_units(0, [LS] * (2 * DEC_B))
                    elif i > 1:
                        t = INDEX_TILES[i - 2]
                        index_units(rel_base[t], [min(512, (t + 1) * P - c) for _, c in RELS[t]])
                    with act.Fori(lo, hi) as b:
                        block_steps(b - lo + b0, P, bass.ds(b * P, P))
                block_steps(FULL_BLOCKS, LAST_COLS, slice(FULL_BLOCKS * P, PROJ), more=False)

            @block.tensor
            def _(pe):
                pe.sem_inc(products, STEPS * CREDIT)

                def block_products(s, cols):
                    for c in range(NCH):
                        pe.wait_ge(low_ready, s * NCH + c + 1 + NCH * CREDIT)
                        for g in range(3):
                            if c == 0:
                                pe.wait_ge(evacuated, s * 3 + g + 1)
                            for k in range(CK):
                                kk = c * CK + k
                                tok = slice(g * G3, (g + 1) * G3)
                                first, end = c == 0 and k == 0, c == NCH - 1 and k == CK - 1
                                o = bank[g][0:cols, 0:G3]
                                high, low = wH[c % 2][:, k, 0:cols], wL[c % 2][:, k, 0:cols]
                                pe.matmul(o, low, hH[:, kk, tok], start=first, stop=False)
                                pe.matmul(o, high, hL[:, kk, tok], start=False, stop=False)
                                last = pe.matmul(o, high, hH[:, kk, tok], start=False, stop=end)
                            if c == NCH - 1:
                                last.then_inc(products, 1)
                        if c < NCH - 1:
                            last.then_inc(products, 1)

                def sample_index():
                    pe.wait_ge(kiw_loaded, 16)
                    for t in range(TILES):
                        o = bank[3 + t // 5][:, (t % 5) * 80:(t % 5 + 1) * 80]
                        last = pe.transpose(o, kiw[:, t * P:(t + 1) * P], ident[0:80, 0:80])
                        if t in (4, 8):
                            last.then_inc(turned, 1)
                    pe.wait_ge(idx_loaded, 16 * (3 + DEC_B))
                    for n in range(4):
                        if n == 2:
                            pe.wait_ge(turned_out, 2)
                        for m in range(4):
                            last = pe.transpose(bank[(5, 6, 3, 4)[n]][0:ID, m * P:(m + 1) * P], kc_nat[:, 4 * n + m, :], ident[:, :])
                        last.then_inc(turned, 1)
                    pe.wait_ge(tables, 3 + H)
                    for half in range(2):
                        last = pe.matmul(bank[7][:, half * P:(half + 1) * P], spread[:, half * H:(half + 1) * H, :], wT[:, :], start=True, stop=True)
                    last.then_inc(turned, 1)
                    pe.wait_ge(turned_out, 7)

                    def relate(u):
                        b, half = divmod(u, 2)
                        if u >= BANKS_REL:
                            pe.wait_ge(relu_done, u - BANKS_REL + 1)
                        pe.matmul(rel[u % BANKS_REL][:, 0:LS], qs[:, b, half * H:(half + 1) * H, :],
                                  kcT[:, b, :], start=True, stop=True).then_inc(rel_done, 1)

                    relate(0)
                    for u in range(2 * DEC_B):
                        if u + 1 < 2 * DEC_B:
                            relate(u + 1)
                        pe.wait_ge(relu_done, u + 1)
                        pe.wait_ge(picked, u + 1)
                        pe.matmul(bank[7][:, 0:LS], pick[u % 2][:, :], relued[u % 2][:, 0:LS],
                                  start=(u == 0), stop=(u == 2 * DEC_B - 1)).then_inc(summed, 1)

                def prompt_index(i, t):
                    pe.wait_ge(idx_loaded, 16 * (5 + DEC_B))
                    pe.wait_ge(q_loaded, 16 * i)
                    for u, (hd, c) in enumerate(RELS[t], rel_base[t]):
                        pe.wait_ge(relu_done, u - BANKS_REL + 1)
                        width = min(512, (t + 1) * P - c)
                        rows = slice(hd % 2 * ID, hd % 2 * ID + ID)
                        pe.matmul(rel[u % BANKS_REL][:, 0:width], qi[i % 2][rows, hd // 2, :], kiT[rows, c:c + width],
                                  start=True, stop=True).then_inc(rel_done, 1)

                for i, ((lo, hi), b0) in enumerate(zip(segs, base)):
                    if i == 1:
                        sample_index()
                    elif i > 1:
                        prompt_index(i - 1, INDEX_TILES[i - 2])
                    with pe.Fori(lo, hi) as b:
                        block_products(b - lo + b0, P)
                block_products(FULL_BLOCKS, LAST_COLS)

            @block.vector
            def _(dve):
                steps = [0]

                def chain(instruction):
                    steps[0] += 1
                    instruction.then_inc(dve_step, 1)
                    dve.wait_ge(dve_step, steps[0])

                def select(i, width, top):
                    sc = score[:, 0:width]
                    for r in range(top // 8):
                        chain(nc.vector.max(top8[:, :], sc))
                        chain(nc.vector.match_replace(out=sc, in_to_replace=top8[:, :], in_values=sc, imm_value=TAKEN))
                    if top % 8:
                        chain(nc.vector.max(top8[:, :], sc))
                        chain(nc.vector.memset(top8[:, top % 8:8], TAKEN))
                        chain(nc.vector.match_replace(out=sc, in_to_replace=top8[:, :], in_values=sc, imm_value=TAKEN))
                    if i:
                        dve.wait_ge(mask_stored, 16 * i)
                    nc.vector.tensor_scalar(mask[:, 0:width], sc, TAKEN, OUT_MASK, ALU.not_equal, ALU.mult).then_inc(mask_ready, 1)

                dve.wait_ge(turned_out, 2)
                chain(nc.vector.tensor_scalar(w_idx[:, :, :], kiN[:, :, ID:80], IDX_SCALE, None, ALU.mult))
                dve.wait_ge(turned_out, 7)
                dve.wait_ge(tables, 3 + H)
                for u in range(2 * DEC_B):
                    b, half = divmod(u, 2)
                    if u >= 2:
                        dve.wait_ge(summed, u - 1)
                    at = P - DEC_T - DEC_T * b
                    nc.vector.tensor_tensor(pick[u % 2][:, :], wbc[:, half, :], diag[:, at:at + P], ALU.mult).then_inc(picked, 1)
                dve.wait_ge(summed, 2 * DEC_B)
                chain(nc.vector.tensor_copy(score[:, 0:LS], bank[7][:, 0:LS]))
                select(0, LS, SAMPLE_TOP)
                for i, t in enumerate(INDEX_TILES, 1):
                    dve.wait_ge(mask_ready, i)
                    for u, (hd, c) in enumerate(RELS[t], rel_base[t] - 2 * DEC_B):
                        width = min(512, (t + 1) * P - c)
                        sc, r = score[:, c:c + width], relued[u % 2][:, 0:width]
                        dve.wait_ge(relu_done, u + 1 + 2 * DEC_B)
                        if u > rel_base[t] - 2 * DEC_B:
                            dve.wait_ge(acc_done, u)
                        w = w_idx[:, t, hd:hd + 1]
                        if hd == 0:
                            nc.vector.tensor_scalar(sc, r, w, None, ALU.mult).then_inc(acc_done, 1)
                        else:
                            nc.vector.scalar_tensor_tensor(out=sc, in0=r, scalar=w, in1=sc, op0=ALU.mult, op1=ALU.add).then_inc(acc_done, 1)
                    dve.wait_ge(acc_done, u + 1)
                    chain(nc.vector.memset(score[0:CHUNK, t * P + CHUNK:(t + 1) * P], NOT_ALLOWED))
                    select(i, (t + 1) * P, PROMPT_TOP)
        return used


class Signal:

    def __init__(self, sem, per):
        self.sem, self.per = sem, per

    def now(self, h, k):
        return h * self.per + (self.per + k)

    def before(self, h, k):
        return h * self.per + k


LEVELS = 7
SAMPLE_LEVELS = 4
GATES = 6
G_LOG, G_CUM, G_BETA, G_BETA_EXP, G_EXP, G_REST = range(GATES)


def prepare_heads(nc, io, scratch, keep, ident, done_with):
    with ExitStack() as ctx:
        def sbt(name, shape, dt=F32):
            return ctx.enter_context(nc.sbuf_tensor(name, shape, dt))

        def sem(name):
            return ctx.enter_context(nc.semaphore(name))

        proj = scratch["proj"]
        kvT = sbt("kvT", [P, 4, TOK])
        kvN = sbt("kvN", [P, TILES, 4, P])
        abT = sbt("abT", [16, TOK])
        ab = sbt("ab", [P, TILES, 16])
        dtb, alog, aexp = sbt("dtb", [P, H]), sbt("alog", [P, H]), sbt("aexp", [P, H])
        wk = [sbt(f"wk{i}", [P, TILES, H]) for i in range(6)]
        gnat = sbt("gnat", [P, TILES, H])
        ones = sbt("ones", [P, P])
        same16 = sbt("same16", [P, P])
        dist = sbt("dist", [P, SEQ], mybir.dt.int32)
        loaded, tabled, built, stepped, acted, turned, moved, stored = map(
            sem, ["loaded", "tabled", "built", "stepped", "acted", "turned", "moved", "stored"])
        gate_loaded, kv_loaded, summed, drained = map(sem, ["gate_loaded", "kv_loaded", "summed", "drained"])
        bank = [ctx.enter_context(nc.psum_tensor(f"pb{i}", [P, 4, P], F32)) for i in range(4)]
        abp = ctx.enter_context(nc.psum_tensor("abp", [P, TILES, 16], F32))
        gcp = ctx.enter_context(nc.psum_tensor("gcp", [P, 2, TILES, H], F32))
        G, K = keep["gates"], keep
        cumP, cumS, segcol, segs16 = K["cum"][:, 0, :], K["cum"][:, 1, :], K["segcol"], same16

        with nc.Block() as block:
            @block.sync
            def _(sp):
                sp.dma_start(abT[:, :], proj[C_AB:PROJ, :]).then_inc(gate_loaded, 16)
                sp.dma_start(dtb[:, :], io["dt_bias"].to_broadcast([P, H])).then_inc(gate_loaded, 16)
                sp.dma_start(alog[:, :], io["a_log"].to_broadcast([P, H])).then_inc(gate_loaded, 16)
                sp.dma_start(kvT[:, :, :], proj[C_K:C_Z, :].rearrange("(n p) t -> p n t", p=P)).then_inc(kv_loaded, 16)
                sp.dma_start(K["kT"][:, :, :], proj[C_K:C_V, 0:SEQ].rearrange("(n p) t -> p n t", p=P)).then_inc(loaded, 16)
                at = 0
                for t in range(NT):
                    w = (t + 1) * P
                    if t >= 2:
                        sp.dma_start(K["mask"][:, at:at + w], scratch["mask"][t, :, 0:w]).then_inc(loaded, 16)
                    at += w
                sp.dma_start(K["gnw"][:, :], io["gnorm_w"].rearrange("a d -> d a")).then_inc(loaded, 16)
                sp.wait_ge(moved, TILES)
                flat = kvN[:, :, :, :].rearrange("p t n d -> p t (n d)")
                for name, c in (("new_k", 0), ("new_v", 2 * P)):
                    sp.dma_start(io[name + "_prompt"].rearrange("a b (t p) k d -> p (a b t) (k d)", p=P), flat[:, 0:NT, c:c + 2 * P]).then_inc(stored, 16)
                    sp.dma_start(io[name + "_sample"].rearrange("a b t k d -> (a b t) (k d)"), flat[:, NT, c:c + 2 * P]).then_inc(stored, 16)
                sp.wait_ge(stored, 64)
                sp.wait_ge(loaded, 16 * 8)

            @block.gpsimd
            def _(pool):
                for old in done_with:
                    pool.sem_clear(old)
                n = [0]

                def chain(instruction):
                    n[0] += 1
                    instruction.then_inc(tabled, 1)
                    pool.wait_ge(tabled, n[0])

                def keep_where(ap, op, base, pattern, mult, fill=0.0):
                    chain(pool.affine_select(out=ap, in_=ap, compare_op=op, fill=fill, base=base, pattern=pattern, channel_multiplier=mult))

                pool.memset(ones[:, :], 1.0).then_inc(tabled, 1)
                n[0] += 1
                chain(pool.memset(segcol[:, :], 1.0))
                keep_where(segcol[:, :], ALU.is_ge, 0, [[-DEC_T, DEC_B]], 1)
                keep_where(segcol[:, :], ALU.is_ge, DEC_T - 1, [[DEC_T, DEC_B]], -1)
                chain(pool.tensor_copy(same16[:, :].rearrange("p (b t) -> p b t", b=DEC_B), segcol[:, :].unsqueeze(2).to_broadcast([P, DEC_B, DEC_T])))
                for name, base, step, mult in (("cum", 0, 1, -1), ("dmN", 0, -1, 1)):
                    chain(pool.memset(K[name][:, 0, :], 1.0))
                    keep_where(K[name][:, 0, :], ALU.is_ge, base, [[step, P]], mult)
                    chain(pool.tensor_tensor(K[name][:, 1, :], K[name][:, 0, :], same16[:, :], ALU.mult))
                chain(pool.tensor_scalar(K["dmT"][:, :, :], K["cum"][:, :, :], 1.0, -OUT_MASK, ALU.subtract, ALU.mult))
                chain(pool.tensor_scalar(K["dmN"][:, :, :], K["dmN"][:, :, :], 1.0, -OUT_MASK, ALU.subtract, ALU.mult))
                chain(pool.memset(K["level"][:, :, :], 0.0))
                for m in range(LEVELS):
                    b = 2 ** m
                    first = K["level"][:, m, :].rearrange("p (n e r) -> p n e r", e=2, r=b)[:, :, 0, :]
                    chain(pool.memset(first, 1.0))
                    keep_where(first, ALU.is_ge, -b, [[-2 * b, P // (2 * b)], [0, b]], 1)
                    keep_where(first, ALU.is_ge, 2 * b - 1, [[2 * b, P // (2 * b)], [0, b]], -1)
                chain(pool.tensor_copy(K["identb"][:, :], ident[:, :]))
                chain(pool.iota(dist[:, :], pattern=[[-1, SEQ]], base=SEQ - P, channel_multiplier=1))
                chain(pool.memset(K["mask"][:, 0:3 * P], 0.0))
                for at in (0, 2 * P):
                    chain(pool.memset(K["mask"][0:CHUNK, at + CHUNK:at + P], OUT_MASK))
                pool.sem_inc(built, 1)

            @block.tensor
            def _(pe):
                pe.wait_ge(gate_loaded, 48)
                for t in range(TILES):
                    last = pe.transpose(abp[:, t, :], abT[:, t * P:(t + 1) * P], ident[0:16, 0:16])
                last.then_inc(turned, 1)
                pe.wait_ge(kv_loaded, 16)
                for t in range(TILES):
                    if t >= 4:
                        pe.wait_ge(moved, t - 3)
                    for n in range(4):
                        last = pe.transpose(bank[t % 4][:, n, :], kvT[:, n, t * P:(t + 1) * P], ident[:, :])
                    last.then_inc(turned, 1)
                pe.wait_ge(stepped, 9)
                pe.wait_ge(built, 1)
                pe.matmul(gcp[:, 0, 0:NT, :], cumP, gnat[:, 0:NT, :], start=True, stop=True)
                pe.matmul(gcp[:, 0, NT, :], cumS, gnat[:, NT, :], start=True, stop=True)
                pe.matmul(gcp[:, 1, 0:NT, :], ones[:, :], gnat[:, 0:NT, :], start=True, stop=True)
                pe.matmul(gcp[:, 1, NT, :], same16[:, :], gnat[:, NT, :], start=True, stop=True).then_inc(summed, 1)

            @block.scalar
            def _(act):
                act.wait_ge(stepped, 3)
                nc.scalar.activation(wk[2][:, :, :], wk[1][:, :, :], ACT.Exp, scale=-1.0).then_inc(acted, 1)
                nc.scalar.activation(aexp[:, :], alog[:, :], ACT.Exp).then_inc(acted, 1)
                nc.scalar.activation(wk[4][:, :, :], ab[:, :, H:16], ACT.Exp, scale=-1.0).then_inc(acted, 1)
                act.wait_ge(acted, 1)
                nc.scalar.activation(wk[3][:, :, :], wk[2][:, :, :], ACT.Ln, bias=1.0).then_inc(acted, 1)
                for t in range(TILES):
                    act.wait_ge(turned, t + 2)
                    nc.scalar.activation(kvN[:, t, :, :], bank[t % 4][:, :, :], ACT.Copy).then_inc(moved, 1)
                act.wait_ge(stepped, 11)
                nc.scalar.activation(G[:, :, G_EXP, :].rearrange("p h t -> p t h"), wk[0][:, :, :], ACT.Exp).then_inc(acted, 1)
                nc.scalar.activation(G[:, :, G_REST, :].rearrange("p h t -> p t h"), wk[1][:, :, :], ACT.Exp).then_inc(acted, 1)
                act.wait_ge(moved, TILES)
                for t in range(NT):
                    last = nc.scalar.activation(K["vN"][:, t, :, :], kvN[:, t, 2:4, :], ACT.Copy)
                    last.then_inc(drained, 1)

            @block.vector
            def _(dve):
                n = [0]

                def chain(instruction):
                    n[0] += 1
                    instruction.then_inc(stepped, 1)
                    dve.wait_ge(stepped, n[0])

                gv = lambda k: G[:, :, k, :].rearrange("p h t -> p t h")
                dve.wait_ge(turned, 1)
                dve.wait_ge(gate_loaded, 48)
                chain(nc.vector.tensor_copy(ab[:, :, :], abp[:, :, :]))
                chain(nc.vector.tensor_tensor(wk[0][:, :, :], ab[:, :, 0:H], dtb[:, :].unsqueeze(1).to_broadcast([P, TILES, H]), ALU.add))
                chain(nc.vector.scalar_tensor_tensor(out=wk[1][:, :, :], in0=wk[0][:, :, :], scalar=-1.0, in1=wk[0][:, :, :], op0=ALU.mult, op1=ALU.max))
                dve.wait_ge(acted, 4)
                chain(nc.vector.scalar_tensor_tensor(out=wk[5][:, :, :], in0=wk[0][:, :, :], scalar=0.0, in1=wk[3][:, :, :], op0=ALU.max, op1=ALU.add))
                chain(nc.vector.tensor_tensor(wk[5][:, :, :], wk[5][:, :, :], aexp[:, :].unsqueeze(1).to_broadcast([P, TILES, H]), ALU.mult))
                chain(nc.vector.tensor_scalar(gnat[:, :, :], wk[5][:, :, :], -1.0, None, ALU.mult))
                chain(nc.vector.tensor_copy(gv(G_LOG), gnat[:, :, :]))
                chain(nc.vector.tensor_scalar(wk[4][:, :, :], wk[4][:, :, :], 1.0, None, ALU.add))
                chain(nc.vector.reciprocal(gv(G_BETA), wk[4][:, :, :]))
                dve.wait_ge(summed, 1)
                chain(nc.vector.tensor_copy(wk[0][:, :, :], gcp[:, 0, :, :]))
                chain(nc.vector.tensor_tensor(wk[1][:, :, :], gcp[:, 1, :, :], wk[0][:, :, :], ALU.subtract))
                chain(nc.vector.tensor_copy(gv(G_CUM), wk[0][:, :, :]))
                dve.wait_ge(acted, 5)
                chain(nc.vector.tensor_tensor(gv(G_BETA_EXP), gv(G_BETA), gv(G_EXP), ALU.mult))
                dve.wait_ge(built, 1)
                chain(nc.vector.tensor_copy(K["alibi"][:, :], dist[:, :]))
                chain(nc.vector.scalar_tensor_tensor(out=K["alibi"][:, :], in0=K["alibi"][:, :], scalar=-1.0, in1=K["alibi"][:, :], op0=ALU.mult, op1=ALU.min))
                chain(nc.vector.tensor_scalar(K["alibi"][:, :], K["alibi"][:, :], 2.0 ** (-8.0 / H) / SCALE, None, ALU.mult))
                dve.wait_ge(drained, NT)
                dve.wait_ge(acted, 6)


def head_order(last):
    order = [("A_logits", 0), ("D_squares", 0), ("A_bias", 0), ("D_norms", 0), ("A_exp", 0), ("D_unit", 0), ("D_keys", 0)]

    def attend(t):
        out = [("A_turn_p", t)]
        if t + 1 < NT:
            out += [("A_logits", t + 1), ("A_bias", t + 1), ("A_exp", t + 1)]
        if t:
            out += [("A_turn_o", t - 1)]
        return out + [("A_values", t)]

    order += attend(0) + [("D_turn", 0)] + attend(1) + [("D_turn", 1), ("D_turn", 2)] + attend(2)
    order += [("D_turn", 3), ("D_turn", 4)]
    for t in range(TILES):
        order += [("D_decay", t)]
        if t:
            order += [("D_gram", t - 1)]
        if t == 4:
            order += attend(3)
    order += [("D_gram", TILES - 1)]
    order += [("D_first", g) for g in range(len(QUADS))]
    fill = [] if last else [("N_rows", 0), ("N_tails", 0)] + [("N_tap", n) for n in range(3)] \
        + [("N_conv", n * (CONV - 1) + j) for n in range(3) for j in range(CONV - 1)] + [("N_silu", n) for n in range(3)]
    fill += [("D_gate", 0)]
    n = len(LEVEL_STEPS) + LAG
    for s in range(n):
        order += [("D_level", s)]
        while fill and len(fill) > (n - 1 - s) * 17 // n:
            order += [fill.pop(0)]
    rest = [x for t in range(4, NT) for x in attend(t)] + [("A_turn_o", NT - 1)]
    share = lambda k: [rest.pop(0) for _ in range(min(k, len(rest)))]
    for t in range(TILES):
        order += [("D_solve", t)]
        if t in (2, 5):
            order += share(2)
    for step in ("D_sample_state", "D_sample_turn", "D_sample_new", "D_sample_out"):
        order += [(step, 0)] + share(2)
    for t in range(NT):
        order += [("D_state", t)] + share(2)
    order += share(len(rest)) + [("D_out_squares", 0)]
    if not last:
        order += [("N_turn", t) for t in range(5)]
    order += [("D_out_norms", 0)]
    if not last:
        order += [("N_turn", t) for t in range(5, TILES)]
    return order + [("D_out", g) for g in range(3)]


QUADS = [(0, 4), (4, 8), (8, 9)]
PAIRS5 = [(0, 2), (2, 4), (4, 6), (6, 8), (8, 9)]
LEVEL_STEPS = [(m, g) for m in range(1, LEVELS) for g in range(5) if g < 4 or m < SAMPLE_LEVELS]
LAG = 2
PREPARE = [("N_rows", 0), ("N_tails", 0)] + [("N_tap", n) for n in range(3)] + [("N_conv", i) for i in range(9)] \
    + [("N_silu", n) for n in range(3)] + [("N_turn", t) for t in range(TILES)]


def run_heads(nc, io, scratch, keep, ident):
    with ExitStack() as ctx:
        def sbt(name, shape, dt=F32):
            return ctx.enter_context(nc.sbuf_tensor(name, shape, dt))

        def signal(name, per):
            return Signal(ctx.enter_context(nc.semaphore(name)), per)

        proj, mix = scratch["proj"], scratch["mix"]
        K = keep
        ROWS = DEC_B * 3 + CONV
        conv_rows = sbt("conv_rows", [P, 3, P])
        cw = sbt("cw", [P, 3, ROWS])
        xin = sbt("xin", [P, 3, 3 + SEQ])
        xsm = sbt("xsm", [P, 3, DEC_B, 3 + DEC_T])
        tail = sbt("tail", [P, 3, 3 * (DEC_B + 1)])
        tailN = sbt("tailN", [3 * (DEC_B + 1), 3, P])
        y = sbt("y", [P, 3, TOK])
        nat = sbt("nat", [P, TILES, 3, P])
        qkT = sbt("qkT", [P, TILES, 2, P])
        ssq = sbt("ssq", [P, 3, TILES, 2])
        cur = sbt("cur", [P, GATES, TILES])
        vb, kbe, kd = (sbt(n, [P, TILES, P]) for n in ("vb", "kbe", "kd"))
        dd = [sbt(f"dd{i}", [P, 2, P]) for i in range(2)]
        de = [sbt(f"de{i}", [P, 2, P]) for i in range(2)]
        egl = sbt("egl", [P, NT + DEC_B])
        A = sbt("A", [P, TILES, P])
        Bm = [sbt(f"Bm{i}", [P, TILES, P]) for i in range(2)]
        TU = sbt("TU", [P, TILES, 2, P])
        WT = [sbt(f"WT{i}", [P, 2, P]) for i in range(LAG + 1)]
        qkd = sbt("qkd", [P, TILES, P])
        uw = sbt("uw", [P, TILES, 2, P])
        S = sbt("S", [P, P])
        Ss = sbt("Ss", [P, DEC_B, P])
        vn = sbt("vn", [P, P])
        o = sbt("o", [P, TILES, P])
        zb, za, qa = sbt("zb", [P, TOK]), sbt("za", [P, SEQ]), sbt("qa", [P, SEQ])
        mixB = sbt("mixB", [P, TOK])
        swq = sbt("swq", [P, 2, P])
        vmask = vb[:, 0:DEC_B, :]
        o_sq = kbe
        lg = [sbt(f"lg{i}", [P, SEQ]) for i in range(2)]
        PT = [sbt(f"PT{i}", [P, NT, P]) for i in range(2)]
        am = sbt("am", [P, NT, 4])
        oN = sbt("oN", [P, P])
        mixA = sbt("mixA", [P, SEQ])
        big = ctx.enter_context(nc.psum_tensor("big", [P, 8, 512], F32))

        rows_loaded, x_loaded, qz_loaded, zb_loaded, s_loaded = (signal(n, k) for n, k in (
            ("rows_loaded", 32), ("x_loaded", 96), ("qz_loaded", 32), ("zb_loaded", 16), ("s_loaded", 16)))
        mixa_stored, mixb_stored, state_stored, sm_stored, tail_stored = (signal(n, k) for n, k in (
            ("mixa_stored", 16), ("mixb_stored", 16), ("state_stored", 16), ("sm_stored", 16), ("tail_stored", 32)))
        rows_turned, rows_ready, pads_ready, taps, convolved, silued = (signal(n, k) for n, k in (
            ("rows_turned", 1), ("rows_ready", 1), ("pads_ready", 1), ("taps", 6), ("convolved", 18), ("silued", 3)))
        tails_ready, tails_turned, tails_out, nat_turned, nat_ready = (signal(n, k) for n, k in (
            ("tails_ready", 2), ("tails_turned", 1), ("tails_out", 1), ("nat_turned", TILES), ("nat_ready", TILES)))
        gates_cur, squares, norms, rooted, scaled, kv_scaled = (signal(n, k) for n, k in (
            ("gates_cur", 1), ("squares", 1), ("norms", 5), ("rooted", 1), ("scaled", 1), ("kv_scaled", 3)))
        qk_turned, qk_ready, cum_done, diff_ready, decay_ready, last_ready = (signal(n, k) for n, k in (
            ("qk_turned", 5), ("qk_ready", 5), ("cum_done", TILES), ("diff_ready", 2 * TILES), ("decay_ready", TILES), ("last_ready", TILES)))
        NS = len(LEVEL_STEPS)
        gram_done, a_ready, level_ready, b0_turned, tu_first = (signal(n, k) for n, k in (
            ("gram_done", TILES), ("a_ready", 2 * TILES), ("level_ready", 3 * LEVELS), ("b0_turned", 3), ("tu_first", 6)))
        wt_done, wt_ready, z_done, tu_ready = (signal(n, NS) for n in ("wt_done", "wt_ready", "z_done", "tu_ready"))
        uw_done, uw_ready, state_zero, ws_done, vn_ready, ds_done, s_ready = (signal(n, k) for n, k in (
            ("uw_done", TILES), ("uw_ready", TILES), ("state_zero", 1), ("ws_done", NT), ("vn_ready", NT), ("ds_done", NT), ("s_ready", NT)))
        oo_done, o1_ready, o_ready = signal("oo_done", NT), signal("o1_ready", TILES), signal("o_ready", TILES)
        sm_done, sm_out, sm_back, sm_vn, sm_mask, sm_ds, sm_state = (signal(n, k) for n, k in (
            ("sm_done", 1), ("sm_out", 1), ("sm_back", 1), ("sm_vn", 1), ("sm_mask", 1), ("sm_ds", 3), ("sm_state", DEC_B)))
        o_squares, o_norms, o_rooted, o_scaled, o_turned, zb_silu, mixb_ready = (signal(n, k) for n, k in (
            ("o_squares", 1), ("o_norms", 3), ("o_rooted", 1), ("o_scaled", 1), ("o_turned", 3), ("zb_silu", 1), ("mixb_ready", 3)))
        PARTS = [(t, q) for t in range(NT) for q in range(0, t + 1, 4)]
        za_silu, lg_done, lg_ready, max_ready, bias_ready, exp_ready = (signal(n, k) for n, k in (
            ("za_silu", 1), ("lg_done", NT), ("lg_ready", NT), ("max_ready", NT + 1), ("bias_ready", NT), ("exp_ready", NT)))
        p_turned, p_ready = signal("p_turned", len(PARTS)), signal("p_ready", len(PARTS))
        pv_done, inv_ready, on_ready, on_turned, mixa_ready = (signal(n, NT) for n in ("pv_done", "inv_ready", "on_ready", "on_turned", "mixa_ready"))
        zeros_ready = ctx.enter_context(nc.semaphore("zeros_ready"))
        at = [sum((k + 1) * P for k in range(t)) for t in range(NT)]

        def wait(eng, sig, h, k):
            eng.wait_ge(sig.sem, sig.now(h, k))

        def wait_before(eng, sig, h, k):
            eng.wait_ge(sig.sem, sig.before(h, k))

        def part(t, q):
            return PARTS.index((t, q)) + 1

        def quad(b):
            return big[:, b, :].rearrange("p (t c) -> p t c", t=4)

        def run(order, steps, h):
            for name, k in order:
                if name in steps:
                    steps[name](h + 1 if name[0] == "N" else h, k)

        def over_heads(eng, steps, ranges=((0, H - 1),)):
            run(PREPARE, steps, -1)
            for lo, hi in ranges:
                with eng.Fori(lo, hi) as h:
                    run(head_order(False), steps, h)
            run(head_order(True), steps, H - 1)

        with nc.Block() as block:
            @block.sync
            def _(sp):
                for sig in (mixa_stored, mixb_stored, state_stored, sm_stored, tail_stored, rows_loaded, x_loaded, qz_loaded, zb_loaded, s_loaded):
                    sp.sem_inc(sig.sem, sig.per)

                def load_x(h):
                    wait_before(sp, rows_turned, h, 1)
                    sp.dma_start(conv_rows[0:3 * DEC_B, :, :], io["state_conv"].rearrange("a b j (n c) -> (a b j) n c", n=3)[:, :, bass.ds(h * P, P)]).then_inc(rows_loaded.sem, 16)
                    sp.dma_start(conv_rows[3 * DEC_B:ROWS, :, :], io["conv_w"].rearrange("a j (n c) -> (a j) n c", n=3)[:, :, bass.ds(h * P, P)]).then_inc(rows_loaded.sem, 16)
                    wait_before(sp, convolved, h, 18)
                    wait_before(sp, tails_ready, h, 2)
                    for n in range(3):
                        rows = proj[bass.ds(h * P + (C_B + n * H * P), P), :]
                        sp.dma_start(xin[:, n, 3:], rows[:, 0:SEQ]).then_inc(x_loaded.sem, 16)
                        sp.dma_start(xsm[:, n, :, 3:], rows[:, SEQ:TOK].rearrange("p (b t) -> p b t", b=DEC_B)).then_inc(x_loaded.sem, 16)

                def load_qz(h):
                    wait_before(sp, lg_done, h, NT)
                    wait_before(sp, mixa_ready, h, NT)
                    sp.dma_start(qa[:, :], proj[bass.ds(h * P + C_Q, P), 0:SEQ]).then_inc(qz_loaded.sem, 16)
                    sp.dma_start(za[:, :], proj[bass.ds(h * P + C_Z, P), 0:SEQ]).then_inc(qz_loaded.sem, 16)

                def load_zb(h):
                    wait_before(sp, mixb_ready, h, 3)
                    sp.dma_start(zb[:, :], proj[bass.ds(h * P + C_ZB, P), :]).then_inc(zb_loaded.sem, 16)

                def load_state(h):
                    wait_before(sp, sm_stored, h, 16)
                    sp.dma_start(Ss[:, :, :], io["state_delta"].rearrange("a b h k v -> k (a h) b v")[:, bass.ds(h, 1), :, :].rearrange("k h b v -> k (h b) v")).then_inc(s_loaded.sem, 16)

                def store_tails(h):
                    wait(sp, tails_out, h, 1)
                    sp.dma_start(io["new_conv_prompt"].rearrange("a b j (n c) -> (a b j) n c", n=3)[:, :, bass.ds(h * P, P)], tailN[3 * DEC_B:, :, :]).then_inc(tail_stored.sem, 16)
                    sp.dma_start(io["new_conv_sample"].rearrange("a b j (n c) -> (a b j) n c", n=3)[:, :, bass.ds(h * P, P)], tailN[0:3 * DEC_B, :, :]).then_inc(tail_stored.sem, 16)

                def store(h):
                    wait(sp, sm_state, h, DEC_B)
                    sp.dma_start(io["new_delta_sample"].rearrange("a b h k v -> k (a h) b v")[:, bass.ds(h, 1), :, :].rearrange("k h b v -> k (h b) v"), Ss[:, :, :]).then_inc(sm_stored.sem, 16)
                    wait(sp, mixa_ready, h, NT)
                    sp.dma_start(mix[bass.ds(h * P, P), 0:SEQ], mixA[:, :]).then_inc(mixa_stored.sem, 16)

                def store_end(h):
                    wait(sp, s_ready, h, NT)
                    sp.dma_start(io["new_delta_prompt"].rearrange("a b h k v -> k (a b h) v")[:, bass.ds(h, 1), :], S[:, :].unsqueeze(1)).then_inc(state_stored.sem, 16)
                    wait(sp, mixb_ready, h, 3)
                    sp.dma_start(mix[bass.ds(h * P + H * P, P), :], mixB[:, :]).then_inc(mixb_stored.sem, 16)

                sp.wait_ge(zeros_ready, 2)
                load_x(0)
                load_qz(0)
                store_tails(0)
                with sp.Fori(0, H - 1) as h:
                    load_state(h)
                    load_x(h + 1)
                    load_zb(h)
                    store_tails(h + 1)
                    store(h)
                    load_qz(h + 1)
                    store_end(h)
                load_state(H - 1)
                load_zb(H - 1)
                store(H - 1)
                store_end(H - 1)
                for sig in (mixa_stored, mixb_stored, state_stored, sm_stored, tail_stored):
                    sp.wait_ge(sig.sem, sig.now(H - 1, sig.per))

            @block.gpsimd
            def _(pool):
                for sig in (kv_scaled, level_ready, sm_mask):
                    pool.sem_inc(sig.sem, sig.per)
                bc = lambda g: cur[:, g, :].unsqueeze(2).to_broadcast([P, TILES, P])

                def scale_keys(h, _k):
                    wait(pool, scaled, h, 1)
                    pool.tensor_tensor(kbe[:, :, :], nat[:, :, 1, :], bc(G_BETA_EXP), ALU.mult).then_inc(kv_scaled.sem, 1)
                    pool.tensor_tensor(kd[:, :, :], nat[:, :, 1, :], bc(G_REST), ALU.mult).then_inc(kv_scaled.sem, 1)
                    pool.tensor_tensor(vb[:, :, :], nat[:, :, 2, :], bc(G_BETA), ALU.mult).then_inc(kv_scaled.sem, 1)

                def level(h, m, g):
                    lo, hi = QUADS[g]
                    n = hi - lo
                    if m >= 2:
                        wait(pool, level_ready, h, 3 * (m - 2) + g + 1)
                    pool.tensor_tensor(Bm[m % 2][:, lo:hi, :], A[:, lo:hi, :], K["level"][:, m, :].unsqueeze(1).to_broadcast([P, n, P]), ALU.mult).then_inc(level_ready.sem, 1)

                def first(h, g):
                    wait(pool, a_ready, h, 2 * QUADS[g][1])
                    if g == 0:
                        wait_before(pool, level_ready, h, 3 * LEVELS)
                        wait_before(pool, wt_done, h, NS)
                    level(h, 0, g)

                def levels(h, s):
                    if s == 0:
                        for g in range(3):
                            level(h, 1, g)
                        wait(pool, tu_first, h, 6)
                        for g in range(3):
                            level(h, 2, g)
                    for m in range(3, LEVELS):
                        if s == max(i for i, (mm, _) in enumerate(LEVEL_STEPS) if mm == m - 2) + 1:
                            wait(pool, wt_done, h, s)
                            for g in range(3):
                                level(h, m, g)

                def sample_mask(h, _k):
                    wait(pool, sm_vn, h, 1)
                    pool.tensor_tensor(vmask, vn[:, :].unsqueeze(1).to_broadcast([P, DEC_B, P]), K["segcol"][:, :].unsqueeze(2).to_broadcast([P, DEC_B, P]), ALU.mult).then_inc(sm_mask.sem, 1)

                pool.memset(xin[:, :, 0:3], 0.0).then_inc(zeros_ready, 1)
                pool.memset(conv_rows[:, :, :], 0.0).then_inc(zeros_ready, 1)
                over_heads(pool, {"D_keys": scale_keys, "D_first": first, "D_level": levels, "D_sample_out": sample_mask})

            @block.scalar
            def _(act):
                for sig in (rows_ready, taps, silued, tails_ready, tails_out, nat_ready, squares, rooted, qk_ready, decay_ready, last_ready, wt_ready, uw_ready,
                            o1_ready, sm_out, o_squares, o_rooted, zb_silu, za_silu, exp_ready, p_ready):
                    act.sem_inc(sig.sem, sig.per)
                act.wait_ge(zeros_ready, 2)
                do = nc.scalar.activation
                copy = lambda out, in_, **kw: nc.scalar.activation(out, in_, ACT.Copy, **kw)

                def rows(h, _k):
                    wait(act, rows_turned, h, 1)
                    copy(cw[:, :, :], big[:, 6, 0:3 * P].rearrange("p (n c) -> p n c", n=3)[:, :, 0:ROWS]).then_inc(rows_ready.sem, 1)

                def tails(h, _k):
                    wait(act, x_loaded, h, 96)
                    wait_before(act, tails_turned, h, 1)
                    copy(tail[:, :, 0:3 * DEC_B].rearrange("p n (b j) -> p n b j", b=DEC_B), xsm[:, :, :, DEC_T:]).then_inc(tails_ready.sem, 1)
                    copy(tail[:, :, 3 * DEC_B:], xin[:, :, SEQ:]).then_inc(tails_ready.sem, 1)
                    wait(act, tails_turned, h, 1)
                    act.wait_ge(tail_stored.sem, tail_stored.before(h, 32))
                    copy(tailN[:, :, :], big[0:27, 7, 0:3 * P].rearrange("p (n c) -> p n c", n=3)).then_inc(tails_out.sem, 1)

                def tap(h, n):
                    if n == 0:
                        wait(act, pads_ready, h, 1)
                        wait_before(act, nat_turned, h, TILES)
                    w = cw[:, n, 3 * DEC_B:3 * DEC_B + 1]
                    copy(y[:, n, 0:SEQ], xin[:, n, 0:SEQ], scale=w).then_inc(taps.sem, 1)
                    copy(y[:, n, SEQ:].rearrange("p (b t) -> p b t", b=DEC_B), xsm[:, n, :, 0:DEC_T], scale=w).then_inc(taps.sem, 1)

                def silu(h, n):
                    wait(act, convolved, h, 6 * n + 6)
                    do(y[:, n, :], y[:, n, :], ACT.Silu).then_inc(silued.sem, 1)

                def natural(h, t):
                    if t == 0:
                        wait_before(act, kv_scaled, h, 3)
                    wait(act, nat_turned, h, t + 1)
                    copy(nat[:, t, :, :], big[:, 4 + t % 4, 0:3 * P].rearrange("p (n c) -> p n c", n=3)).then_inc(nat_ready.sem, 1)

                def head_squares(h, _k):
                    wait(act, qz_loaded, h, 32)
                    do(za[:, :], za[:, :], ACT.Silu).then_inc(za_silu.sem, 1)
                    wait(act, nat_ready, h, TILES)
                    wait_before(act, o_ready, h, TILES)
                    do(qkT[:, :, :, :], nat[:, :, 0:2, :], ACT.Square).then_inc(squares.sem, 1)

                def root(h, _k):
                    wait(act, norms, h, 3)
                    do(ssq[:, 1, :, :], ssq[:, 2, :, :], ACT.Sqrt).then_inc(rooted.sem, 1)

                def qk_out(h, i):
                    k = min(2, TILES - 2 * i)
                    wait(act, qk_turned, h, i + 1)
                    copy(qkT[:, 2 * i:2 * i + k, :, :], quad(i % 2)[:, 0:2 * k, :].rearrange("p (t n) c -> p t n c", n=2)).then_inc(qk_ready.sem, 1)

                def decay(h, t):
                    wait(act, diff_ready, h, 2 * t + 2)
                    if t >= 2:
                        wait(act, a_ready, h, 2 * t - 2)
                    do(de[t % 2][:, :, :], dd[t % 2][:, :, :], ACT.Exp).then_inc(decay_ready.sem, 1)
                    cum = big[:, 2 + t % 2, :]
                    if t < NT:
                        do(egl[:, t:t + 1], cum[:, P - 1:P], ACT.Exp).then_inc(last_ready.sem, 1)
                    else:
                        do(egl[:, NT:], cum[:, 0:P].rearrange("p (b t) -> p b t", t=DEC_T)[:, :, DEC_T - 1], ACT.Exp).then_inc(last_ready.sem, 1)

                def level(h, s):
                    if s < NS:
                        lo, hi = PAIRS5[LEVEL_STEPS[s][1]]
                        wait(act, wt_done, h, s + 1)
                        if s > LAG:
                            wait(act, z_done, h, s - LAG)
                        copy(WT[s % (LAG + 1)][:, 0:hi - lo, :], quad(s % 2)[:, 0:hi - lo, :]).then_inc(wt_ready.sem, 1)

                def gate_b(h, _k):
                    wait(act, zb_loaded, h, 16)
                    do(zb[:, :], zb[:, :], ACT.Silu).then_inc(zb_silu.sem, 1)

                def solve(h, t):
                    wait(act, uw_done, h, t + 1)
                    copy(uw[:, t, :, :], big[:, t % 2, 0:2 * P].rearrange("p (n c) -> p n c", n=2)).then_inc(uw_ready.sem, 1)

                def sample_state(h, _k):
                    wait(act, sm_done, h, 1)
                    copy(swq[:, :, :].rearrange("p n (b t) -> p b n t", b=DEC_B), big[:, 2, 0:2 * P].rearrange("p (b n t) -> p b n t", b=DEC_B, n=2)).then_inc(sm_out.sem, 1)

                def sample_new(h, _k):
                    wait(act, sm_vn, h, 1)
                    copy(o[:, NT, :], big[:, 3, P:2 * P], scale=cur[:, G_EXP, NT:TILES]).then_inc(o1_ready.sem, 1)

                def state(h, t):
                    wait(act, oo_done, h, t + 1)
                    copy(o[:, t, :], big[:, 2 + t % 2, 0:P], scale=cur[:, G_EXP, t:t + 1]).then_inc(o1_ready.sem, 1)

                def out_squares(h, _k):
                    wait(act, o_ready, h, TILES)
                    do(o_sq[:, :, :], o[:, :, :], ACT.Square).then_inc(o_squares.sem, 1)

                def out_root(h, _k):
                    wait(act, o_norms, h, 3)
                    do(ssq[:, 2, :, 0], ssq[:, 1, :, 0], ACT.Sqrt).then_inc(o_rooted.sem, 1)

                def exps(h, t):
                    w = (t + 1) * P
                    wait(act, bias_ready, h, t + 1)
                    do(lg[t % 2][:, 0:w], lg[t % 2][:, 0:w], ACT.Exp, scale=SCALE, bias=am[:, t, 1:2], accum_out=am[:, t, 2:3]).then_inc(exp_ready.sem, 1)

                def p_out(h, t):
                    for q in range(0, t + 1, 4):
                        k = min(4, t + 1 - q)
                        wait(act, p_turned, h, part(t, q))
                        if q == 0 and t >= 2:
                            wait(act, pv_done, h, t - 1)
                        copy(PT[t % 2][:, q:q + k, :], quad(6)[:, 0:k, :]).then_inc(p_ready.sem, 1)

                over_heads(act, {
                    "N_rows": rows, "N_tails": tails, "N_tap": tap, "N_silu": silu, "N_turn": natural,
                    "D_squares": head_squares, "D_norms": root, "D_turn": qk_out, "D_decay": decay, "D_level": level,
                    "D_gate": gate_b, "D_solve": solve, "D_sample_state": sample_state, "D_sample_new": sample_new,
                    "D_state": state, "D_out_squares": out_squares, "D_out_norms": out_root,
                    "A_exp": exps, "A_turn_p": p_out})

            @block.tensor
            def _(pe):
                for sig in (rows_turned, tails_turned, nat_turned, qk_turned, cum_done, gram_done, b0_turned, wt_done, z_done, uw_done, ws_done, ds_done,
                            oo_done, sm_done, sm_back, sm_ds, o_turned, lg_done, p_turned, pv_done, on_turned):
                    pe.sem_inc(sig.sem, sig.per)

                def rows(h, _k):
                    wait(pe, rows_loaded, h, 32)
                    wait_before(pe, p_ready, h, part(3, 0))
                    wait_before(pe, nat_ready, h, TILES)
                    for n in range(3):
                        last = pe.transpose(big[:, 6, n * P:(n + 1) * P], conv_rows[:, n, :], ident[:, :])
                    last.then_inc(rows_turned.sem, 1)

                def tails(h, _k):
                    wait(pe, tails_ready, h, 2)
                    wait_before(pe, on_ready, h, 4)
                    for n in range(3):
                        last = pe.transpose(big[0:27, 7, n * P:(n + 1) * P], tail[:, n, :], ident[:, :])
                    last.then_inc(tails_turned.sem, 1)

                def natural(h, t):
                    if t == 0:
                        wait(pe, silued, h, 3)
                        wait_before(pe, lg_ready, h, NT)
                    if t == 2:
                        wait_before(pe, p_ready, h, len(PARTS))
                        wait(pe, rows_ready, h, 1)
                    if t == 3:
                        wait_before(pe, mixa_ready, h, NT)
                        wait(pe, tails_out, h, 1)
                    if t >= 4:
                        wait(pe, nat_ready, h, t - 3)
                    for n in range(3):
                        last = pe.transpose(big[:, 4 + t % 4, n * P:(n + 1) * P], y[:, n, t * P:(t + 1) * P], ident[:, :])
                    last.then_inc(nat_turned.sem, 1)

                def logits_of(kv):
                    def logits(h, t):
                        w = (t + 1) * P
                        if t == 0:
                            wait(pe, qz_loaded, h, 32)
                            wait(pe, nat_ready, h, TILES)
                        else:
                            wait(pe, lg_ready, h, t)
                        for c in range(0, w, 512):
                            e = min(512, w - c)
                            o_ = big[:, 4 + c // 512, 0:e]
                            pe.matmul(o_, K["identb"][:, :], K["mask"][:, at[t] + c:at[t] + c + e], start=True, stop=False)
                            last = pe.matmul(o_, qa[:, t * P:(t + 1) * P], K["kT"][:, kv, c:c + e], start=False, stop=True)
                        last.then_inc(lg_done.sem, 1)
                    return logits

                def turn_p(h, t):
                    wait(pe, exp_ready, h, t + 1)
                    for q in range(0, t + 1, 4):
                        if q or t:
                            wait(pe, p_ready, h, part(t, q) - 1)
                        for kb in range(q, min(q + 4, t + 1)):
                            last = pe.transpose(quad(6)[:, kb - q, :], lg[t % 2][:, kb * P:(kb + 1) * P], ident[:, :])
                        last.then_inc(p_turned.sem, 1)

                def values_of(kv):
                    def values(h, t):
                        wait(pe, p_ready, h, part(t, t // 4 * 4))
                        if t:
                            wait(pe, mixa_ready, h, t)
                        for kb in range(t + 1):
                            last = pe.matmul(big[:, 7, 0:P], PT[t % 2][:, kb, :], K["vN"][:, kb, kv, :], start=(kb == 0), stop=(kb == t))
                        last.then_inc(pv_done.sem, 1)
                    return values

                def turn_o(h, t):
                    wait(pe, on_ready, h, t + 1)
                    pe.transpose(big[:, 7, P:2 * P], oN[:, :], ident[:, :]).then_inc(on_turned.sem, 1)

                def qk_turn(h, i):
                    if i == 0:
                        wait(pe, scaled, h, 1)
                        wait_before(pe, mixb_ready, h, 3)
                    if i >= 2:
                        wait(pe, qk_ready, h, i - 1)
                    for k in range(min(2, TILES - 2 * i)):
                        for n in range(2):
                            last = pe.transpose(quad(i % 2)[:, 2 * k + n, :], nat[:, 2 * i + k, n, :], ident[:, :])
                    last.then_inc(qk_turned.sem, 1)

                def decay(h, t):
                    if t == 0:
                        wait(pe, gates_cur, h, 1)
                    if t >= 2:
                        wait(pe, last_ready, h, t - 1)
                    pe.matmul(big[:, 2 + t % 2, 0:P], cur[:, G_LOG, t:t + 1].to_broadcast([P, P]), K["cum"][:, int(t == NT), :], start=True, stop=True).then_inc(cum_done.sem, 1)
                    if t == 0:
                        wait(pe, qk_ready, h, 5)
                    if t >= 2:
                        wait(pe, a_ready, h, 2 * t - 2)
                    pe.matmul(big[:, t % 2, 0:2 * P], qkT[:, t, 1, :], qkT[:, t, :, :], start=True, stop=True).then_inc(gram_done.sem, 1)

                def first(h, g):
                    lo, hi = QUADS[g]
                    wait(pe, level_ready, h, g + 1)
                    if g == 0:
                        wait(pe, last_ready, h, TILES)
                    if g == 2:
                        wait(pe, tu_first, h, 2)
                    for t in range(lo, hi):
                        last = pe.transpose(quad(2 + g % 2)[:, t - lo, :], Bm[0][:, t, :], ident[:, :])
                    last.then_inc(b0_turned.sem, 1)

                def level(h, s):
                    if s < NS:
                        m, g = LEVEL_STEPS[s]
                        lo, hi = PAIRS5[g]
                        if m == 1:
                            wait(pe, tu_first, h, 2 * (g // 2 + 1))
                        else:
                            wait(pe, tu_ready, h, LEVEL_STEPS.index((m - 1, g)) + 1)
                        wait(pe, level_ready, h, 3 * m + g // 2 + 1)
                        if s < 2:
                            wait(pe, a_ready, h, 2 * TILES)
                        else:
                            wait(pe, wt_ready, h, s - 1)
                        for t in range(lo, hi):
                            last = pe.matmul(quad(s % 2)[:, t - lo, :], Bm[m % 2][:, t, :], TU[:, t, 1, :], start=True, stop=True)
                        last.then_inc(wt_done.sem, 1)
                    if s >= LAG:
                        r = s - LAG
                        m, g = LEVEL_STEPS[r]
                        lo, hi = PAIRS5[g]
                        wait(pe, wt_ready, h, r + 1)
                        if r < 2:
                            wait(pe, tu_first, h, 6)
                        else:
                            wait(pe, tu_ready, h, r - 1)
                        for t in range(lo, hi):
                            z = big[:, 2 + r % 2, (t - lo) * 2 * P:(t - lo + 1) * 2 * P]
                            if m < LEVELS - 1:
                                pe.matmul(z[:, 0:P], WT[r % (LAG + 1)][:, t - lo, :], TU[:, t, 0, :], start=True, stop=True)
                            last = pe.matmul(z[:, P:2 * P], TU[:, t, 0, :], WT[r % (LAG + 1)][:, t - lo, :], start=True, stop=True)
                        last.then_inc(z_done.sem, 1)

                def solve(h, t):
                    if t == 0:
                        wait(pe, tu_ready, h, NS)
                        wait(pe, kv_scaled, h, 3)
                    if t >= 2:
                        wait(pe, uw_ready, h, t - 1)
                    pe.matmul(big[:, t % 2, 0:P], TU[:, t, 1, :], vb[:, t, :], start=True, stop=True)
                    pe.matmul(big[:, t % 2, P:2 * P], kbe[:, t, :], TU[:, t, 1, :], start=True, stop=True).then_inc(uw_done.sem, 1)

                def sample_state(h, _k):
                    wait(pe, s_loaded, h, 16)
                    wait(pe, uw_ready, h, TILES)
                    for b in range(DEC_B):
                        tok = slice(b * DEC_T, (b + 1) * DEC_T)
                        pe.matmul(big[:, 2, b * 2 * DEC_T:b * 2 * DEC_T + DEC_T], Ss[:, b, :], uw[:, NT, 1, tok], start=True, stop=True)
                        last = pe.matmul(big[:, 2, b * 2 * DEC_T + DEC_T:(b + 1) * 2 * DEC_T], Ss[:, b, :], qkT[:, NT, 0, tok], start=True, stop=True)
                    last.then_inc(sm_done.sem, 1)

                def sample_turn(h, _k):
                    wait(pe, sm_out, h, 1)
                    pe.transpose(big[:, 3, 0:P], swq[:, 0, :], ident[:, :])
                    pe.transpose(big[:, 3, P:2 * P], swq[:, 1, :], ident[:, :]).then_inc(sm_back.sem, 1)

                def sample_out(h, _k):
                    wait(pe, sm_vn, h, 1)
                    pe.matmul(big[:, 0, 0:P], qkd[:, NT, :], vn[:, :], start=True, stop=True).then_inc(sm_ds.sem, 1)
                    wait(pe, sm_mask, h, 1)
                    for half in range(2):
                        pe.matmul(big[:, 1 + half, :], kd[:, NT, :], vmask[:, 4 * half:4 * half + 4, :], start=True, stop=True).then_inc(sm_ds.sem, 1)

                def state(h, t):
                    if t == 0:
                        wait(pe, state_zero, h, 1)
                        wait(pe, o_ready, h, 1)
                    else:
                        wait(pe, s_ready, h, t)
                    pe.matmul(big[:, 0, 0:P], uw[:, t, 1, :], S[:, :], start=True, stop=True).then_inc(ws_done.sem, 1)
                    if t < 2:
                        wait(pe, sm_state, h, DEC_B)
                        wait(pe, o1_ready, h, 1)
                    else:
                        wait(pe, o_ready, h, t)
                    pe.matmul(big[:, 2 + t % 2, 0:P], qkT[:, t, 0, :], S[:, :], start=True, stop=True)
                    wait(pe, vn_ready, h, t + 1)
                    pe.matmul(big[:, 1, 0:P], kd[:, t, :], vn[:, :], start=True, stop=True).then_inc(ds_done.sem, 1)
                    pe.matmul(big[:, 2 + t % 2, P:2 * P], qkd[:, t, :], vn[:, :], start=True, stop=True).then_inc(oo_done.sem, 1)

                def out(h, g):
                    lo, hi = QUADS[g]
                    if g == 0:
                        wait(pe, o_scaled, h, 1)
                    for t in range(lo, hi):
                        last = pe.transpose(quad(g)[:, t - lo, :], o[:, t, :], ident[:, :])
                    last.then_inc(o_turned.sem, 1)

                def steps(kv):
                    return {
                        "N_rows": rows, "N_tails": tails, "N_turn": natural, "A_logits": logits_of(kv), "A_turn_p": turn_p,
                        "A_values": values_of(kv), "A_turn_o": turn_o, "D_turn": qk_turn, "D_decay": decay, "D_first": first,
                        "D_level": level, "D_solve": solve, "D_sample_state": sample_state, "D_sample_turn": sample_turn,
                        "D_sample_out": sample_out, "D_state": state, "D_out": out}

                run(PREPARE, steps(0), -1)
                with pe.Fori(0, GROUP) as h:
                    run(head_order(False), steps(0), h)
                with pe.Fori(GROUP, H - 1) as h:
                    run(head_order(False), steps(1), h)
                run(head_order(True), steps(1), H - 1)

            @block.vector
            def _(dve):
                for sig in (pads_ready, convolved, norms, gates_cur, scaled, diff_ready, a_ready, tu_first, tu_ready, state_zero, vn_ready, s_ready, o_ready,
                            sm_vn, sm_state, o_norms, o_scaled, mixb_ready, max_ready, lg_ready, bias_ready, inv_ready, on_ready, mixa_ready):
                    dve.sem_inc(sig.sem, sig.per)
                V = nc.vector

                def conv(h, i):
                    n, j = i // 3, i % 3 + 1
                    w = cw[:, n, 3 * DEC_B + j:3 * DEC_B + j + 1]
                    wait(dve, taps, h, 2 * n + 2)
                    if j > 1:
                        wait(dve, convolved, h, 6 * n + 2 * (j - 1))
                    V.scalar_tensor_tensor(out=y[:, n, 0:SEQ], in0=xin[:, n, j:j + SEQ], scalar=w, in1=y[:, n, 0:SEQ], op0=ALU.mult, op1=ALU.add).then_inc(convolved.sem, 1)
                    ys = y[:, n, SEQ:].rearrange("p (b t) -> p b t", b=DEC_B)
                    V.scalar_tensor_tensor(out=ys, in0=xsm[:, n, :, j:j + DEC_T], scalar=w, in1=ys, op0=ALU.mult, op1=ALU.add).then_inc(convolved.sem, 1)

                def rows(h, _k):
                    wait(dve, rows_ready, h, 1)
                    V.tensor_copy(xsm[:, :, :, 0:3], cw[:, :, 0:3 * DEC_B].rearrange("p n (b j) -> p n b j", b=DEC_B)).then_inc(pads_ready.sem, 1)

                def bias(h, t):
                    w = (t + 1) * P
                    if t == 0:
                        wait_before(dve, max_ready, h, NT + 1)
                        wait_before(dve, p_turned, h, len(PARTS))
                    wait(dve, lg_done, h, t + 1)
                    if t >= 2:
                        wait(dve, p_turned, h, part(t - 1, 0) - 1)
                    src = big[:, 4:6, :].rearrange("p b c -> p (b c)")[:, 0:w]
                    V.tensor_tensor(lg[t % 2][:, 0:w], src, K["alibi"][:, SEQ - w:SEQ], ALU.add).then_inc(lg_ready.sem, 1)
                    wait(dve, lg_ready, h, t + 1)
                    V.tensor_reduce(am[:, t, 0:1], lg[t % 2][:, 0:w], AX_X, ALU.max).then_inc(max_ready.sem, 1)
                    wait(dve, max_ready, h, t + 1)
                    V.tensor_scalar(am[:, t, 1:2], am[:, t, 0:1], -SCALE, None, ALU.mult).then_inc(bias_ready.sem, 1)
                    if t == NT - 1:
                        V.tensor_scalar(K["alibi"][:, :], K["alibi"][:, :], 2.0 ** (-8.0 / H), None, ALU.mult).then_inc(max_ready.sem, 1)

                def values(h, t):
                    wait(dve, exp_ready, h, t + 1)
                    V.reciprocal(am[:, t, 3:4], am[:, t, 2:3]).then_inc(inv_ready.sem, 1)
                    wait(dve, inv_ready, h, t + 1)
                    wait(dve, pv_done, h, t + 1)
                    V.tensor_scalar(oN[:, :], big[:, 7, 0:P], am[:, t, 3:4], None, ALU.mult).then_inc(on_ready.sem, 1)

                def turn_o(h, t):
                    if t == 0:
                        wait(dve, za_silu, h, 1)
                        wait_before(dve, mixa_stored, h, 16)
                    wait(dve, on_turned, h, t + 1)
                    V.tensor_tensor(mixA[:, t * P:(t + 1) * P], big[:, 7, P:2 * P], za[:, t * P:(t + 1) * P], ALU.mult).then_inc(mixa_ready.sem, 1)

                def head_norms(h, _k):
                    wait_before(dve, o_ready, h, TILES)
                    wait_before(dve, kv_scaled, h, 3)
                    wait_before(dve, mixb_ready, h, 3)
                    V.tensor_copy(cur[:, :, :], K["gates"][:, bass.ds(h, 1), :, :].rearrange("p h g t -> p (h g) t")).then_inc(gates_cur.sem, 1)
                    wait(dve, squares, h, 1)
                    V.tensor_reduce(ssq[:, 0, :, :], qkT[:, :, :, :], AX_X, ALU.add).then_inc(norms.sem, 1)
                    wait(dve, norms, h, 1)
                    V.tensor_scalar(ssq[:, 1, :, :], ssq[:, 0, :, :], EPS, None, ALU.add).then_inc(norms.sem, 1)
                    wait(dve, norms, h, 2)
                    V.reciprocal(ssq[:, 2, :, :], ssq[:, 1, :, :]).then_inc(norms.sem, 1)

                def unit(h, _k):
                    wait(dve, rooted, h, 1)
                    V.tensor_scalar(ssq[:, 2, :, 0], ssq[:, 1, :, 0], SCALE, None, ALU.mult).then_inc(norms.sem, 1)
                    V.tensor_copy(ssq[:, 2, :, 1], ssq[:, 1, :, 1]).then_inc(norms.sem, 1)
                    wait(dve, norms, h, 5)
                    V.tensor_tensor(nat[:, :, 0:2, :], nat[:, :, 0:2, :], ssq[:, 2, :, :].unsqueeze(3).to_broadcast([P, TILES, 2, P]), ALU.mult).then_inc(scaled.sem, 1)

                def decay(h, t):
                    s = int(t == NT)
                    cum = big[:, 2 + t % 2, 0:P]
                    gc = cur[:, G_CUM, t:t + 1]
                    wait(dve, cum_done, h, t + 1)
                    if t == 0:
                        wait(dve, gates_cur, h, 1)
                    if t >= 2:
                        wait(dve, decay_ready, h, t - 1)
                    V.scalar_tensor_tensor(out=dd[t % 2][:, 0, :], in0=cum, scalar=gc, in1=K["dmT"][:, s, :], op0=ALU.subtract, op1=ALU.add).then_inc(diff_ready.sem, 1)
                    V.scalar_tensor_tensor(out=dd[t % 2][:, 1, :], in0=cum, scalar=gc, in1=K["dmN"][:, s, :], op0=ALU.subtract, op1=ALU.subtract, reverse1=True).then_inc(diff_ready.sem, 1)

                def gram(h, t):
                    if t == 0:
                        wait_before(dve, level_ready, h, 3 * LEVELS)
                    wait(dve, gram_done, h, t + 1)
                    wait(dve, decay_ready, h, t + 1)
                    V.tensor_tensor(qkd[:, t, :], big[:, t % 2, 0:P], de[t % 2][:, 0, :], ALU.mult).then_inc(a_ready.sem, 1)
                    V.scalar_tensor_tensor(out=A[:, t, :], in0=big[:, t % 2, P:2 * P], scalar=cur[:, G_BETA, t:t + 1], in1=de[t % 2][:, 1, :], op0=ALU.mult, op1=ALU.mult).then_inc(a_ready.sem, 1)

                def first(h, g):
                    lo, hi = QUADS[g]
                    eye = ident[:, :].unsqueeze(1).to_broadcast([P, hi - lo, P])
                    wait(dve, level_ready, h, g + 1)
                    V.tensor_tensor(TU[:, lo:hi, 0, :], eye, Bm[0][:, lo:hi, :], ALU.subtract).then_inc(tu_first.sem, 1)
                    wait(dve, b0_turned, h, g + 1)
                    V.tensor_tensor(TU[:, lo:hi, 1, :], eye, quad(2 + g % 2)[:, 0:hi - lo, :], ALU.subtract).then_inc(tu_first.sem, 1)

                def level(h, s):
                    if s < LAG:
                        return
                    r = s - LAG
                    m, g = LEVEL_STEPS[r]
                    lo, hi = PAIRS5[g]
                    wait(dve, z_done, h, r + 1)
                    if m == 1:
                        wait(dve, tu_first, h, 6)
                    else:
                        wait(dve, tu_ready, h, LEVEL_STEPS.index((m - 1, g)) + 1)
                    z = big[:, 2 + r % 2, :].rearrange("p (t n c) -> p t n c", t=2, n=2)[:, 0:hi - lo, :, :]
                    n0 = 0 if m < LEVELS - 1 else 1
                    V.tensor_tensor(TU[:, lo:hi, n0:, :], TU[:, lo:hi, n0:, :], z[:, :, n0:, :], ALU.subtract).then_inc(tu_ready.sem, 1)

                def sample_new(h, _k):
                    wait(dve, sm_back, h, 1)
                    V.tensor_tensor(vn[:, :], uw[:, NT, 0, :], big[:, 3, 0:P], ALU.subtract).then_inc(sm_vn.sem, 1)

                def sample_out(h, _k):
                    wait(dve, sm_ds, h, 1)
                    wait(dve, o1_ready, h, 1)
                    V.tensor_tensor(o[:, NT, :], o[:, NT, :], big[:, 0, 0:P], ALU.add).then_inc(o_ready.sem, 1)
                    wait_before(dve, state_stored, h, 16)
                    V.memset(S[:, :], 0.0).then_inc(state_zero.sem, 1)
                    for b in range(DEC_B):
                        wait(dve, sm_ds, h, 2 + b // 4)
                        V.scalar_tensor_tensor(out=Ss[:, b, :], in0=Ss[:, b, :], scalar=egl[:, NT + b:NT + b + 1], in1=big[:, 1 + b // 4, b % 4 * P:(b % 4 + 1) * P], op0=ALU.mult, op1=ALU.add).then_inc(sm_state.sem, 1)

                def add_out(h, t):
                    wait(dve, o1_ready, h, t + 2)
                    V.tensor_tensor(o[:, t, :], o[:, t, :], big[:, 2 + t % 2, P:2 * P], ALU.add).then_inc(o_ready.sem, 1)

                def state(h, t):
                    wait(dve, ws_done, h, t + 1)
                    if t == 0:
                        wait(dve, sm_ds, h, 3)
                    else:
                        wait(dve, oo_done, h, t)
                    V.tensor_tensor(vn[:, :], uw[:, t, 0, :], big[:, 0, 0:P], ALU.subtract).then_inc(vn_ready.sem, 1)
                    if t:
                        add_out(h, t - 1)
                    wait(dve, ds_done, h, t + 1)
                    if t == 0:
                        wait(dve, state_zero, h, 1)
                    V.scalar_tensor_tensor(out=S[:, :], in0=S[:, :], scalar=egl[:, t:t + 1], in1=big[:, 1, 0:P], op0=ALU.mult, op1=ALU.add).then_inc(s_ready.sem, 1)
                    if t == NT - 1:
                        add_out(h, t)

                def out_norms(h, _k):
                    wait(dve, o_squares, h, 1)
                    V.tensor_reduce(ssq[:, 0, :, 0], o_sq[:, :, :], AX_X, ALU.add).then_inc(o_norms.sem, 1)
                    wait(dve, o_norms, h, 1)
                    V.tensor_scalar(ssq[:, 0, :, 1], ssq[:, 0, :, 0], 1.0 / HD, EPS, ALU.mult, ALU.add).then_inc(o_norms.sem, 1)
                    wait(dve, o_norms, h, 2)
                    V.reciprocal(ssq[:, 1, :, 0], ssq[:, 0, :, 1]).then_inc(o_norms.sem, 1)
                    wait(dve, o_rooted, h, 1)
                    V.tensor_tensor(o[:, :, :], o[:, :, :], ssq[:, 2, :, 0].unsqueeze(2).to_broadcast([P, TILES, P]), ALU.mult).then_inc(o_scaled.sem, 1)

                def out(h, g):
                    lo, hi = QUADS[g]
                    wait(dve, o_turned, h, g + 1)
                    if g == 0:
                        wait(dve, zb_silu, h, 1)
                        wait_before(dve, mixb_stored, h, 16)
                    V.scalar_tensor_tensor(out=mixB[:, lo * P:hi * P], in0=big[:, g, 0:(hi - lo) * P], scalar=K["gnw"][:, 0:1], in1=zb[:, lo * P:hi * P], op0=ALU.mult, op1=ALU.mult).then_inc(mixb_ready.sem, 1)

                over_heads(dve, {
                    "N_rows": rows, "N_conv": conv, "A_bias": bias, "A_values": values, "A_turn_o": turn_o,
                    "D_norms": head_norms, "D_unit": unit, "D_decay": decay, "D_gram": gram, "D_first": first, "D_level": level,
                    "D_sample_new": sample_new, "D_sample_out": sample_out, "D_state": state, "D_out_norms": out_norms, "D_out": out})


def kept_tensors(nc, ctx):
    shapes = {
        "kT": ([P, KV, SEQ], F32), "vN": ([P, NT, KV, P], F32), "mask": ([P, NT * (NT + 1) // 2 * P], BF16),
        "alibi": ([P, SEQ], F32), "gates": ([P, H, GATES, TILES], F32), "cum": ([P, 2, P], F32),
        "dmT": ([P, 2, P], F32), "dmN": ([P, 2, P], F32), "level": ([P, LEVELS, P], F32),
        "segcol": ([P, DEC_B], F32), "gnw": ([P, 1], F32), "identb": ([P, P], BF16),
    }
    return {n: ctx.enter_context(nc.sbuf_tensor("keep_" + n, s, dt)) for n, (s, dt) in shapes.items()}


def attend_samples(nc, io, scratch, keep, ident):
    with ExitStack() as ctx:
        def sbt(name, shape, dt=F32):
            return ctx.enter_context(nc.sbuf_tensor(name, shape, dt))

        def sem(name):
            return ctx.enter_context(nc.semaphore(name))

        proj, mix = scratch["proj"], scratch["mix"]
        PAIRS = DEC_B // 2
        UNITS = KV * PAIRS
        SLICES = ((0, P), (P, P), (2 * P, DEC_T))
        qs = sbt("qs", [P, KV, DEC_B, GROUP, DEC_T])
        zs = sbt("zs", [P, H, P])
        kn = sbt("kn", [P, DEC_B, 2, KV * P])
        kT = sbt("kTs", [P, KV, DEC_B, LS])
        vn = sbt("vns", [P, DEC_B, 2, KV * P])
        vnew = sbt("vnew", [DEC_T, DEC_B, KV * P])
        smask = sbt("smask", [P, LS], BF16)
        rsel = sbt("rsel", [P, PAIRS, P], BF16)
        row = sbt("row", [P, LS], mybir.dt.int32)
        rowf = sbt("rowf", [P, LS])
        col = sbt("col", [P, 4])
        pcol = sbt("pcol", [P, 1], mybir.dt.int32)
        bval = sbt("bval", [P, 3, DEC_B])
        alibi = sbt("alibis", [P, KV, LS])
        lg = [sbt(f"lgs{i}", [P, LS]) for i in range(2)]
        pT = [sbt(f"pT{i}", [P, 3, P]) for i in range(2)]
        am = sbt("ams", [P, UNITS, 4])
        oN = [sbt(f"oNs{i}", [P, P]) for i in range(2)]
        mixS = sbt("mixS", [P, H, P])
        bank = [ctx.enter_context(nc.psum_tensor(f"sb{i}", [P, 512], F32)) for i in range(8)]

        cache_loaded, q_loaded, z_loaded, v_loaded, tabled, stepped, silued = map(
            sem, ["cache_loaded", "qs_loaded", "zs_loaded", "v_loaded", "s_tabled", "s_stepped", "s_silued"])
        turned, moved, lg_done, lg_ready, bias_ready, exp_ready = map(
            sem, ["s_turned", "s_moved", "s_lg_done", "s_lg_ready", "s_bias_ready", "s_exp_ready"])
        p_turned, p_ready, pv_done, inv_ready, on_ready, on_turned, mixed, stored = map(
            sem, ["s_p_turned", "s_p_ready", "s_pv_done", "s_inv_ready", "s_on_ready", "s_on_turned", "s_mixed", "s_stored"])

        with nc.Block() as block:
            @block.sync
            def _(sp):
                sp.dma_start(kn[:, :, :, :], io["cache_k"].rearrange("a b (n p) k d -> p (a b) n (k d)", p=P)).then_inc(cache_loaded, 16)
                for k in range(KV):
                    for b in range(DEC_B):
                        at = SEQ + b * DEC_T
                        rows = slice(C_Q + k * GROUP * P, C_Q + (k + 1) * GROUP * P)
                        sp.dma_start(qs[:, k, b, :, :], proj[rows, at:at + DEC_T].rearrange("(g d) t -> d g t", d=P)).then_inc(q_loaded, 16)
                    sp.dma_start(kT[:, k, :, PAST:], proj[C_K + k * P:C_K + (k + 1) * P, SEQ:].rearrange("d (b t) -> d b t", b=DEC_B)).then_inc(q_loaded, 16)
                sp.dma_start(smask[:, :], scratch["sample_mask"]).then_inc(q_loaded, 16)
                sp.dma_start(vn[:, :, :, :], io["cache_v"].rearrange("a b (n p) k d -> p (a b) n (k d)", p=P)).then_inc(v_loaded, 16)
                sp.dma_start(vnew[:, :, :], io["new_v_sample"].rearrange("a b t k d -> t (a b) (k d)")).then_inc(v_loaded, 16)
                sp.dma_start(zs[:, :, :], proj[C_Z:C_QI, SEQ:].rearrange("(h d) t -> d h t", d=P)).then_inc(z_loaded, 16)
                sp.wait_ge(mixed, UNITS)
                sp.dma_start(mix[0:H * P, SEQ:].rearrange("(h d) t -> d h t", d=P), mixS[:, :, :]).then_inc(stored, 16)
                sp.wait_ge(stored, 16)

            @block.gpsimd
            def _(pool):
                n = [0]

                def chain(instruction):
                    n[0] += 1
                    instruction.then_inc(tabled, 1)
                    pool.wait_ge(tabled, n[0])

                chain(pool.memset(rsel[:, :, :], 0.0))
                chain(pool.affine_select(out=rsel[:, :, :], in_=rsel[:, :, :], compare_op=ALU.not_equal, fill=1.0, base=0,
                                         pattern=[[-2 * DEC_T, PAIRS], [-DEC_T, 2], [0, GROUP], [-1, DEC_T]], channel_multiplier=1))
                chain(pool.iota(row[:, :], pattern=[[-1, LS]], base=PAST, channel_multiplier=0))
                chain(pool.iota(pcol[:, :], pattern=[[0, 1]], base=0, channel_multiplier=1))
                for b in range(DEC_B):
                    chain(pool.memset(bval[:, 0, b:b + 1], float(DEC_T * b)))
                    chain(pool.memset(bval[:, 1, b:b + 1], 2.0 ** (-8.0 * (b % GROUP + 1) / H) / SCALE))

            @block.tensor
            def _(pe):
                pe.wait_ge(cache_loaded, 16)
                for k in range(KV):
                    for pair in range(PAIRS):
                        i = k * PAIRS + pair
                        if i >= 4:
                            pe.wait_ge(moved, i - 3)
                        for j in range(4):
                            last = pe.transpose(bank[i % 4][:, j * P:(j + 1) * P], kn[:, 2 * pair + j // 2, j % 2, k * P:(k + 1) * P], ident[:, :])
                        last.then_inc(turned, 1)
                pe.wait_ge(q_loaded, 16 * (KV * (DEC_B + 1) + 1))
                pe.wait_ge(tabled, 2)
                pe.wait_ge(moved, UNITS)

                def logits(i):
                    k, pair = divmod(i, PAIRS)
                    if i >= 2:
                        pe.wait_ge(lg_ready, i - 1)
                    o = bank[i % 2]
                    pe.matmul(o[:, 0:LS], rsel[:, pair, :], smask[:, :], start=True, stop=False, skip_group_check=True)
                    for j in range(2):
                        b = 2 * pair + j
                        last = pe.matmul(o[j * 64:(j + 1) * 64, 0:LS], qs[:, k, b, :, :].rearrange("p g t -> p (g t)"), kT[:, k, b, :],
                                         start=False, stop=True, skip_group_check=True)
                    last.then_inc(lg_done, 1)

                def turn_out(i):
                    pe.wait_ge(on_ready, i + 1)
                    if i >= 2:
                        pe.wait_ge(mixed, i - 1)
                    pe.transpose(bank[6 + i % 2][:, 0:P], oN[i % 2][:, :], ident[:, :]).then_inc(on_turned, 1)

                logits(0)
                for i in range(UNITS):
                    k, pair = divmod(i, PAIRS)
                    if i + 1 < UNITS:
                        logits(i + 1)
                    pe.wait_ge(exp_ready, i + 1)
                    if i >= 2:
                        pe.wait_ge(p_ready, i - 1)
                    for n, (c, w) in enumerate(SLICES):
                        last = pe.transpose(bank[2 + i % 2][0:w, n * P:(n + 1) * P], lg[i % 2][:, c:c + w], ident[:, :])
                    last.then_inc(p_turned, 1)
                    if i:
                        turn_out(i - 1)
                    pe.wait_ge(p_ready, i + 1)
                    if i == 0:
                        pe.wait_ge(v_loaded, 32)
                    if i >= 2:
                        pe.wait_ge(on_ready, i - 1)
                    for j in range(2):
                        b = 2 * pair + j
                        for n, (c, w) in enumerate(SLICES):
                            v = vn[:, b, n, k * P:(k + 1) * P] if n < 2 else vnew[:, b, k * P:(k + 1) * P]
                            last = pe.matmul(bank[4 + i % 2][j * 64:(j + 1) * 64, 0:P], pT[i % 2][0:w, n, j * 64:(j + 1) * 64], v,
                                             start=(n == 0), stop=(n == 2))
                    last.then_inc(pv_done, 1)
                turn_out(UNITS - 1)

            @block.scalar
            def _(act):
                for i in range(UNITS):
                    k, pair = divmod(i, PAIRS)
                    act.wait_ge(turned, i + 1)
                    nc.scalar.activation(kT[:, k, 2 * pair:2 * pair + 2, 0:PAST], bank[i % 4][:, :].rearrange("d (b s) -> d b s", b=2), ACT.Copy).then_inc(moved, 1)
                act.wait_ge(z_loaded, 16)
                nc.scalar.activation(zs[:, :, :], zs[:, :, :], ACT.Silu).then_inc(silued, 1)
                for i in range(UNITS):
                    act.wait_ge(bias_ready, i + 1)
                    nc.scalar.activation(lg[i % 2][:, :], lg[i % 2][:, :], ACT.Exp, scale=SCALE, bias=am[:, i, 1:2], accum_out=am[:, i, 2:3]).then_inc(exp_ready, 1)
                    act.wait_ge(p_turned, i + 1)
                    if i >= 2:
                        act.wait_ge(pv_done, i - 1)
                    nc.scalar.activation(pT[i % 2][:, 0:2, :], bank[2 + i % 2][:, 0:2 * P].rearrange("p (n c) -> p n c", n=2), ACT.Copy)
                    nc.scalar.activation(pT[i % 2][0:DEC_T, 2, :], bank[2 + i % 2][0:DEC_T, 2 * P:3 * P], ACT.Copy).then_inc(p_ready, 1)

            @block.vector
            def _(dve):
                n = [0]

                def chain(instruction):
                    n[0] += 1
                    instruction.then_inc(stepped, 1)
                    dve.wait_ge(stepped, n[0])

                V = nc.vector
                dve.wait_ge(tabled, 4 + 2 * DEC_B)
                chain(V.tensor_tensor(bval[:, 2, :], bval[:, 0, :], keep["segcol"][:, :], ALU.mult))
                chain(V.tensor_reduce(col[:, 0:1], bval[:, 2, :], AX_X, ALU.add))
                chain(V.tensor_tensor(bval[:, 2, :], bval[:, 1, :], keep["segcol"][:, :], ALU.mult))
                chain(V.tensor_reduce(col[:, 2:3], bval[:, 2, :], AX_X, ALU.add))
                chain(V.tensor_copy(col[:, 3:4], pcol[:, :]))
                chain(V.tensor_tensor(col[:, 1:2], col[:, 3:4], col[:, 0:1], ALU.subtract))
                chain(V.tensor_copy(rowf[:, :], row[:, :]))
                chain(V.tensor_scalar(rowf[:, :], rowf[:, :], col[:, 1:2], None, ALU.add))
                chain(V.scalar_tensor_tensor(out=rowf[:, :], in0=rowf[:, :], scalar=-1.0, in1=rowf[:, :], op0=ALU.mult, op1=ALU.min))
                for k in range(KV):
                    chain(V.tensor_scalar(alibi[:, k, :], rowf[:, :], col[:, 2:3], 2.0 ** (-8.0 * k * GROUP / H), ALU.mult, ALU.mult))

                def add(i):
                    dve.wait_ge(lg_done, i + 1)
                    if i >= 2:
                        dve.wait_ge(p_turned, i - 1)
                    V.tensor_tensor(lg[i % 2][:, :], bank[i % 2][:, 0:LS], alibi[:, i // PAIRS, :], ALU.add).then_inc(lg_ready, 1)
                    dve.wait_ge(lg_ready, i + 1)
                    chain(V.tensor_reduce(am[:, i, 0:1], lg[i % 2][:, :], AX_X, ALU.max))
                    V.tensor_scalar(am[:, i, 1:2], am[:, i, 0:1], -SCALE, None, ALU.mult).then_inc(bias_ready, 1)

                def gate(i):
                    k, pair = divmod(i, PAIRS)
                    dve.wait_ge(on_turned, i + 1)
                    out = mixS[:, k * GROUP:(k + 1) * GROUP, 2 * DEC_T * pair:2 * DEC_T * (pair + 1)].rearrange("d g (b t) -> d b g t", b=2)
                    z = zs[:, k * GROUP:(k + 1) * GROUP, 2 * DEC_T * pair:2 * DEC_T * (pair + 1)].rearrange("d g (b t) -> d b g t", b=2)
                    V.tensor_tensor(out, bank[6 + i % 2][:, 0:P].rearrange("d (b g t) -> d b g t", b=2, g=GROUP), z, ALU.mult).then_inc(mixed, 1)

                add(0)
                dve.wait_ge(silued, 1)
                for i in range(UNITS):
                    if i + 1 < UNITS:
                        add(i + 1)
                    if i:
                        gate(i - 1)
                    dve.wait_ge(exp_ready, i + 1)
                    V.reciprocal(am[:, i, 3:4], am[:, i, 2:3]).then_inc(inv_ready, 1)
                    dve.wait_ge(inv_ready, i + 1)
                    dve.wait_ge(pv_done, i + 1)
                    V.tensor_scalar(oN[i % 2][:, :], bank[4 + i % 2][:, 0:P], am[:, i, 3:4], None, ALU.mult).then_inc(on_ready, 1)
                gate(UNITS - 1)


THIRD_TILES = 3
NW = 512


def project_out(nc, io, scratch):
    with ExitStack() as ctx:
        def sbt(name, shape, dt=F32):
            return ctx.enter_context(nc.sbuf_tensor(name, shape, dt))

        def sem(name):
            return ctx.enter_context(nc.semaphore(name))

        mix = scratch["mix"]
        THIRDS = TILES // THIRD_TILES
        CB = D // NW
        QUARTERS = KT // CK
        CH = 4
        TT = THIRD_TILES * P
        raw = [sbt(f"oraw{i}", [P, CK, NW]) for i in range(2)]
        wH = [sbt(f"owH{i}", [P, CK, NW], F32R) for i in range(2)]
        wL = [sbt(f"owL{i}", [P, CK, NW], F32R) for i in range(2)]
        mraw = [sbt(f"mraw{i}", [P, KT // 4, TT]) for i in range(2)]
        mH = sbt("mH", [P, KT, TT], F32R)
        mL = sbt("mL", [P, KT, TT], F32R)
        x = [sbt(f"ox{i}", [P, THIRD_TILES, NW]) for i in range(2)]
        yv = sbt("yv", [P, THIRD_TILES, D])
        fw = sbt("fw", [P, D])
        squares = sbt("osquares", [P, D])
        stat = sbt("ostat", [P, THIRD_TILES, 4])
        bank = [ctx.enter_context(nc.psum_tensor(f"ob{i}", [P, NW], F32)) for i in range(2 * THIRD_TILES)]

        w_loaded = [sem(f"ow_loaded{i}") for i in range(2)]
        x_loaded = [sem(f"ox_loaded{i}") for i in range(2)]
        m_loaded = [sem(f"m_loaded{i}") for i in range(2)]
        fw_loaded = sem("fw_loaded")
        high_ready, low_ready, m_ready, chunk_used = map(sem, ["ohigh_ready", "olow_ready", "m_ready", "ochunk_used"])
        block_done, added, squared, stepped, rooted, scaled, weighted, stored = map(
            sem, ["block_done", "added", "osquared", "ostepped", "orooted", "oscaled", "oweighted", "ystored"])
        w_view = io["w_out"].rearrange("a (k p) n -> (a p) k n", p=P)
        xp = io["x_prompt"].rearrange("b (t p) d -> p (b t) d", p=P)
        xs = io["x_sample"].rearrange("b t d -> (b t) d")
        yp = io["y_prompt"].rearrange("b (t p) d -> p (b t) d", p=P)
        ys = io["y_sample"].rearrange("b t d -> (b t) d")
        units = [(r, c) for r in range(THIRDS) for c in range(CB)]

        with nc.Block() as block:
            @block.sync
            def _(sp):
                sp.dma_start(fw[:, :], io["final_norm_w"].rearrange("(a d) -> a d", a=1).to_broadcast([P, D])).then_inc(fw_loaded, 16)
                n = 0
                for i, (r, c) in enumerate(units):
                    if c == 0:
                        for q in range(QUARTERS):
                            j = r * QUARTERS + q
                            if j >= 2:
                                sp.wait_ge(m_ready, 2 * (j - 1))
                            rows = slice(q * CK * P, (q + 1) * CK * P)
                            sp.dma_start(mraw[j % 2][:, :, :], mix[rows, r * TT:(r + 1) * TT].rearrange("(k p) t -> p k t", p=P)).then_inc(m_loaded[j % 2], 16)
                    for ch in range(CH):
                        if n >= 2:
                            sp.wait_ge(low_ready, n - 1)
                        sp.dma_start(raw[n % 2][:, :, :], w_view[:, ch * CK:(ch + 1) * CK, c * NW:(c + 1) * NW]).then_inc(w_loaded[n % 2], 16)
                        n += 1
                    if i >= 2:
                        sp.wait_ge(added, THIRD_TILES * (i - 1))
                    cols = slice(c * NW, (c + 1) * NW)
                    if r < THIRDS - 1:
                        sp.dma_start(x[i % 2][:, :, :], xp[:, r * THIRD_TILES:(r + 1) * THIRD_TILES, cols]).then_inc(x_loaded[i % 2], 16)
                    else:
                        sp.dma_start(x[i % 2][:, 0:THIRD_TILES - 1, :], xp[:, r * THIRD_TILES:NT, cols]).then_inc(x_loaded[i % 2], 16)
                        sp.dma_start(x[i % 2][:, THIRD_TILES - 1, :], xs[:, cols]).then_inc(x_loaded[i % 2], 16)

            @block.gpsimd
            def _(pool):
                n = 0
                for i, (r, c) in enumerate(units):
                    if c == 0:
                        for q in range(QUARTERS):
                            j = r * QUARTERS + q
                            pool.wait_ge(m_ready, 2 * j + 1)
                            ks = slice(q * CK, (q + 1) * CK)
                            pool.tensor_tensor(mL[:, ks, :], mraw[j % 2][:, :, :], mH[:, ks, :].bitcast(F32), ALU.subtract).then_inc(m_ready, 1)
                    for ch in range(CH):
                        pool.wait_ge(high_ready, n + 1)
                        pool.tensor_tensor(wL[n % 2][:, :, :], raw[n % 2][:, :, :], wH[n % 2][:, :, :].bitcast(F32), ALU.subtract).then_inc(low_ready, 1)
                        n += 1

            @block.scalar
            def _(act):
                n = 0

                def finish(r):
                    for t in range(THIRD_TILES):
                        k = r * THIRD_TILES + t
                        act.wait_ge(stepped, 2 * (k + 1))
                        nc.scalar.activation(stat[:, t, 3:4], stat[:, t, 2:3], ACT.Sqrt).then_inc(rooted, 1)
                        act.wait_ge(weighted, k + 1)
                        dst = yp[:, k, :] if k < NT else ys
                        act.dma_start(dst, yv[:, t, :]).then_inc(stored, 16)
                    if r == THIRDS - 1:
                        act.wait_ge(stored, 16 * TILES)

                def high(n):
                    act.wait_ge(w_loaded[n % 2], 16 * (n // 2 + 1))
                    if n >= 2:
                        act.wait_ge(chunk_used, n - 1)
                    nc.scalar.activation(wH[n % 2][:, :, :], raw[n % 2][:, :, :], ACT.Copy).then_inc(high_ready, 1)

                for i, (r, c) in enumerate(units):
                    if c == 0:
                        if r:
                            act.wait_ge(chunk_used, CH * i)
                        for q in range(QUARTERS):
                            j = r * QUARTERS + q
                            act.wait_ge(m_loaded[j % 2], 16 * (j // 2 + 1))
                            if j:
                                act.wait_ge(m_ready, 2 * j)
                            ks = slice(q * CK, (q + 1) * CK)
                            nc.scalar.activation(mH[:, ks, :], mraw[j % 2][:, :, :], ACT.Copy).then_inc(m_ready, 1)
                    for ch in range(CH):
                        high(n)
                        n += 1
                    if c == CB - 1:
                        finish(r)

            @block.tensor
            def _(pe):
                n = 0
                for i, (r, c) in enumerate(units):
                    if c == 0:
                        pe.wait_ge(m_ready, 2 * QUARTERS * (r + 1))
                    for ch in range(CH):
                        pe.wait_ge(low_ready, n + 1)
                        for t in range(THIRD_TILES):
                            o = bank[i % 2 * THIRD_TILES + t][:, :]
                            if ch == 0 and i >= 2:
                                pe.wait_ge(added, THIRD_TILES * (i - 2) + t + 1)
                            for k in range(CK):
                                kk = ch * CK + k
                                a = slice(t * P, (t + 1) * P)
                                first, end = kk == 0, kk == KT - 1
                                pe.matmul(o, mL[:, kk, a], wH[n % 2][:, k, :], start=first, stop=False)
                                pe.matmul(o, mH[:, kk, a], wL[n % 2][:, k, :], start=False, stop=False)
                                last = pe.matmul(o, mH[:, kk, a], wH[n % 2][:, k, :], start=False, stop=end)
                        last.then_inc(chunk_used, 1)
                        n += 1

            @block.vector
            def _(dve):
                dve.wait_ge(fw_loaded, 16)
                V = nc.vector
                for i, (r, c) in enumerate(units):
                    dve.wait_ge(x_loaded[i % 2], 16 * (i // 2 + 1) if r < THIRDS - 1 else 16 * (CB * (THIRDS - 1) // 2 + 2 * (i // 2 - CB * (THIRDS - 1) // 2 + 1)))
                    if r and c == 0:
                        dve.wait_ge(stored, 16 * THIRD_TILES * r)
                    for t in range(THIRD_TILES):
                        dve.wait_ge(chunk_used, CH * (i + 1))
                        V.tensor_tensor(yv[:, t, c * NW:(c + 1) * NW], bank[i % 2 * THIRD_TILES + t][:, :], x[i % 2][:, t, :], ALU.add).then_inc(added, 1)
                    if c == CB - 1:
                        for t in range(THIRD_TILES):
                            k = r * THIRD_TILES + t
                            dve.wait_ge(added, THIRD_TILES * (i + 1))
                            V.tensor_tensor_reduce(out=squares[:, :], in0=yv[:, t, :], in1=yv[:, t, :], scale=1.0, scalar=0.0, op0=ALU.mult, op1=ALU.add, accum_out=stat[:, t, 0:1]).then_inc(squared, 1)
                            dve.wait_ge(squared, k + 1)
                            V.tensor_scalar(stat[:, t, 1:2], stat[:, t, 0:1], 1.0 / D, EPS, ALU.mult, ALU.add).then_inc(stepped, 1)
                            dve.wait_ge(stepped, 2 * k + 1)
                            V.reciprocal(stat[:, t, 2:3], stat[:, t, 1:2]).then_inc(stepped, 1)
                        for t in range(THIRD_TILES):
                            k = r * THIRD_TILES + t
                            dve.wait_ge(rooted, k + 1)
                            V.scalar_tensor_tensor(out=yv[:, t, :], in0=yv[:, t, :], scalar=stat[:, t, 3:4], in1=fw[:, :], op0=ALU.mult, op1=ALU.mult).then_inc(weighted, 1)


INPUTS = ["x_prompt", "x_sample", "cache_k", "cache_v", "cache_idx_k", "state_conv", "state_delta", "norm_w", "w_in",
          "conv_w", "a_log", "dt_bias", "gnorm_w", "w_out", "final_norm_w"]
OUTPUTS = [("y_prompt", (1, SEQ, D)), ("y_sample", (DEC_B, DEC_T, D)),
           ("new_k_prompt", (1, 1, SEQ, KV, HD)), ("new_v_prompt", (1, 1, SEQ, KV, HD)), ("new_idx_k_prompt", (1, 1, SEQ, ID)),
           ("new_conv_prompt", (1, 1, 3, 3 * H * HD)), ("new_delta_prompt", (1, 1, H, HD, HD)),
           ("new_k_sample", (1, DEC_B, DEC_T, KV, HD)), ("new_v_sample", (1, DEC_B, DEC_T, KV, HD)),
           ("new_idx_k_sample", (1, DEC_B, DEC_T, ID)), ("new_conv_sample", (1, DEC_B, 3, 3 * H * HD)),
           ("new_delta_sample", (1, DEC_B, H, HD, HD))]


def build(nc, io):
    scratch = {
        "proj": nc.dram_tensor("proj_scratch", (PROJ, TOK), F32, kind="Internal").ap(),
        "mask": nc.dram_tensor("mask_scratch", (NT, P, SEQ), BF16, kind="Internal").ap(),
        "sample_mask": nc.dram_tensor("sample_mask_scratch", (P, LS), BF16, kind="Internal").ap(),
        "mix": nc.dram_tensor("mix_scratch", (2 * H * P, TOK), F32, kind="Internal").ap(),
    }
    with ExitStack() as ctx:
        ident = ctx.enter_context(nc.sbuf_tensor("ident", [P, P], F32))
        with ExitStack() as inner:
            hH = inner.enter_context(nc.sbuf_tensor("hH", [P, KT, TOK], F32R))
            hL = inner.enter_context(nc.sbuf_tensor("hL", [P, KT, TOK], F32R))
            done_with = normalise_inputs(nc, io, hH, hL, ident)
            done_with = project_and_select(nc, io, scratch, hH, hL, ident, done_with)
        with ExitStack() as inner:
            keep = kept_tensors(nc, inner)
            prepare_heads(nc, io, scratch, keep, ident, done_with)
            run_heads(nc, io, scratch, keep, ident)
            attend_samples(nc, io, scratch, keep, ident)
        project_out(nc, io, scratch)


def kernel(**inputs):
    import numpy as np
    from concourse import bacc
    from concourse.bass_utils import run_bass_kernel_spmd

    nc = bacc.Bacc("TRN2", target_bir_lowering=False, num_devices=1)
    arrays, io = {}, {}
    for name in INPUTS:
        a = np.ascontiguousarray(inputs[name])
        arrays["in_" + name] = a
        io[name] = nc.dram_tensor("in_" + name, a.shape, mybir.dt.from_np(a.dtype), kind="ExternalInput").ap()
    for name, shape in OUTPUTS:
        io[name] = nc.dram_tensor("out_" + name, shape, F32, kind="ExternalOutput").ap()
    build(nc, io)
    result = run_bass_kernel_spmd(nc, [arrays], core_ids=[0])
    return tuple(result.results[0]["out_" + name] for name, _ in OUTPUTS)
```

```python
from contextlib import ExitStack

import concourse.bass as bass
from concourse import mybir

F32 = mybir.dt.float32
F32R = mybir.dt.float32r
BF16 = mybir.dt.bfloat16
ACT = mybir.ActivationFunctionType
ALU = mybir.AluOpType
AX_X = mybir.AxisListType.X

P = 128
D = 2048
KT = D // P
SEQ = 1024
DEC_B, DEC_T, PAST = 8, 16, 256
NT = SEQ // P
TILES = NT + 1
TOK = TILES * P
CHUNK = 64
EPS = 1e-6
H = 8
KV = 2
GROUP = H // KV
HD = 128
IH, ID = 16, 64
PROMPT_TOP = 256
LS = PAST + DEC_T
SAMPLE_TOP = LS // 4
CONV = 4
C_Q, C_K, C_V, C_Z = 0, 1024, 1280, 1536
C_QI, C_KI, C_WI, C_B, C_ZB, C_AB = 2560, 3584, 3648, 3664, 6736, 7760
PROJ = 7776
IDX_SCALE = (IH * ID) ** -0.5
SCALE = HD ** -0.5
OUT_MASK = -1e30
NOT_ALLOWED = -3.2e38
TAKEN = -3.4e38

FULL_BLOCKS = PROJ // P
LAST_COLS = PROJ - FULL_BLOCKS * P
NCH = 4
CK = KT // NCH
G3 = TOK // 3
FIRST = (C_QI // P, 30)
SEGMENTS = [(0, 7), (7, 14), (14, 20), (30, 37), (37, 44), (44, 51), (51, FULL_BLOCKS)]
INDEX_TILES = [7, 6, 5, 4, 3, 2]


def normalise_inputs(nc, io, hH, hL, ident):
    with ExitStack() as ctx:
        def sbt(name, shape, dt=F32):
            return ctx.enter_context(nc.sbuf_tensor(name, shape, dt))

        used = []

        def sem(name):
            used.append(ctx.enter_context(nc.semaphore(name)))
            return used[-1]

        SLOTS = 3
        x = [sbt(f"x{i}", [P, D]) for i in range(SLOTS)]
        squares = sbt("squares", [P, D])
        normw_rows = sbt("normw_rows", [KT, P])
        normw = sbt("normw", [P, KT])
        stat = sbt("stat", [P, SLOTS, 4])
        hf = [sbt(f"hf{i}", [P, 4, P]) for i in range(2)]
        turned = [ctx.enter_context(nc.psum_tensor(f"turned{i}", [P, 4, P], F32)) for i in range(4)]
        pw = ctx.enter_context(nc.psum_tensor("pw", [P, KT], F32))

        ident_ready, normw_loaded, normw_turned, normw_ready = map(
            sem, ["ident_ready", "normw_loaded", "normw_turned", "normw_ready"])
        x_loaded = [sem(f"x_loaded{i}") for i in range(SLOTS)]
        x_free, squared, meaned, rooted, scaled = map(sem, ["x_free", "squared", "meaned", "rooted", "scaled"])
        quad_turned, weighted, high_ready, low_ready = map(
            sem, ["quad_turned", "weighted", "high_ready", "low_ready"])
        xp = io["x_prompt"].rearrange("b (t p) d -> (b t) p d", p=P)
        xs = io["x_sample"].rearrange("b t d -> (b t) d")

        with nc.Block() as block:
            @block.sync
            def _(sp):
                sp.dma_start(normw_rows[:, :], io["norm_w"].rearrange("a (k p) -> (a k) p", p=P)).then_inc(normw_loaded, 16)
                for t in range(TILES):
                    if t >= SLOTS:
                        sp.wait_ge(quad_turned, 4 * (t - SLOTS + 1))
                    sp.dma_start(x[t % SLOTS][:, :], xp[t] if t < NT else xs).then_inc(x_loaded[t % SLOTS], 16)

            @block.gpsimd
            def _(pool):
                pool.memset(ident[:, :], 0.0).then_inc(ident_ready, 1)
                pool.wait_ge(ident_ready, 1)
                pool.affine_select(out=ident[:, :], in_=ident[:, :], compare_op=ALU.not_equal, fill=1.0,
                                   base=0, pattern=[[-1, P]], channel_multiplier=1).then_inc(ident_ready, 1)
                for q in range(4 * TILES):
                    t, j = divmod(q, 4)
                    pool.wait_ge(high_ready, q + 1)
                    cols = slice(t * P, (t + 1) * P)
                    pool.tensor_tensor(hL[:, 4 * j:4 * j + 4, cols], hf[q % 2][:, :, :],
                                       hH[:, 4 * j:4 * j + 4, cols].bitcast(F32), ALU.subtract).then_inc(low_ready, 1)

            @block.scalar
            def _(act):
                for t in range(TILES):
                    s = t % SLOTS
                    act.wait_ge(x_loaded[s], 16 * (t // SLOTS + 1))
                    if t:
                        act.wait_ge(squared, t)
                    nc.scalar.activation(squares[:, :], x[s][:, :], ACT.Square,
                                         accum_out=stat[:, s, 0:1]).then_inc(squared, 1)
                    act.wait_ge(meaned, 2 * (t + 1))
                    nc.scalar.activation(stat[:, s, 3:4], stat[:, s, 2:3], ACT.Sqrt).then_inc(rooted, 1)
                    act.wait_ge(rooted, t + 1)
                    nc.scalar.activation(x[s][:, :], x[s][:, :], ACT.Copy, scale=stat[:, s, 3:4]).then_inc(scaled, 1)

            @block.tensor
            def _(pe):
                pe.wait_ge(ident_ready, 2)
                pe.wait_ge(normw_loaded, 16)
                pe.transpose(pw[:, :], normw_rows[:, :], ident[0:KT, 0:KT]).then_inc(normw_turned, 1)
                for q in range(4 * TILES):
                    t, j = divmod(q, 4)
                    pe.wait_ge(scaled, t + 1)
                    if q >= 4:
                        pe.wait_ge(weighted, q - 3)
                    for k in range(4):
                        kk = 4 * j + k
                        last = pe.transpose(turned[q % 4][:, k, :], x[t % SLOTS][:, kk * P:(kk + 1) * P], ident[:, :])
                    last.then_inc(quad_turned, 1)

            @block.vector
            def _(dve):
                dve.wait_ge(normw_turned, 1)
                nc.vector.tensor_copy(normw[:, :], pw[:, :]).then_inc(normw_ready, 1)
                dve.wait_ge(normw_ready, 1)

                def statistics(t):
                    s = t % SLOTS
                    dve.wait_ge(squared, t + 1)
                    nc.vector.tensor_scalar(stat[:, s, 1:2], stat[:, s, 0:1], 1.0 / D, EPS, ALU.mult, ALU.add).then_inc(meaned, 1)
                    dve.wait_ge(meaned, 2 * t + 1)
                    nc.vector.reciprocal(stat[:, s, 2:3], stat[:, s, 1:2]).then_inc(meaned, 1)

                statistics(0)
                for q in range(4 * TILES):
                    t, j = divmod(q, 4)
                    if j == 0 and t + 1 < TILES:
                        statistics(t + 1)
                    dve.wait_ge(quad_turned, q + 1)
                    if q >= 2:
                        dve.wait_ge(low_ready, q - 1)
                    nc.vector.tensor_tensor(hf[q % 2][:, :, :], turned[q % 4][:, :, :],
                                            normw[:, 4 * j:4 * j + 4].unsqueeze(2).to_broadcast([P, 4, P]),
                                            ALU.mult).then_inc(weighted, 1)
                    dve.wait_ge(weighted, q + 1)
                    nc.vector.tensor_copy(hH[:, 4 * j:4 * j + 4, t * P:(t + 1) * P], hf[q % 2][:, :, :]).then_inc(high_ready, 1)
                dve.wait_ge(low_ready, 4 * TILES)
        return used


def project_and_select(nc, io, scratch, hH, hL, ident, done_with):
    with ExitStack() as ctx:
        def sbt(name, shape, dt=F32):
            return ctx.enter_context(nc.sbuf_tensor(name, shape, dt))

        used = []

        def sem(name):
            used.append(ctx.enter_context(nc.semaphore(name)))
            return used[-1]

        proj, masks, smask = scratch["proj"], scratch["mask"], scratch["sample_mask"]
        raw = [sbt(f"raw{c}", [P, CK, P]) for c in range(NCH)]
        wH = [sbt(f"wH{i}", [P, CK, P], F32R) for i in range(2)]
        wL = [sbt(f"wL{i}", [P, CK, P], F32R) for i in range(2)]
        ptbuf = sbt("ptbuf", [P, TOK])
        score = sbt("score", [P, SEQ])
        relued = [sbt(f"relued{i}", [P, 512]) for i in range(2)]
        top8 = sbt("top8", [P, 8])
        mask = sbt("mask", [P, SEQ], BF16)
        kiN = sbt("kiN", [P, TILES, 80])
        w_idx = sbt("w_idx", [P, TILES, IH])
        diag = sbt("diag", [P, 2 * P - DEC_T])
        spread = sbt("spread", [IH, IH, DEC_T])
        wbc = sbt("wbc", [P, 2, P])
        pick = [sbt(f"pick{i}", [P, P]) for i in range(2)]
        wT = sbt("wT", [IH, P])
        region = sbt("region", [P, 5248])
        qs = region[0:ID, 0:2048].rearrange("d (b h t) -> d b h t", b=DEC_B, h=IH)
        kcT = region[0:ID, 2048:2048 + DEC_B * LS].rearrange("d (b s) -> d b s", b=DEC_B)
        kc_nat = region[:, 4224:5248].rearrange("p (n d) -> p n d", d=ID)
        qi = [region[:, i * 1024:(i + 1) * 1024].rearrange("p (j t) -> p j t", j=H) for i in range(2)]
        kiT = region[:, 2048:2048 + SEQ]
        kiw = ptbuf[0:80, :]

        bank = [ctx.enter_context(nc.psum_tensor(f"bank{i}", [P, 512], F32)) for i in range(8)]
        BANKS_REL = 4
        rel = bank[3:7]

        w_loaded = [sem(f"w_loaded{c}") for c in range(NCH)]
        high_ready = sem("high_ready")
        low_ready = sem("low_ready")
        products = sem("products")
        evacuated, pt_stored = map(sem, ["evacuated", "pt_stored"])
        idx_loaded, q_loaded, tables = map(sem, ["idx_loaded", "q_loaded", "tables"])
        turned, turned_out, new_k_stored = map(sem, ["turned", "turned_out", "new_k_stored"])
        rel_done, relu_done, acc_done, picked, summed = map(
            sem, ["rel_done", "relu_done", "acc_done", "picked", "summed"])
        dve_step, mask_ready, mask_stored, kiw_loaded = map(sem, ["dve_step", "mask_ready", "mask_stored", "kiw_loaded"])

        w_view = io["w_in"].rearrange("a (k p) n -> (a p) k n", p=P)
        segs = [FIRST] + SEGMENTS
        base, n = [], 0
        for lo, hi in segs:
            base.append(n)
            n += hi - lo
        assert n == FULL_BLOCKS
        RELS = {t: [(hd, c) for hd in range(IH) for c in range(0, (t + 1) * P, 512)] for t in INDEX_TILES}
        rel_base, n = {}, 2 * DEC_B
        for t in INDEX_TILES:
            rel_base[t] = n
            n += len(RELS[t])
        CREDIT = 1
        STEPS = 6

        with nc.Block() as block:
            @block.sync
            def _(sp):
                def load_block(s, cols):
                    for c in range(NCH):
                        sp.wait_ge(low_ready, s * NCH + c + 1)
                        width = LAST_COLS if cols is None else P
                        src = (w_view[:, c * CK:(c + 1) * CK, FULL_BLOCKS * P:PROJ] if cols is None
                               else w_view[:, c * CK:(c + 1) * CK, bass.ds(cols, P)])
                        sp.dma_start(raw[c][:, :, 0:width], src).then_inc(w_loaded[c], 16)

                lo, hi = segs[0]
                with sp.Fori(lo, hi) as b:
                    load_block(b - lo, b * P)
                for i, t in enumerate([None] + INDEX_TILES):
                    lo, hi = segs[i + 1]
                    load_block(base[i + 1], lo * P)
                    sp.wait_ge(pt_stored, 16 * (base[1] + CREDIT))
                    if t is None:
                        sp.dma_start(kiw, proj[C_KI:C_KI + 80, :]).then_inc(kiw_loaded, 16)
                        sp.dma_start(wT[:, :], proj[C_WI:C_WI + IH, SEQ:TOK]).then_inc(idx_loaded, 16)
                        for b in range(DEC_B):
                            at = SEQ + b * DEC_T
                            sp.dma_start(qs[:, b, :, :], proj[C_QI:C_KI, at:at + DEC_T].rearrange("(h d) t -> d h t", d=ID)).then_inc(idx_loaded, 16)
                        sp.dma_start(kc_nat, io["cache_idx_k"].rearrange("a b (n p) d -> p (a b n) d", p=P)).then_inc(idx_loaded, 16)
                        sp.dma_start(kcT[:, :, PAST:LS], proj[C_KI:C_WI, SEQ:TOK].rearrange("d (b t) -> d b t", b=DEC_B)).then_inc(idx_loaded, 16)
                        sp.wait_ge(turned_out, 2)
                        sp.dma_start(io["new_idx_k_prompt"].rearrange("a b (t p) d -> p (a b t) d", p=P), kiN[:, 0:NT, 0:ID]).then_inc(new_k_stored, 16)
                        sp.dma_start(io["new_idx_k_sample"].rearrange("a b t d -> (a b t) d"), kiN[:, NT, 0:ID]).then_inc(new_k_stored, 16)
                    else:
                        if t == INDEX_TILES[0]:
                            sp.wait_ge(rel_done, 2 * DEC_B)
                            for half in range(2):
                                sp.dma_start(kiT[half * ID:(half + 1) * ID, :], proj[C_KI:C_WI, 0:SEQ]).then_inc(idx_loaded, 16)
                        else:
                            n = rel_base[INDEX_TILES[i - 2]] + len(RELS[INDEX_TILES[i - 2]])
                            sp.wait_ge(rel_done, n)
                        sp.dma_start(qi[i % 2], proj[C_QI:C_KI, t * P:(t + 1) * P].rearrange("(j p) t -> p j t", p=P)).then_inc(q_loaded, 16)
                    if hi - lo > 1:
                        with sp.Fori(lo + 1, hi) as b:
                            load_block(b - lo + base[i + 1], b * P)
                    sp.wait_ge(mask_ready, i + 1)
                    if t is None:
                        sp.dma_start(smask, mask[:, 0:LS]).then_inc(mask_stored, 16)
                    else:
                        sp.dma_start(masks[t, :, 0:(t + 1) * P], mask[:, 0:(t + 1) * P]).then_inc(mask_stored, 16)
                load_block(FULL_BLOCKS, None)
                sp.wait_ge(pt_stored, 16 * (FULL_BLOCKS + 1 + CREDIT))
                sp.wait_ge(mask_stored, 16 * len(segs[1:]))
                sp.wait_ge(new_k_stored, 32)

            @block.gpsimd
            def _(pool):
                for old in done_with:
                    pool.sem_clear(old)
                pool.sem_inc(low_ready, CREDIT * NCH)
                pool.memset(diag[:, :], 0.0).then_inc(tables, 1)
                pool.memset(spread[:, :, :], 1.0).then_inc(tables, 1)
                pool.wait_ge(tables, 2)
                for hd in range(H):
                    ones = diag[:, P - DEC_T:P]
                    pool.affine_select(out=ones, in_=ones, compare_op=ALU.not_equal, fill=1.0, base=DEC_T * hd,
                                       pattern=[[1, DEC_T]], channel_multiplier=-1).then_inc(tables, 1)
                    pool.wait_ge(tables, 3 + hd)
                pool.affine_select(out=spread[:, :, :], in_=spread[:, :, :], compare_op=ALU.is_equal, fill=0.0,
                                   base=0, pattern=[[-1, IH], [0, DEC_T]], channel_multiplier=1).then_inc(tables, 1)

                def low_parts(s):
                    for c in range(NCH):
                        pool.wait_ge(high_ready, s * NCH + c + 1)
                        pool.tensor_tensor(wL[c % 2][:, :, :], raw[c][:, :, :], wH[c % 2][:, :, :].bitcast(F32),
                                           ALU.subtract).then_inc(low_ready, 1)

                for (lo, hi), b0 in zip(segs, base):
                    with pool.Fori(lo, hi) as b:
                        low_parts(b - lo + b0)
                low_parts(FULL_BLOCKS)

            @block.scalar
            def _(act):
                act.sem_inc(pt_stored, 16 * CREDIT)
                act.sem_inc(evacuated, 3 * CREDIT)

                def high_part(s, c):
                    act.wait_ge(w_loaded[c], s * 16 + 16)
                    act.wait_ge(products, s * STEPS + (3, 6, 7, 8)[c])
                    nc.scalar.activation(wH[c % 2][:, :, :], raw[c][:, :, :], ACT.Copy).then_inc(high_ready, 1)

                def block_steps(s, rows, cols, more=True):
                    high_part(s, 2)
                    high_part(s, 3)
                    if more:
                        high_part(s + 1, 0)
                    act.wait_ge(pt_stored, s * 16 + 16 * CREDIT)
                    for g in range(3):
                        act.wait_ge(products, s * STEPS + 4 + g + STEPS * CREDIT)
                        nc.scalar.activation(ptbuf[0:rows, g * G3:(g + 1) * G3], bank[g][0:rows, 0:G3], ACT.Copy).then_inc(evacuated, 1)
                    act.wait_ge(evacuated, s * 3 + 3 + 3 * CREDIT)
                    act.dma_start(proj[cols, :], ptbuf[0:rows, :]).then_inc(pt_stored, 16)
                    if more:
                        high_part(s + 1, 1)

                def index_units(first, widths):
                    for u, width in enumerate(widths, first):
                        act.wait_ge(rel_done, u + 1)
                        if 2 <= u < 2 * DEC_B + 2:
                            act.wait_ge(summed, min(u - 1, 2 * DEC_B))
                        if u >= 2 * DEC_B + 2:
                            act.wait_ge(acc_done, u - 2 * DEC_B - 1)
                        nc.scalar.activation(relued[u % 2][:, 0:width], rel[u % BANKS_REL][:, 0:width], ACT.Relu).then_inc(relu_done, 1)

                high_part(0, 0)
                high_part(0, 1)
                for i, ((lo, hi), b0) in enumerate(zip(segs, base)):
                    if i == 1:
                        for half in range(2):
                            act.wait_ge(turned, half + 1)
                            n0, n1 = (0, 5) if half == 0 else (5, 9)
                            nc.scalar.activation(kiN[:, n0:n1, :], bank[3 + half][:, 0:(n1 - n0) * 80].rearrange("p (t c) -> p t c", c=80), ACT.Copy).then_inc(turned_out, 1)
                        for n in range(4):
                            act.wait_ge(turned, 3 + n)
                            nc.scalar.activation(kcT[:, 2 * n:2 * n + 2, 0:PAST], bank[(5, 6, 3, 4)[n]][0:ID, 0:512].rearrange("d (b s) -> d b s", b=2), ACT.Copy).then_inc(turned_out, 1)
                        act.wait_ge(turned, 7)
                        nc.scalar.activation(wbc[:, :, :], bank[7][:, 0:256].rearrange("p (a t) -> p a t", a=2), ACT.Copy, scale=IDX_SCALE).then_inc(turned_out, 1)
                        index_units(0, [LS] * (2 * DEC_B))
                    elif i > 1:
                        t = INDEX_TILES[i - 2]
                        index_units(rel_base[t], [min(512, (t + 1) * P - c) for _, c in RELS[t]])
                    with act.Fori(lo, hi) as b:
                        block_steps(b - lo + b0, P, bass.ds(b * P, P))
                block_steps(FULL_BLOCKS, LAST_COLS, slice(FULL_BLOCKS * P, PROJ), more=False)

            @block.tensor
            def _(pe):
                pe.sem_inc(products, STEPS * CREDIT)

                def block_products(s, cols):
                    for c in range(NCH):
                        pe.wait_ge(low_ready, s * NCH + c + 1 + NCH * CREDIT)
                        for g in range(3):
                            if c == 0:
                                pe.wait_ge(evacuated, s * 3 + g + 1)
                            for k in range(CK):
                                kk = c * CK + k
                                tok = slice(g * G3, (g + 1) * G3)
                                first, end = c == 0 and k == 0, c == NCH - 1 and k == CK - 1
                                o = bank[g][0:cols, 0:G3]
                                high, low = wH[c % 2][:, k, 0:cols], wL[c % 2][:, k, 0:cols]
                                pe.matmul(o, low, hH[:, kk, tok], start=first, stop=False)
                                pe.matmul(o, high, hL[:, kk, tok], start=False, stop=False)
                                last = pe.matmul(o, high, hH[:, kk, tok], start=False, stop=end)
                            if c == NCH - 1:
                                last.then_inc(products, 1)
                        if c < NCH - 1:
                            last.then_inc(products, 1)

                def sample_index():
                    pe.wait_ge(kiw_loaded, 16)
                    for t in range(TILES):
                        o = bank[3 + t // 5][:, (t % 5) * 80:(t % 5 + 1) * 80]
                        last = pe.transpose(o, kiw[:, t * P:(t + 1) * P], ident[0:80, 0:80])
                        if t in (4, 8):
                            last.then_inc(turned, 1)
                    pe.wait_ge(idx_loaded, 16 * (3 + DEC_B))
                    for n in range(4):
                        if n == 2:
                            pe.wait_ge(turned_out, 2)
                        for m in range(4):
                            last = pe.transpose(bank[(5, 6, 3, 4)[n]][0:ID, m * P:(m + 1) * P], kc_nat[:, 4 * n + m, :], ident[:, :])
                        last.then_inc(turned, 1)
                    pe.wait_ge(tables, 3 + H)
                    for half in range(2):
                        last = pe.matmul(bank[7][:, half * P:(half + 1) * P], spread[:, half * H:(half + 1) * H, :], wT[:, :], start=True, stop=True)
                    last.then_inc(turned, 1)
                    pe.wait_ge(turned_out, 7)

                    def relate(u):
                        b, half = divmod(u, 2)
                        if u >= BANKS_REL:
                            pe.wait_ge(relu_done, u - BANKS_REL + 1)
                        pe.matmul(rel[u % BANKS_REL][:, 0:LS], qs[:, b, half * H:(half + 1) * H, :],
                                  kcT[:, b, :], start=True, stop=True).then_inc(rel_done, 1)

                    relate(0)
                    for u in range(2 * DEC_B):
                        if u + 1 < 2 * DEC_B:
                            relate(u + 1)
                        pe.wait_ge(relu_done, u + 1)
                        pe.wait_ge(picked, u + 1)
                        pe.matmul(bank[7][:, 0:LS], pick[u % 2][:, :], relued[u % 2][:, 0:LS],
                                  start=(u == 0), stop=(u == 2 * DEC_B - 1)).then_inc(summed, 1)

                def prompt_index(i, t):
                    pe.wait_ge(idx_loaded, 16 * (5 + DEC_B))
                    pe.wait_ge(q_loaded, 16 * i)
                    for u, (hd, c) in enumerate(RELS[t], rel_base[t]):
                        pe.wait_ge(relu_done, u - BANKS_REL + 1)
                        width = min(512, (t + 1) * P - c)
                        rows = slice(hd % 2 * ID, hd % 2 * ID + ID)
                        pe.matmul(rel[u % BANKS_REL][:, 0:width], qi[i % 2][rows, hd // 2, :], kiT[rows, c:c + width],
                                  start=True, stop=True).then_inc(rel_done, 1)

                for i, ((lo, hi), b0) in enumerate(zip(segs, base)):
                    if i == 1:
                        sample_index()
                    elif i > 1:
                        prompt_index(i - 1, INDEX_TILES[i - 2])
                    with pe.Fori(lo, hi) as b:
                        block_products(b - lo + b0, P)
                block_products(FULL_BLOCKS, LAST_COLS)

            @block.vector
            def _(dve):
                steps = [0]

                def chain(instruction):
                    steps[0] += 1
                    instruction.then_inc(dve_step, 1)
                    dve.wait_ge(dve_step, steps[0])

                def select(i, width, top):
                    sc = score[:, 0:width]
                    for r in range(top // 8):
                        chain(nc.vector.max(top8[:, :], sc))
                        chain(nc.vector.match_replace(out=sc, in_to_replace=top8[:, :], in_values=sc, imm_value=TAKEN))
                    if top % 8:
                        chain(nc.vector.max(top8[:, :], sc))
                        chain(nc.vector.memset(top8[:, top % 8:8], TAKEN))
                        chain(nc.vector.match_replace(out=sc, in_to_replace=top8[:, :], in_values=sc, imm_value=TAKEN))
                    if i:
                        dve.wait_ge(mask_stored, 16 * i)
                    nc.vector.tensor_scalar(mask[:, 0:width], sc, TAKEN, OUT_MASK, ALU.not_equal, ALU.mult).then_inc(mask_ready, 1)

                dve.wait_ge(turned_out, 2)
                chain(nc.vector.tensor_scalar(w_idx[:, :, :], kiN[:, :, ID:80], IDX_SCALE, None, ALU.mult))
                dve.wait_ge(turned_out, 7)
                dve.wait_ge(tables, 3 + H)
                for u in range(2 * DEC_B):
                    b, half = divmod(u, 2)
                    if u >= 2:
                        dve.wait_ge(summed, u - 1)
                    at = P - DEC_T - DEC_T * b
                    nc.vector.tensor_tensor(pick[u % 2][:, :], wbc[:, half, :], diag[:, at:at + P], ALU.mult).then_inc(picked, 1)
                dve.wait_ge(summed, 2 * DEC_B)
                chain(nc.vector.tensor_copy(score[:, 0:LS], bank[7][:, 0:LS]))
                select(0, LS, SAMPLE_TOP)
                for i, t in enumerate(INDEX_TILES, 1):
                    dve.wait_ge(mask_ready, i)
                    for u, (hd, c) in enumerate(RELS[t], rel_base[t] - 2 * DEC_B):
                        width = min(512, (t + 1) * P - c)
                        sc, r = score[:, c:c + width], relued[u % 2][:, 0:width]
                        dve.wait_ge(relu_done, u + 1 + 2 * DEC_B)
                        if u > rel_base[t] - 2 * DEC_B:
                            dve.wait_ge(acc_done, u)
                        w = w_idx[:, t, hd:hd + 1]
                        if hd == 0:
                            nc.vector.tensor_scalar(sc, r, w, None, ALU.mult).then_inc(acc_done, 1)
                        else:
                            nc.vector.scalar_tensor_tensor(out=sc, in0=r, scalar=w, in1=sc, op0=ALU.mult, op1=ALU.add).then_inc(acc_done, 1)
                    dve.wait_ge(acc_done, u + 1)
                    chain(nc.vector.memset(score[0:CHUNK, t * P + CHUNK:(t + 1) * P], NOT_ALLOWED))
                    select(i, (t + 1) * P, PROMPT_TOP)
        return used


class Signal:

    def __init__(self, sem, per):
        self.sem, self.per = sem, per

    def now(self, h, k):
        return h * self.per + (self.per + k)

    def before(self, h, k):
        return h * self.per + k


LEVELS = 7
SAMPLE_LEVELS = 4
GATES = 6
G_LOG, G_CUM, G_BETA, G_BETA_EXP, G_EXP, G_REST = range(GATES)


def prepare_heads(nc, io, scratch, keep, ident, done_with):
    with ExitStack() as ctx:
        def sbt(name, shape, dt=F32):
            return ctx.enter_context(nc.sbuf_tensor(name, shape, dt))

        def sem(name):
            return ctx.enter_context(nc.semaphore(name))

        proj = scratch["proj"]
        kvT = sbt("kvT", [P, 4, TOK])
        kvN = sbt("kvN", [P, TILES, 4, P])
        abT = sbt("abT", [16, TOK])
        ab = sbt("ab", [P, TILES, 16])
        dtb, alog, aexp = sbt("dtb", [P, H]), sbt("alog", [P, H]), sbt("aexp", [P, H])
        wk = [sbt(f"wk{i}", [P, TILES, H]) for i in range(6)]
        gnat = sbt("gnat", [P, TILES, H])
        ones = sbt("ones", [P, P])
        same16 = sbt("same16", [P, P])
        dist = sbt("dist", [P, SEQ], mybir.dt.int32)
        loaded, tabled, built, stepped, acted, turned, moved, stored = map(
            sem, ["loaded", "tabled", "built", "stepped", "acted", "turned", "moved", "stored"])
        gate_loaded, kv_loaded, summed, drained = map(sem, ["gate_loaded", "kv_loaded", "summed", "drained"])
        bank = [ctx.enter_context(nc.psum_tensor(f"pb{i}", [P, 4, P], F32)) for i in range(4)]
        abp = ctx.enter_context(nc.psum_tensor("abp", [P, TILES, 16], F32))
        gcp = ctx.enter_context(nc.psum_tensor("gcp", [P, 2, TILES, H], F32))
        G, K = keep["gates"], keep
        cumP, cumS, segcol, segs16 = K["cum"][:, 0, :], K["cum"][:, 1, :], K["segcol"], same16

        with nc.Block() as block:
            @block.sync
            def _(sp):
                sp.dma_start(abT[:, :], proj[C_AB:PROJ, :]).then_inc(gate_loaded, 16)
                sp.dma_start(dtb[:, :], io["dt_bias"].to_broadcast([P, H])).then_inc(gate_loaded, 16)
                sp.dma_start(alog[:, :], io["a_log"].to_broadcast([P, H])).then_inc(gate_loaded, 16)
                sp.dma_start(kvT[:, :, :], proj[C_K:C_Z, :].rearrange("(n p) t -> p n t", p=P)).then_inc(kv_loaded, 16)
                sp.dma_start(K["kT"][:, :, :], proj[C_K:C_V, 0:SEQ].rearrange("(n p) t -> p n t", p=P)).then_inc(loaded, 16)
                at = 0
                for t in range(NT):
                    w = (t + 1) * P
                    if t >= 2:
                        sp.dma_start(K["mask"][:, at:at + w], scratch["mask"][t, :, 0:w]).then_inc(loaded, 16)
                    at += w
                sp.dma_start(K["gnw"][:, :], io["gnorm_w"].rearrange("a d -> d a")).then_inc(loaded, 16)
                sp.wait_ge(moved, TILES)
                flat = kvN[:, :, :, :].rearrange("p t n d -> p t (n d)")
                for name, c in (("new_k", 0), ("new_v", 2 * P)):
                    sp.dma_start(io[name + "_prompt"].rearrange("a b (t p) k d -> p (a b t) (k d)", p=P), flat[:, 0:NT, c:c + 2 * P]).then_inc(stored, 16)
                    sp.dma_start(io[name + "_sample"].rearrange("a b t k d -> (a b t) (k d)"), flat[:, NT, c:c + 2 * P]).then_inc(stored, 16)
                sp.wait_ge(stored, 64)
                sp.wait_ge(loaded, 16 * 8)

            @block.gpsimd
            def _(pool):
                for old in done_with:
                    pool.sem_clear(old)
                n = [0]

                def chain(instruction):
                    n[0] += 1
                    instruction.then_inc(tabled, 1)
                    pool.wait_ge(tabled, n[0])

                def keep_where(ap, op, base, pattern, mult, fill=0.0):
                    chain(pool.affine_select(out=ap, in_=ap, compare_op=op, fill=fill, base=base, pattern=pattern, channel_multiplier=mult))

                pool.memset(ones[:, :], 1.0).then_inc(tabled, 1)
                n[0] += 1
                chain(pool.memset(segcol[:, :], 1.0))
                keep_where(segcol[:, :], ALU.is_ge, 0, [[-DEC_T, DEC_B]], 1)
                keep_where(segcol[:, :], ALU.is_ge, DEC_T - 1, [[DEC_T, DEC_B]], -1)
                chain(pool.tensor_copy(same16[:, :].rearrange("p (b t) -> p b t", b=DEC_B), segcol[:, :].unsqueeze(2).to_broadcast([P, DEC_B, DEC_T])))
                for name, base, step, mult in (("cum", 0, 1, -1), ("dmN", 0, -1, 1)):
                    chain(pool.memset(K[name][:, 0, :], 1.0))
                    keep_where(K[name][:, 0, :], ALU.is_ge, base, [[step, P]], mult)
                    chain(pool.tensor_tensor(K[name][:, 1, :], K[name][:, 0, :], same16[:, :], ALU.mult))
                chain(pool.tensor_scalar(K["dmT"][:, :, :], K["cum"][:, :, :], 1.0, -OUT_MASK, ALU.subtract, ALU.mult))
                chain(pool.tensor_scalar(K["dmN"][:, :, :], K["dmN"][:, :, :], 1.0, -OUT_MASK, ALU.subtract, ALU.mult))
                chain(pool.memset(K["level"][:, :, :], 0.0))
                for m in range(LEVELS):
                    b = 2 ** m
                    first = K["level"][:, m, :].rearrange("p (n e r) -> p n e r", e=2, r=b)[:, :, 0, :]
                    chain(pool.memset(first, 1.0))
                    keep_where(first, ALU.is_ge, -b, [[-2 * b, P // (2 * b)], [0, b]], 1)
                    keep_where(first, ALU.is_ge, 2 * b - 1, [[2 * b, P // (2 * b)], [0, b]], -1)
                chain(pool.tensor_copy(K["identb"][:, :], ident[:, :]))
                chain(pool.iota(dist[:, :], pattern=[[-1, SEQ]], base=SEQ - P, channel_multiplier=1))
                chain(pool.memset(K["mask"][:, 0:3 * P], 0.0))
                for at in (0, 2 * P):
                    chain(pool.memset(K["mask"][0:CHUNK, at + CHUNK:at + P], OUT_MASK))
                pool.sem_inc(built, 1)

            @block.tensor
            def _(pe):
                pe.wait_ge(gate_loaded, 48)
                for t in range(TILES):
                    last = pe.transpose(abp[:, t, :], abT[:, t * P:(t + 1) * P], ident[0:16, 0:16])
                last.then_inc(turned, 1)
                pe.wait_ge(kv_loaded, 16)
                for t in range(TILES):
                    if t >= 4:
                        pe.wait_ge(moved, t - 3)
                    for n in range(4):
                        last = pe.transpose(bank[t % 4][:, n, :], kvT[:, n, t * P:(t + 1) * P], ident[:, :])
                    last.then_inc(turned, 1)
                pe.wait_ge(stepped, 9)
                pe.wait_ge(built, 1)
                pe.matmul(gcp[:, 0, 0:NT, :], cumP, gnat[:, 0:NT, :], start=True, stop=True)
                pe.matmul(gcp[:, 0, NT, :], cumS, gnat[:, NT, :], start=True, stop=True)
                pe.matmul(gcp[:, 1, 0:NT, :], ones[:, :], gnat[:, 0:NT, :], start=True, stop=True)
                pe.matmul(gcp[:, 1, NT, :], same16[:, :], gnat[:, NT, :], start=True, stop=True).then_inc(summed, 1)

            @block.scalar
            def _(act):
                act.wait_ge(stepped, 3)
                nc.scalar.activation(wk[2][:, :, :], wk[1][:, :, :], ACT.Exp, scale=-1.0).then_inc(acted, 1)
                nc.scalar.activation(aexp[:, :], alog[:, :], ACT.Exp).then_inc(acted, 1)
                nc.scalar.activation(wk[4][:, :, :], ab[:, :, H:16], ACT.Exp, scale=-1.0).then_inc(acted, 1)
                act.wait_ge(acted, 1)
                nc.scalar.activation(wk[3][:, :, :], wk[2][:, :, :], ACT.Ln, bias=1.0).then_inc(acted, 1)
                for t in range(TILES):
                    act.wait_ge(turned, t + 2)
                    nc.scalar.activation(kvN[:, t, :, :], bank[t % 4][:, :, :], ACT.Copy).then_inc(moved, 1)
                act.wait_ge(stepped, 11)
                nc.scalar.activation(G[:, :, G_EXP, :].rearrange("p h t -> p t h"), wk[0][:, :, :], ACT.Exp).then_inc(acted, 1)
                nc.scalar.activation(G[:, :, G_REST, :].rearrange("p h t -> p t h"), wk[1][:, :, :], ACT.Exp).then_inc(acted, 1)
                act.wait_ge(moved, TILES)
                for t in range(NT):
                    last = nc.scalar.activation(K["vN"][:, t, :, :], kvN[:, t, 2:4, :], ACT.Copy)
                    last.then_inc(drained, 1)

            @block.vector
            def _(dve):
                n = [0]

                def chain(instruction):
                    n[0] += 1
                    instruction.then_inc(stepped, 1)
                    dve.wait_ge(stepped, n[0])

                gv = lambda k: G[:, :, k, :].rearrange("p h t -> p t h")
                dve.wait_ge(turned, 1)
                dve.wait_ge(gate_loaded, 48)
                chain(nc.vector.tensor_copy(ab[:, :, :], abp[:, :, :]))
                chain(nc.vector.tensor_tensor(wk[0][:, :, :], ab[:, :, 0:H], dtb[:, :].unsqueeze(1).to_broadcast([P, TILES, H]), ALU.add))
                chain(nc.vector.scalar_tensor_tensor(out=wk[1][:, :, :], in0=wk[0][:, :, :], scalar=-1.0, in1=wk[0][:, :, :], op0=ALU.mult, op1=ALU.max))
                dve.wait_ge(acted, 4)
                chain(nc.vector.scalar_tensor_tensor(out=wk[5][:, :, :], in0=wk[0][:, :, :], scalar=0.0, in1=wk[3][:, :, :], op0=ALU.max, op1=ALU.add))
                chain(nc.vector.tensor_tensor(wk[5][:, :, :], wk[5][:, :, :], aexp[:, :].unsqueeze(1).to_broadcast([P, TILES, H]), ALU.mult))
                chain(nc.vector.tensor_scalar(gnat[:, :, :], wk[5][:, :, :], -1.0, None, ALU.mult))
                chain(nc.vector.tensor_copy(gv(G_LOG), gnat[:, :, :]))
                chain(nc.vector.tensor_scalar(wk[4][:, :, :], wk[4][:, :, :], 1.0, None, ALU.add))
                chain(nc.vector.reciprocal(gv(G_BETA), wk[4][:, :, :]))
                dve.wait_ge(summed, 1)
                chain(nc.vector.tensor_copy(wk[0][:, :, :], gcp[:, 0, :, :]))
                chain(nc.vector.tensor_tensor(wk[1][:, :, :], gcp[:, 1, :, :], wk[0][:, :, :], ALU.subtract))
                chain(nc.vector.tensor_copy(gv(G_CUM), wk[0][:, :, :]))
                dve.wait_ge(acted, 5)
                chain(nc.vector.tensor_tensor(gv(G_BETA_EXP), gv(G_BETA), gv(G_EXP), ALU.mult))
                dve.wait_ge(built, 1)
                chain(nc.vector.tensor_copy(K["alibi"][:, :], dist[:, :]))
                chain(nc.vector.scalar_tensor_tensor(out=K["alibi"][:, :], in0=K["alibi"][:, :], scalar=-1.0, in1=K["alibi"][:, :], op0=ALU.mult, op1=ALU.min))
                chain(nc.vector.tensor_scalar(K["alibi"][:, :], K["alibi"][:, :], 2.0 ** (-8.0 / H) / SCALE, None, ALU.mult))
                dve.wait_ge(drained, NT)
                dve.wait_ge(acted, 6)


def weave(main, between):
    out, done = [], 0
    for i, step in enumerate(main):
        upto = (i + 1) * len(between) // len(main)
        out += [step] + between[done:upto]
        done = upto
    return out


def head_order(first, last):
    finish = [] if first else FINISH

    def score(t):
        return [("A_logits", t), ("A_bias", t), ("A_max", t), ("A_exp", t)]

    def attend(t, following):
        ahead = score(t + 1) if following else [None] * 4
        turn_o = ("A_turn_o", t - 1) if t not in (0, 4) else None
        turn_p2 = ("A_turn_p2", t) if t >= 4 else None
        steps = [ahead[0], ("A_turn_p", t), ahead[1], turn_p2, turn_o, ahead[2], ("A_values", t), ahead[3], ("A_scale", t)]
        return [step for step in steps if step]

    grams = [("D_decay", 0)]
    for t in range(1, TILES):
        grams += [("D_decay", t), ("D_gram", t - 1)]
    grams += [("D_gram", TILES - 1)]
    turns = [("D_gates", 0), ("D_keys", 0)] + [("D_turn", i) for i in range(5)]
    rows = [] if last else [("N_rows", 0), ("N_tails", 0)]
    early = attend(0, True) + attend(1, True) + attend(2, True)
    taps = [] if last else [("N_tap", n) for n in range(3)]
    score0 = score(0)
    order = weave(turns, finish[:1] + score0[:3]) + [("A_gate", 0), score0[3]]
    order += weave(grams[:7], finish[1:] + rows) + weave(grams[7:], taps[:1] + weave(early, taps[1:]))
    order += [("D_first", g) for g in range(len(QUADS))]
    levels = [("D_level", s) for s in range(len(LEVEL_STEPS) + LAG)]
    split = len(levels) * 2 // 3
    fill = attend(3, False) + [("A_turn_o", 3), ("D_gate", 0)]
    if not last:
        fill = weave([("N_conv", i) for i in range(9)] + [("N_silu", n) for n in range(3)], fill)
    turned = [] if last else [("N_turn", t) for t in range(TILES)] + NORMS[:2]
    levels = weave(levels[:split], fill) + weave(levels[split:], turned)
    s = LEVEL_STEPS.index((SAMPLE_LEVELS - 1, 4)) + LAG + 4
    for step, every in (("D_solve_sample", 0), ("D_sample_state", 2), ("D_sample_turn", 3), ("D_sample_new", 1), ("D_sample_out", 2)):
        s += every
        levels.insert(levels.index(("D_level", s)), (step, 0))
    order += levels
    rest = ([] if last else [("N_done", 0)]) + score(4)
    for t in range(4, NT):
        rest += attend(t, t + 1 < NT)
    rest += [("A_turn_o", NT - 1)]
    if not last:
        k = len(rest) * 3 // 4
        rest = weave(rest[:k], NORMS[2:]) + rest[k:]
    states = [("D_solve", 0)]
    for t in range(NT):
        states += [("D_read", t)] + ([("D_solve", t + 1)] if t + 1 < NT else []) + [("D_state", t), ("D_square", t - 1 if t else NT)]
    return order + weave(states, rest) + [("D_square", NT - 1)]


OUT_BANKS = (5, 7, 6)
QUADS = [(0, 4), (4, 8), (8, 9)]
PAIRS5 = [(0, 2), (2, 4), (4, 6), (6, 8), (8, 9)]
LEVEL_STEPS = [(m, g) for m in range(1, LEVELS) for g in range(5) if g < 4 or m < SAMPLE_LEVELS]
LAG = 2
NORMS = [("N_squares", 0), ("N_sum", 0), ("N_sum", 1), ("N_norms", 0), ("N_unit", 0), ("N_unit", 1)]
PREPARE = [("N_rows", 1), ("N_tails", 0)] + [("N_tap", n) for n in range(3)] + [("N_conv", i) for i in range(9)] \
    + [("N_silu", n) for n in range(3)] + [("N_turn", t) for t in range(TILES)] + NORMS
FINISH = [("P_norms", 0)] + [("P_out", g) for g in range(3)]


def run_heads(nc, io, scratch, keep, ident):
    with ExitStack() as ctx:
        def sbt(name, shape, dt=F32):
            return ctx.enter_context(nc.sbuf_tensor(name, shape, dt))

        def signal(name, per):
            return Signal(ctx.enter_context(nc.semaphore(name)), per)

        proj, mix = scratch["proj"], scratch["mix"]
        K = keep
        ROWS = DEC_B * 3 + CONV
        conv_rows = sbt("conv_rows", [P, 3, P])
        cw = sbt("cw", [P, 3, ROWS])
        xin = sbt("xin", [P, 3, 3 + SEQ])
        xsm = sbt("xsm", [P, 3, DEC_B, 3 + DEC_T])
        tail = sbt("tail", [P, 3, 3 * (DEC_B + 1)])
        tailN = sbt("tailN", [3 * (DEC_B + 1), 3, P])
        y = sbt("y", [P, 3, TOK])
        nat = sbt("nat", [P, TILES, 3, P])
        qkT = sbt("qkT", [P, TILES, 2, P])
        ssq = sbt("ssq", [P, 3, TILES, 2])
        osq = sbt("osq", [P, 4, TILES])
        cur = sbt("cur", [P, GATES, TILES])
        vb, kbe, kd = (sbt(n, [P, TILES, P]) for n in ("vb", "kbe", "kd"))
        decays = sbt("decays", [P, 8, P])
        dd = [decays[:, 2 * i:2 * i + 2, :] for i in range(2)]
        de = [decays[:, 4 + 2 * i:6 + 2 * i, :] for i in range(2)]
        egl = sbt("egl", [P, NT + DEC_B])
        A = sbt("A", [P, TILES, P])
        Bm = [sbt(f"Bm{i}", [P, TILES, P]) for i in range(2)]
        TU = sbt("TU", [P, TILES, 2, P])
        WT = [sbt(f"WT{i}", [P, 2, P]) for i in range(LAG + 1)]
        qkd = sbt("qkd", [P, TILES, P])
        uw = sbt("uw", [P, TILES, 2, P])
        S = sbt("S", [P, P])
        Ss = sbt("Ss", [P, DEC_B, P])
        vn = sbt("vn", [P, P])
        vn_sample = sbt("vn_sample", [P, P])
        o = sbt("o", [P, TILES, P])
        zb, za, qa = sbt("zb", [P, TOK]), sbt("za", [P, SEQ]), sbt("qa", [P, SEQ])
        mixB = sbt("mixB", [P, TOK])
        wq = sbt("wq", [P, DEC_B, 2, DEC_T])
        swq = sbt("swq", [P, 2, P])
        vmask = decays
        o_sq = mixB[:, :].rearrange("p (t c) -> p t c", t=TILES)
        qk_sq = y[:, 0:2, :].rearrange("p n (t c) -> p t n c", t=TILES)
        lg = [sbt(f"lg{i}", [P, SEQ]) for i in range(2)]
        PT = [sbt(f"PT{i}", [P, NT, P]) for i in range(2)]
        am = sbt("am", [P, NT, 4])
        oN = sbt("oN", [P, P])
        mixA = sbt("mixA", [P, SEQ])
        big = ctx.enter_context(nc.psum_tensor("big", [P, 8, 512], F32))

        rows_loaded, x_loaded, qa_loaded, za_loaded, zb_loaded, s_loaded = (signal(n, k) for n, k in (
            ("rows_loaded", 32), ("x_loaded", 96), ("qa_loaded", 16), ("za_loaded", 16), ("zb_loaded", 16), ("s_loaded", 16)))
        mixa_stored, mixb_stored, state_stored, sm_stored, tail_stored = (signal(n, k) for n, k in (
            ("mixa_stored", 16), ("mixb_stored", 16), ("state_stored", 16), ("sm_stored", 16), ("tail_stored", 32)))
        rows_turned, rows_ready, pads_ready, taps, convolved, silued = (signal(n, k) for n, k in (
            ("rows_turned", 1), ("rows_ready", 1), ("pads_ready", 1), ("taps", 6), ("convolved", 18), ("silued", 3)))
        tails_ready, tails_turned, tails_out, nat_turned, nat_ready = (signal(n, k) for n, k in (
            ("tails_ready", 2), ("tails_turned", 1), ("tails_out", 1), ("nat_turned", TILES), ("nat_ready", TILES)))
        gates_cur, squares, norms, rooted, scaled, kv_scaled = (signal(n, k) for n, k in (
            ("gates_cur", 1), ("squares", 1), ("norms", 6), ("rooted", 1), ("scaled", 2), ("kv_scaled", 3)))
        qk_turned, qk_ready, cum_done, diff_ready, decay_ready, last_ready = (signal(n, k) for n, k in (
            ("qk_turned", 5), ("qk_ready", 5), ("cum_done", TILES), ("diff_ready", 2 * TILES), ("decay_ready", TILES), ("last_ready", TILES)))
        NS = len(LEVEL_STEPS)
        gram_done, a_ready, level_ready, b0_turned, tu_first = (signal(n, k) for n, k in (
            ("gram_done", TILES), ("a_ready", 2 * TILES), ("level_ready", 3 * LEVELS), ("b0_turned", 3), ("tu_first", 6)))
        wt_done, wt_ready, z_done, tu_ready = (signal(n, NS) for n in ("wt_done", "wt_ready", "z_done", "tu_ready"))
        uw_done, uw_ready, state_zero, ws_done, vn_ready, ds_done, s_ready = (signal(n, k) for n, k in (
            ("uw_done", NT), ("uw_ready", NT), ("state_zero", 1), ("ws_done", NT), ("vn_ready", NT), ("ds_done", NT), ("s_ready", NT)))
        oo_done, o1_ready, o_ready = signal("oo_done", NT), signal("o1_ready", TILES), signal("o_ready", TILES)
        solved_sample, uw_sample = signal("solved_sample", 1), signal("uw_sample", 3)
        sm_done, sm_out, sm_back, sm_vn, sm_mask, sm_ds, sm_state = (signal(n, k) for n, k in (
            ("sm_done", 1), ("sm_out", 1), ("sm_back", 1), ("sm_vn", 1), ("sm_mask", 1), ("sm_ds", 3), ("sm_state", DEC_B)))
        o_squares, o_norms, o_rooted, o_scaled, o_turned, zb_silu, mixb_ready = (signal(n, k) for n, k in (
            ("o_squares", TILES), ("o_norms", 2), ("o_rooted", 1), ("o_scaled", 1), ("o_turned", 3), ("zb_silu", 1), ("mixb_ready", 3)))
        PARTS = [(t, q) for t in range(NT) for q in range(0, t + 1, 4)]
        za_silu, lg_done, lg_ready, max_ready, bias_ready, exp_ready = (signal(n, k) for n, k in (
            ("za_silu", 1), ("lg_done", NT), ("lg_ready", NT), ("max_ready", NT + 1), ("bias_ready", NT), ("exp_ready", NT)))
        p_turned, p_ready = signal("p_turned", len(PARTS)), signal("p_ready", len(PARTS))
        pv_done, inv_ready, on_ready, on_turned, mixa_ready = (signal(n, NT) for n in ("pv_done", "inv_ready", "on_ready", "on_turned", "mixa_ready"))
        zeros_ready = ctx.enter_context(nc.semaphore("zeros_ready"))
        at = [sum((k + 1) * P for k in range(t)) for t in range(NT)]

        def wait(eng, sig, h, k):
            eng.wait_ge(sig.sem, sig.now(h, k))

        def wait_before(eng, sig, h, k):
            eng.wait_ge(sig.sem, sig.before(h, k))

        def part(t, q):
            return PARTS.index((t, q)) + 1

        def quad(b):
            return big[:, b, :].rearrange("p (t c) -> p t c", t=4)

        def run(order, steps, h):
            for name, k in order:
                if name in steps:
                    steps[name](h + {"N": 1, "P": -1}.get(name[0], 0), k)

        def over_heads(eng, steps):
            run(PREPARE, steps, -1)
            run(head_order(True, False), steps, 0)
            with eng.Fori(1, H - 1) as h:
                run(head_order(False, False), steps, h)
            run(head_order(False, True), steps, H - 1)
            run(FINISH, steps, H)

        with nc.Block() as block:
            @block.sync
            def _(sp):
                for sig in (mixa_stored, mixb_stored, state_stored, sm_stored, tail_stored, rows_loaded, x_loaded, qa_loaded, za_loaded, zb_loaded, s_loaded):
                    sp.sem_inc(sig.sem, sig.per)

                def load_x(h):
                    wait_before(sp, rows_turned, h, 1)
                    sp.dma_start(conv_rows[0:3 * DEC_B, :, :], io["state_conv"].rearrange("a b j (n c) -> (a b j) n c", n=3)[:, :, bass.ds(h * P, P)]).then_inc(rows_loaded.sem, 16)
                    sp.dma_start(conv_rows[3 * DEC_B:ROWS, :, :], io["conv_w"].rearrange("a j (n c) -> (a j) n c", n=3)[:, :, bass.ds(h * P, P)]).then_inc(rows_loaded.sem, 16)
                    wait_before(sp, convolved, h, 18)
                    wait_before(sp, tails_ready, h, 2)
                    for n in range(3):
                        rows = proj[bass.ds(h * P + (C_B + n * H * P), P), :]
                        sp.dma_start(xin[:, n, 3:], rows[:, 0:SEQ]).then_inc(x_loaded.sem, 16)
                        sp.dma_start(xsm[:, n, :, 3:], rows[:, SEQ:TOK].rearrange("p (b t) -> p b t", b=DEC_B)).then_inc(x_loaded.sem, 16)

                def load_qa(h):
                    wait_before(sp, lg_done, h, NT)
                    sp.dma_start(qa[:, :], proj[bass.ds(h * P + C_Q, P), 0:SEQ]).then_inc(qa_loaded.sem, 16)

                def load_za(h):
                    wait_before(sp, mixa_ready, h, NT)
                    sp.dma_start(za[:, :], proj[bass.ds(h * P + C_Z, P), 0:SEQ]).then_inc(za_loaded.sem, 16)

                def load_zb(h):
                    wait_before(sp, mixb_ready, h, 3)
                    sp.dma_start(zb[:, :], proj[bass.ds(h * P + C_ZB, P), :]).then_inc(zb_loaded.sem, 16)

                def load_state(h):
                    wait_before(sp, sm_stored, h, 16)
                    sp.dma_start(Ss[:, :, :], io["state_delta"].rearrange("a b h k v -> k (a h) b v")[:, bass.ds(h, 1), :, :].rearrange("k h b v -> k (h b) v")).then_inc(s_loaded.sem, 16)

                def store_tails(h):
                    wait(sp, tails_out, h, 1)
                    sp.dma_start(io["new_conv_prompt"].rearrange("a b j (n c) -> (a b j) n c", n=3)[:, :, bass.ds(h * P, P)], tailN[3 * DEC_B:, :, :]).then_inc(tail_stored.sem, 16)
                    sp.dma_start(io["new_conv_sample"].rearrange("a b j (n c) -> (a b j) n c", n=3)[:, :, bass.ds(h * P, P)], tailN[0:3 * DEC_B, :, :]).then_inc(tail_stored.sem, 16)

                def store(h):
                    wait(sp, sm_state, h, DEC_B)
                    sp.dma_start(io["new_delta_sample"].rearrange("a b h k v -> k (a h) b v")[:, bass.ds(h, 1), :, :].rearrange("k h b v -> k (h b) v"), Ss[:, :, :]).then_inc(sm_stored.sem, 16)

                def store_mixa(h):
                    wait(sp, mixa_ready, h, NT)
                    sp.dma_start(mix[bass.ds(h * P, P), 0:SEQ], mixA[:, :]).then_inc(mixa_stored.sem, 16)

                def store_state(h):
                    wait(sp, s_ready, h, NT)
                    sp.dma_start(io["new_delta_prompt"].rearrange("a b h k v -> k (a b h) v")[:, bass.ds(h, 1), :], S[:, :].unsqueeze(1)).then_inc(state_stored.sem, 16)

                def store_mixb(h):
                    wait(sp, mixb_ready, h, 3)
                    sp.dma_start(mix[bass.ds(h * P + H * P, P), :], mixB[:, :]).then_inc(mixb_stored.sem, 16)

                sp.wait_ge(zeros_ready, 2)
                load_x(0)
                load_qa(0)
                load_za(0)
                store_tails(0)

                def head(h, last=False, load=True):
                    load_zb(h)
                    load_state(h)
                    if not last:
                        store_tails(h + 1)
                    store(h)
                    if load:
                        load_x(h + 2)
                    if not last:
                        load_qa(h + 1)
                    store_mixa(h)
                    if not last:
                        load_za(h + 1)
                    store_state(h)

                load_x(1)
                head(0)
                with sp.Fori(1, H - 2) as h:
                    store_mixb(h - 1)
                    head(h)
                store_mixb(H - 3)
                head(H - 2, load=False)
                store_mixb(H - 2)
                head(H - 1, last=True, load=False)
                store_mixb(H - 1)
                for sig in (mixa_stored, mixb_stored, state_stored, sm_stored, tail_stored):
                    sp.wait_ge(sig.sem, sig.now(H - 1, sig.per))

            @block.gpsimd
            def _(pool):
                for sig in (kv_scaled, level_ready, sm_mask):
                    pool.sem_inc(sig.sem, sig.per)
                bc = lambda g: cur[:, g, :].unsqueeze(2).to_broadcast([P, TILES, P])

                def scale_keys(h, _k):
                    wait(pool, scaled, h, 2)
                    wait(pool, gates_cur, h, 1)
                    wait_before(pool, oo_done, h, NT)
                    wait_before(pool, kv_scaled, h, 3)
                    pool.tensor_tensor(kbe[:, :, :], nat[:, :, 1, :], bc(G_BETA_EXP), ALU.mult).then_inc(kv_scaled.sem, 1)
                    pool.tensor_tensor(kd[:, :, :], nat[:, :, 1, :], bc(G_REST), ALU.mult).then_inc(kv_scaled.sem, 1)
                    pool.tensor_tensor(vb[:, :, :], nat[:, :, 2, :], bc(G_BETA), ALU.mult).then_inc(kv_scaled.sem, 1)

                def level(h, m, g):
                    lo, hi = QUADS[g]
                    n = hi - lo
                    if m >= 2:
                        wait(pool, level_ready, h, 3 * (m - 2) + g + 1)
                    pool.tensor_tensor(Bm[m % 2][:, lo:hi, :], A[:, lo:hi, :], K["level"][:, m, :].unsqueeze(1).to_broadcast([P, n, P]), ALU.mult).then_inc(level_ready.sem, 1)

                def first(h, g):
                    wait(pool, a_ready, h, 2 * QUADS[g][1])
                    if g == 0:
                        wait_before(pool, level_ready, h, 3 * LEVELS)
                        wait_before(pool, wt_done, h, NS)
                    level(h, 0, g)

                def levels(h, s):
                    if s == 0:
                        for g in range(3):
                            level(h, 1, g)
                        wait(pool, tu_first, h, 6)
                        for g in range(3):
                            level(h, 2, g)
                    for m in range(3, LEVELS):
                        if s == max(i for i, (mm, _) in enumerate(LEVEL_STEPS) if mm == m - 2) + 1:
                            wait(pool, wt_done, h, s)
                            for g in range(3):
                                level(h, m, g)

                def sample_mask(h, _k):
                    wait(pool, sm_vn, h, 1)
                    pool.tensor_tensor(vmask[:, :, :], vn_sample[:, :].unsqueeze(1).to_broadcast([P, DEC_B, P]), K["segcol"][:, :].unsqueeze(2).to_broadcast([P, DEC_B, P]), ALU.mult).then_inc(sm_mask.sem, 1)

                pool.memset(xin[:, :, 0:3], 0.0).then_inc(zeros_ready, 1)
                pool.memset(conv_rows[:, :, :], 0.0).then_inc(zeros_ready, 1)
                over_heads(pool, {"D_keys": scale_keys, "D_first": first, "D_level": levels, "D_sample_out": sample_mask})

            @block.scalar
            def _(act):
                for sig in (rows_ready, taps, silued, tails_ready, tails_out, nat_ready, squares, rooted, qk_ready, decay_ready, last_ready, wt_ready, uw_ready, uw_sample,
                            o1_ready, sm_out, o_squares, o_rooted, zb_silu, za_silu, exp_ready, p_ready):
                    act.sem_inc(sig.sem, sig.per)
                act.wait_ge(zeros_ready, 2)
                do = nc.scalar.activation
                copy = lambda out, in_, **kw: nc.scalar.activation(out, in_, ACT.Copy, **kw)

                def rows(h, _k):
                    wait(act, rows_turned, h, 1)
                    copy(cw[:, :, :], big[:, 5, 0:3 * P].rearrange("p (n c) -> p n c", n=3)[:, :, 0:ROWS]).then_inc(rows_ready.sem, 1)

                def tails(h, _k):
                    wait(act, x_loaded, h, 96)
                    wait_before(act, tails_turned, h, 1)
                    copy(tail[:, :, 0:3 * DEC_B].rearrange("p n (b j) -> p n b j", b=DEC_B), xsm[:, :, :, DEC_T:]).then_inc(tails_ready.sem, 1)
                    copy(tail[:, :, 3 * DEC_B:], xin[:, :, SEQ:]).then_inc(tails_ready.sem, 1)
                    wait(act, tails_turned, h, 1)
                    act.wait_ge(tail_stored.sem, tail_stored.before(h, 32))
                    copy(tailN[:, :, :], big[0:27, 5, 0:3 * P].rearrange("p (n c) -> p n c", n=3)).then_inc(tails_out.sem, 1)

                def tap(h, n):
                    if n == 0:
                        wait(act, pads_ready, h, 1)
                        wait_before(act, norms, h, 6)
                    w = cw[:, n, 3 * DEC_B:3 * DEC_B + 1]
                    copy(y[:, n, 0:SEQ], xin[:, n, 0:SEQ], scale=w).then_inc(taps.sem, 1)
                    copy(y[:, n, SEQ:].rearrange("p (b t) -> p b t", b=DEC_B), xsm[:, n, :, 0:DEC_T], scale=w).then_inc(taps.sem, 1)

                def silu(h, n):
                    wait(act, convolved, h, 6 * n + 6)
                    do(y[:, n, :], y[:, n, :], ACT.Silu).then_inc(silued.sem, 1)

                def natural(h, t):
                    if t == 0:
                        wait_before(act, kv_scaled, h, 3)
                    wait(act, nat_turned, h, t + 1)
                    copy(nat[:, t, :, :], big[:, 5, 0:3 * P].rearrange("p (n c) -> p n c", n=3)).then_inc(nat_ready.sem, 1)

                def head_squares(h, _k):
                    wait(act, nat_ready, h, TILES)
                    do(qk_sq, nat[:, :, 0:2, :], ACT.Square).then_inc(squares.sem, 1)

                def root(h, _k):
                    wait(act, norms, h, 4)
                    do(ssq[:, 1, :, :], ssq[:, 2, :, :], ACT.Sqrt).then_inc(rooted.sem, 1)

                def qk_out(h, i):
                    k = min(2, TILES - 2 * i)
                    wait(act, qk_turned, h, i + 1)
                    copy(qkT[:, 2 * i:2 * i + k, :, :], quad(i % 2)[:, 0:2 * k, :].rearrange("p (t n) c -> p t n c", n=2)).then_inc(qk_ready.sem, 1)

                def decay(h, t):
                    wait(act, diff_ready, h, 2 * t + 2)
                    if t >= 2:
                        wait(act, a_ready, h, 2 * t - 2)
                    do(de[t % 2][:, :, :], dd[t % 2][:, :, :], ACT.Exp).then_inc(decay_ready.sem, 1)
                    cum = big[:, 2 + t % 2, :]
                    if t < NT:
                        do(egl[:, t:t + 1], cum[:, P - 1:P], ACT.Exp).then_inc(last_ready.sem, 1)
                    else:
                        do(egl[:, NT:], cum[:, 0:P].rearrange("p (b t) -> p b t", t=DEC_T)[:, :, DEC_T - 1], ACT.Exp).then_inc(last_ready.sem, 1)

                def level(h, s):
                    if s < NS:
                        lo, hi = PAIRS5[LEVEL_STEPS[s][1]]
                        wait(act, wt_done, h, s + 1)
                        if s > LAG:
                            wait(act, z_done, h, s - LAG)
                        copy(WT[s % (LAG + 1)][:, 0:hi - lo, :], quad(s % 2)[:, 0:hi - lo, :]).then_inc(wt_ready.sem, 1)

                def gate_a(h, _k):
                    wait(act, za_loaded, h, 16)
                    do(za[:, :], za[:, :], ACT.Silu).then_inc(za_silu.sem, 1)

                def gate_b(h, _k):
                    wait(act, zb_loaded, h, 16)
                    do(zb[:, :], zb[:, :], ACT.Silu).then_inc(zb_silu.sem, 1)

                def solve(h, t):
                    wait(act, uw_done, h, t + 1)
                    copy(uw[:, t, :, :], big[:, 1, 0:2 * P].rearrange("p (n c) -> p n c", n=2)).then_inc(uw_ready.sem, 1)

                def solve_sample(h, _k):
                    wait(act, solved_sample, h, 1)
                    copy(wq[:, :, 0, :], big[:, 4, P:2 * P].rearrange("p (b t) -> p b t", b=DEC_B)).then_inc(uw_sample.sem, 1)
                    copy(wq[:, :, 1, :], qkT[:, NT, 0, :].rearrange("p (b t) -> p b t", b=DEC_B)).then_inc(uw_sample.sem, 1)
                    copy(uw[:, NT, 0, :], big[:, 4, 0:P]).then_inc(uw_sample.sem, 1)

                def sample_state(h, _k):
                    wait(act, sm_done, h, 1)
                    copy(swq[:, :, :].rearrange("p n (b t) -> p b n t", b=DEC_B), big[:, 4, 0:2 * P].rearrange("p (b n t) -> p b n t", b=DEC_B, n=2)).then_inc(sm_out.sem, 1)

                def sample_new(h, _k):
                    wait(act, sm_vn, h, 1)
                    wait_before(act, o_turned, h, 3)
                    copy(o[:, NT, :], big[:, 4, P:2 * P], scale=cur[:, G_EXP, NT:TILES]).then_inc(o1_ready.sem, 1)

                def state(h, t):
                    wait(act, oo_done, h, t + 1)
                    copy(o[:, t, :], big[:, 2 + t % 2, 0:P], scale=cur[:, G_EXP, t:t + 1]).then_inc(o1_ready.sem, 1)

                def square(h, t):
                    wait(act, o_ready, h, 1 if t == NT else t + 2)
                    if t == NT:
                        wait_before(act, mixb_stored, h, 16)
                    do(o_sq[:, t, :], o[:, t, :], ACT.Square, accum_out=osq[:, 0, t:t + 1]).then_inc(o_squares.sem, 1)

                def out_root(h, _k):
                    wait(act, o_norms, h, 2)
                    do(osq[:, 3, :], osq[:, 2, :], ACT.Sqrt).then_inc(o_rooted.sem, 1)

                def exps(h, t):
                    w = (t + 1) * P
                    wait(act, bias_ready, h, t + 1)
                    do(lg[t % 2][:, 0:w], lg[t % 2][:, 0:w], ACT.Exp, scale=SCALE, bias=am[:, t, 1:2], accum_out=am[:, t, 2:3]).then_inc(exp_ready.sem, 1)

                def p_out(h, t, q=0):
                    k = min(4, t + 1 - q)
                    wait(act, p_turned, h, part(t, q))
                    if q == 0 and t >= 2:
                        wait(act, pv_done, h, t - 1)
                    copy(PT[t % 2][:, q:q + k, :], quad(6)[:, 0:k, :]).then_inc(p_ready.sem, 1)

                over_heads(act, {
                    "N_rows": rows, "N_tails": tails, "N_tap": tap, "N_silu": silu, "N_turn": natural,
                    "N_squares": head_squares, "N_norms": root, "D_turn": qk_out, "D_solve_sample": solve_sample, "D_decay": decay, "D_level": level,
                    "D_gate": gate_b, "A_gate": gate_a, "D_solve": solve, "D_sample_state": sample_state, "D_sample_new": sample_new,
                    "D_state": state, "D_square": square, "P_norms": out_root,
                    "A_exp": exps, "A_turn_p": p_out, "A_turn_p2": lambda h, t: p_out(h, t, 4)})

            @block.tensor
            def _(pe):
                for sig in (rows_turned, tails_turned, nat_turned, qk_turned, cum_done, gram_done, b0_turned, wt_done, z_done, uw_done, solved_sample, ws_done, ds_done,
                            oo_done, sm_done, sm_back, sm_ds, o_turned, lg_done, p_turned, pv_done, on_turned):
                    pe.sem_inc(sig.sem, sig.per)

                def rows(h, at_start):
                    wait(pe, rows_loaded, h, 32)
                    if not at_start:
                        wait_before(pe, mixb_ready, h - 1, 3)
                    wait_before(pe, nat_ready, h, TILES)
                    for n in range(3):
                        last = pe.transpose(big[:, 5, n * P:(n + 1) * P], conv_rows[:, n, :], ident[:, :])
                    last.then_inc(rows_turned.sem, 1)

                def tails(h, _k):
                    wait(pe, tails_ready, h, 2)
                    wait(pe, rows_ready, h, 1)
                    for n in range(3):
                        last = pe.transpose(big[0:27, 5, n * P:(n + 1) * P], tail[:, n, :], ident[:, :])
                    last.then_inc(tails_turned.sem, 1)

                def natural(h, t):
                    if t == 0:
                        wait(pe, silued, h, 3)
                        wait(pe, tails_out, h, 1)
                    else:
                        wait(pe, nat_ready, h, t)
                    for n in range(3):
                        last = pe.transpose(big[:, 5, n * P:(n + 1) * P], y[:, n, t * P:(t + 1) * P], ident[:, :])
                    last.then_inc(nat_turned.sem, 1)

                def logits_of(kv):
                    def logits(h, t):
                        w = (t + 1) * P
                        if t == 0:
                            wait(pe, qa_loaded, h, 16)
                            wait_before(pe, lg_ready, h, NT)
                        else:
                            wait(pe, lg_ready, h, t)
                        if t == 4:
                            wait(pe, o_ready, h, 1)
                        for c in range(0, w, 512):
                            e = min(512, w - c)
                            o_ = big[:, 4 + c // 512, 0:e]
                            pe.matmul(o_, K["identb"][:, :], K["mask"][:, at[t] + c:at[t] + c + e], start=True, stop=False)
                            last = pe.matmul(o_, qa[:, t * P:(t + 1) * P], K["kT"][:, kv, c:c + e], start=False, stop=True)
                        last.then_inc(lg_done.sem, 1)
                    return logits

                def turn_p(h, t, q=0):
                    wait(pe, exp_ready, h, t + 1)
                    if t == 0:
                        wait_before(pe, mixb_ready, h, 3)
                    if t == 4 and q == 0:
                        wait(pe, sm_state, h, DEC_B)
                    if q or t:
                        wait(pe, p_ready, h, part(t, q) - 1)
                    for kb in range(q, min(q + 4, t + 1)):
                        last = pe.transpose(quad(6)[:, kb - q, :], lg[t % 2][:, kb * P:(kb + 1) * P], ident[:, :])
                    last.then_inc(p_turned.sem, 1)

                def values_of(kv):
                    def values(h, t):
                        wait(pe, p_ready, h, part(t, t // 4 * 4))
                        if t:
                            wait(pe, mixa_ready, h, t)
                        for kb in range(t + 1):
                            last = pe.matmul(big[:, 7, 0:P], PT[t % 2][:, kb, :], K["vN"][:, kb, kv, :], start=(kb == 0), stop=(kb == t))
                        last.then_inc(pv_done.sem, 1)
                    return values

                def turn_o(h, t):
                    wait(pe, on_ready, h, t + 1)
                    pe.transpose(big[:, 7, P:2 * P], oN[:, :], ident[:, :]).then_inc(on_turned.sem, 1)

                def qk_turn(h, i):
                    if i == 0:
                        wait(pe, scaled, h, 2)
                        wait_before(pe, s_ready, h, NT)
                        wait_before(pe, lg_ready, h, NT)
                        wait_before(pe, uw_ready, h, NT)
                    if i >= 2:
                        wait(pe, qk_ready, h, i - 1)
                    for k in range(min(2, TILES - 2 * i)):
                        for n in range(2):
                            last = pe.transpose(quad(i % 2)[:, 2 * k + n, :], nat[:, 2 * i + k, n, :], ident[:, :])
                    last.then_inc(qk_turned.sem, 1)

                def decay(h, t):
                    if t == 0:
                        wait(pe, gates_cur, h, 1)
                        wait_before(pe, o_ready, h, TILES)
                    if t >= 2:
                        wait(pe, last_ready, h, t - 1)
                    pe.matmul(big[:, 2 + t % 2, 0:P], cur[:, G_LOG, t:t + 1].to_broadcast([P, P]), K["cum"][:, int(t == NT), :], start=True, stop=True).then_inc(cum_done.sem, 1)
                    if t == 0:
                        wait(pe, qk_ready, h, 5)
                    if t >= 2:
                        wait(pe, a_ready, h, 2 * t - 2)
                    pe.matmul(big[:, t % 2, 0:2 * P], qkT[:, t, 1, :], qkT[:, t, :, :], start=True, stop=True).then_inc(gram_done.sem, 1)

                def first(h, g):
                    lo, hi = QUADS[g]
                    wait(pe, level_ready, h, g + 1)
                    if g == 0:
                        wait(pe, last_ready, h, TILES)
                    if g == 2:
                        wait(pe, tu_first, h, 2)
                    for t in range(lo, hi):
                        last = pe.transpose(quad(2 + g % 2)[:, t - lo, :], Bm[0][:, t, :], ident[:, :])
                    last.then_inc(b0_turned.sem, 1)

                def level(h, s):
                    if s < NS:
                        m, g = LEVEL_STEPS[s]
                        lo, hi = PAIRS5[g]
                        if m == 1:
                            wait(pe, tu_first, h, 2 * (g // 2 + 1))
                        else:
                            wait(pe, tu_ready, h, LEVEL_STEPS.index((m - 1, g)) + 1)
                        wait(pe, level_ready, h, 3 * m + g // 2 + 1)
                        if s < 2:
                            wait(pe, a_ready, h, 2 * TILES)
                        else:
                            wait(pe, wt_ready, h, s - 1)
                        for t in range(lo, hi):
                            last = pe.matmul(quad(s % 2)[:, t - lo, :], Bm[m % 2][:, t, :], TU[:, t, 1, :], start=True, stop=True)
                        last.then_inc(wt_done.sem, 1)
                    if s >= LAG:
                        r = s - LAG
                        m, g = LEVEL_STEPS[r]
                        lo, hi = PAIRS5[g]
                        wait(pe, wt_ready, h, r + 1)
                        if r < 2:
                            wait(pe, tu_first, h, 6)
                        else:
                            wait(pe, tu_ready, h, r - 1)
                        for t in range(lo, hi):
                            z = big[:, 2 + r % 2, (t - lo) * 2 * P:(t - lo + 1) * 2 * P]
                            if m < LEVELS - 1:
                                pe.matmul(z[:, 0:P], WT[r % (LAG + 1)][:, t - lo, :], TU[:, t, 0, :], start=True, stop=True)
                            last = pe.matmul(z[:, P:2 * P], TU[:, t, 0, :], WT[r % (LAG + 1)][:, t - lo, :], start=True, stop=True)
                        last.then_inc(z_done.sem, 1)

                def solve(h, t):
                    if t == 0:
                        wait(pe, tu_ready, h, NS)
                        wait(pe, wt_ready, h, NS)
                    else:
                        wait(pe, uw_ready, h, t)
                    pe.matmul(big[:, 1, 0:P], TU[:, t, 1, :], vb[:, t, :], start=True, stop=True)
                    pe.matmul(big[:, 1, P:2 * P], kbe[:, t, :], TU[:, t, 1, :], start=True, stop=True).then_inc(uw_done.sem, 1)

                def solve_sample(h, _k):
                    wait(pe, tu_ready, h, LEVEL_STEPS.index((SAMPLE_LEVELS - 1, 4)) + 1)
                    wait(pe, kv_scaled, h, 3)
                    wait(pe, lg_ready, h, 4)
                    wait(pe, mixa_ready, h, 4)
                    pe.matmul(big[:, 4, 0:P], TU[:, NT, 1, :], vb[:, NT, :], start=True, stop=True)
                    pe.matmul(big[:, 4, P:2 * P], kbe[:, NT, :], TU[:, NT, 1, :], start=True, stop=True).then_inc(solved_sample.sem, 1)

                def sample_state(h, _k):
                    wait(pe, s_loaded, h, 16)
                    wait(pe, uw_sample, h, 3)
                    for b in range(DEC_B):
                        last = pe.matmul(big[:, 4, b * 2 * DEC_T:(b + 1) * 2 * DEC_T], Ss[:, b, :], wq[:, b, :, :], start=True, stop=True)
                    last.then_inc(sm_done.sem, 1)

                def sample_turn(h, _k):
                    wait(pe, sm_out, h, 1)
                    pe.transpose(big[:, 4, 0:P], swq[:, 0, :], ident[:, :])
                    pe.transpose(big[:, 4, P:2 * P], swq[:, 1, :], ident[:, :]).then_inc(sm_back.sem, 1)

                def sample_out(h, _k):
                    wait(pe, sm_vn, h, 1)
                    wait(pe, o1_ready, h, 1)
                    pe.matmul(big[:, 4, 0:P], qkd[:, NT, :], vn_sample[:, :], start=True, stop=True).then_inc(sm_ds.sem, 1)
                    wait(pe, sm_mask, h, 1)
                    for half in range(2):
                        pe.matmul(big[:, 6 + half, :], kd[:, NT, :], vmask[:, 4 * half:4 * half + 4, :], start=True, stop=True).then_inc(sm_ds.sem, 1)

                def read(h, t):
                    wait(pe, uw_ready, h, t + 1)
                    if t == 0:
                        wait(pe, state_zero, h, 1)
                    else:
                        wait(pe, s_ready, h, t)
                    pe.matmul(big[:, 0, 0:P], uw[:, t, 1, :], S[:, :], start=True, stop=True).then_inc(ws_done.sem, 1)
                    if t >= 2:
                        wait(pe, o_ready, h, t)
                    pe.matmul(big[:, 2 + t % 2, 0:P], qkT[:, t, 0, :], S[:, :], start=True, stop=True)

                def state(h, t):
                    wait(pe, vn_ready, h, t + 1)
                    pe.matmul(big[:, 0, P:2 * P], kd[:, t, :], vn[:, :], start=True, stop=True).then_inc(ds_done.sem, 1)
                    pe.matmul(big[:, 2 + t % 2, P:2 * P], qkd[:, t, :], vn[:, :], start=True, stop=True).then_inc(oo_done.sem, 1)

                def prepared(h, _k):
                    wait(pe, nat_ready, h, TILES)

                def out(h, g):
                    lo, hi = QUADS[g]
                    if g == 0:
                        wait(pe, o_scaled, h, 1)
                        wait(pe, lg_ready, h, NT)
                        wait(pe, p_ready, h, len(PARTS))
                        wait(pe, mixa_ready, h, NT)
                    for t in range(lo, hi):
                        last = pe.transpose(quad(OUT_BANKS[g])[:, t - lo, :], o[:, t, :], ident[:, :])
                    last.then_inc(o_turned.sem, 1)

                def steps(kv):
                    return {
                        "N_rows": rows, "N_tails": tails, "N_turn": natural, "A_logits": logits_of(kv), "A_turn_p": turn_p, "A_turn_p2": lambda h, t: turn_p(h, t, 4),
                        "A_values": values_of(kv), "A_turn_o": turn_o, "D_turn": qk_turn, "D_decay": decay, "D_first": first,
                        "D_level": level, "D_solve": solve, "D_sample_state": sample_state, "D_sample_turn": sample_turn,
                        "D_sample_out": sample_out, "D_read": read, "D_state": state, "P_out": out, "D_solve_sample": solve_sample, "N_done": prepared}

                run(PREPARE, steps(0), -1)
                run(head_order(True, False), steps(0), 0)
                with pe.Fori(1, GROUP) as h:
                    run(head_order(False, False), steps(0), h)
                with pe.Fori(GROUP, H - 1) as h:
                    run(head_order(False, False), steps(1), h)
                run(head_order(False, True), steps(1), H - 1)
                run(FINISH, steps(1), H)

            @block.vector
            def _(dve):
                for sig in (pads_ready, convolved, norms, gates_cur, scaled, diff_ready, a_ready, tu_first, tu_ready, state_zero, vn_ready, s_ready, o_ready,
                            sm_vn, sm_state, o_norms, o_scaled, mixb_ready, max_ready, lg_ready, bias_ready, inv_ready, on_ready, mixa_ready):
                    dve.sem_inc(sig.sem, sig.per)
                V = nc.vector

                def conv(h, i):
                    n, j = i // 3, i % 3 + 1
                    w = cw[:, n, 3 * DEC_B + j:3 * DEC_B + j + 1]
                    wait(dve, taps, h, 2 * n + 2)
                    if j > 1:
                        wait(dve, convolved, h, 6 * n + 2 * (j - 1))
                    V.scalar_tensor_tensor(out=y[:, n, 0:SEQ], in0=xin[:, n, j:j + SEQ], scalar=w, in1=y[:, n, 0:SEQ], op0=ALU.mult, op1=ALU.add).then_inc(convolved.sem, 1)
                    ys = y[:, n, SEQ:].rearrange("p (b t) -> p b t", b=DEC_B)
                    V.scalar_tensor_tensor(out=ys, in0=xsm[:, n, :, j:j + DEC_T], scalar=w, in1=ys, op0=ALU.mult, op1=ALU.add).then_inc(convolved.sem, 1)

                def rows(h, _k):
                    wait(dve, rows_ready, h, 1)
                    V.tensor_copy(xsm[:, :, :, 0:3], cw[:, :, 0:3 * DEC_B].rearrange("p n (b j) -> p n b j", b=DEC_B)).then_inc(pads_ready.sem, 1)

                def bias(h, t):
                    w = (t + 1) * P
                    if t == 0:
                        wait_before(dve, max_ready, h, NT + 1)
                        wait_before(dve, p_turned, h, len(PARTS))
                    wait(dve, lg_done, h, t + 1)
                    if t >= 2:
                        wait(dve, p_turned, h, part(t - 1, 0) - 1)
                    src = big[:, 4:6, :].rearrange("p b c -> p (b c)")[:, 0:w]
                    V.tensor_tensor(lg[t % 2][:, 0:w], src, K["alibi"][:, SEQ - w:SEQ], ALU.add).then_inc(lg_ready.sem, 1)

                def biggest(h, t):
                    w = (t + 1) * P
                    wait(dve, lg_ready, h, t + 1)
                    V.tensor_reduce(am[:, t, 0:1], lg[t % 2][:, 0:w], AX_X, ALU.max).then_inc(max_ready.sem, 1)
                    wait(dve, max_ready, h, t + 1)
                    V.tensor_scalar(am[:, t, 1:2], am[:, t, 0:1], -SCALE, None, ALU.mult).then_inc(bias_ready.sem, 1)
                    if t == NT - 1:
                        V.tensor_scalar(K["alibi"][:, :], K["alibi"][:, :], 2.0 ** (-8.0 / H), None, ALU.mult).then_inc(max_ready.sem, 1)

                def values(h, t):
                    wait(dve, exp_ready, h, t + 1)
                    V.reciprocal(am[:, t, 3:4], am[:, t, 2:3]).then_inc(inv_ready.sem, 1)

                def scale(h, t):
                    wait(dve, inv_ready, h, t + 1)
                    wait(dve, pv_done, h, t + 1)
                    V.tensor_scalar(oN[:, :], big[:, 7, 0:P], am[:, t, 3:4], None, ALU.mult).then_inc(on_ready.sem, 1)

                def turn_o(h, t):
                    if t == 0:
                        wait(dve, za_silu, h, 1)
                        wait_before(dve, mixa_stored, h, 16)
                    wait(dve, on_turned, h, t + 1)
                    V.tensor_tensor(mixA[:, t * P:(t + 1) * P], big[:, 7, P:2 * P], za[:, t * P:(t + 1) * P], ALU.mult).then_inc(mixa_ready.sem, 1)

                def gates(h, _k):
                    wait_before(dve, o_ready, h, TILES)
                    wait_before(dve, kv_scaled, h, 3)
                    V.tensor_copy(cur[:, :, :], K["gates"][:, bass.ds(h, 1), :, :].rearrange("p h g t -> p (h g) t")).then_inc(gates_cur.sem, 1)

                def sums(h, n):
                    wait(dve, squares, h, 1)
                    V.tensor_reduce(ssq[:, 0, :, n], qk_sq[:, :, n, :], AX_X, ALU.add).then_inc(norms.sem, 1)

                def head_norms(h, _k):
                    wait(dve, norms, h, 2)
                    V.tensor_scalar(ssq[:, 1, :, :], ssq[:, 0, :, :], EPS, None, ALU.add).then_inc(norms.sem, 1)
                    wait(dve, norms, h, 3)
                    V.reciprocal(ssq[:, 2, :, :], ssq[:, 1, :, :]).then_inc(norms.sem, 1)

                def unit(h, n):
                    if n == 0:
                        wait(dve, rooted, h, 1)
                        V.tensor_scalar(ssq[:, 2, :, 0], ssq[:, 1, :, 0], SCALE, None, ALU.mult).then_inc(norms.sem, 1)
                        V.tensor_copy(ssq[:, 2, :, 1], ssq[:, 1, :, 1]).then_inc(norms.sem, 1)
                    wait(dve, norms, h, 6)
                    V.tensor_tensor(nat[:, :, n, :], nat[:, :, n, :], ssq[:, 2, :, n].unsqueeze(2).to_broadcast([P, TILES, P]), ALU.mult).then_inc(scaled.sem, 1)

                def decay(h, t):
                    s = int(t == NT)
                    cum = big[:, 2 + t % 2, 0:P]
                    gc = cur[:, G_CUM, t:t + 1]
                    wait(dve, cum_done, h, t + 1)
                    if t == 0:
                        wait(dve, gates_cur, h, 1)
                    if t >= 2:
                        wait(dve, decay_ready, h, t - 1)
                    V.scalar_tensor_tensor(out=dd[t % 2][:, 0, :], in0=cum, scalar=gc, in1=K["dmT"][:, s, :], op0=ALU.subtract, op1=ALU.add).then_inc(diff_ready.sem, 1)
                    V.scalar_tensor_tensor(out=dd[t % 2][:, 1, :], in0=cum, scalar=gc, in1=K["dmN"][:, s, :], op0=ALU.subtract, op1=ALU.subtract, reverse1=True).then_inc(diff_ready.sem, 1)

                def gram(h, t):
                    if t == 0:
                        wait_before(dve, level_ready, h, 3 * LEVELS)
                    wait(dve, gram_done, h, t + 1)
                    wait(dve, decay_ready, h, t + 1)
                    V.tensor_tensor(qkd[:, t, :], big[:, t % 2, 0:P], de[t % 2][:, 0, :], ALU.mult).then_inc(a_ready.sem, 1)
                    V.scalar_tensor_tensor(out=A[:, t, :], in0=big[:, t % 2, P:2 * P], scalar=cur[:, G_BETA, t:t + 1], in1=de[t % 2][:, 1, :], op0=ALU.mult, op1=ALU.mult).then_inc(a_ready.sem, 1)

                def first(h, g):
                    lo, hi = QUADS[g]
                    eye = ident[:, :].unsqueeze(1).to_broadcast([P, hi - lo, P])
                    wait(dve, level_ready, h, g + 1)
                    V.tensor_tensor(TU[:, lo:hi, 0, :], eye, Bm[0][:, lo:hi, :], ALU.subtract).then_inc(tu_first.sem, 1)
                    wait(dve, b0_turned, h, g + 1)
                    V.tensor_tensor(TU[:, lo:hi, 1, :], eye, quad(2 + g % 2)[:, 0:hi - lo, :], ALU.subtract).then_inc(tu_first.sem, 1)

                def level(h, s):
                    if s < LAG:
                        return
                    r = s - LAG
                    m, g = LEVEL_STEPS[r]
                    lo, hi = PAIRS5[g]
                    wait(dve, z_done, h, r + 1)
                    if m == 1:
                        wait(dve, tu_first, h, 6)
                    else:
                        wait(dve, tu_ready, h, LEVEL_STEPS.index((m - 1, g)) + 1)
                    z = big[:, 2 + r % 2, :].rearrange("p (t n c) -> p t n c", t=2, n=2)[:, 0:hi - lo, :, :]
                    n0 = 0 if m < LEVELS - 1 else 1
                    V.tensor_tensor(TU[:, lo:hi, n0:, :], TU[:, lo:hi, n0:, :], z[:, :, n0:, :], ALU.subtract).then_inc(tu_ready.sem, 1)

                def sample_new(h, _k):
                    wait(dve, sm_back, h, 1)
                    V.tensor_tensor(vn_sample[:, :], uw[:, NT, 0, :], big[:, 4, 0:P], ALU.subtract).then_inc(sm_vn.sem, 1)

                def sample_out(h, _k):
                    wait(dve, sm_ds, h, 1)
                    wait(dve, o1_ready, h, 1)
                    V.tensor_tensor(o[:, NT, :], o[:, NT, :], big[:, 4, 0:P], ALU.add).then_inc(o_ready.sem, 1)
                    wait_before(dve, state_stored, h, 16)
                    V.memset(S[:, :], 0.0).then_inc(state_zero.sem, 1)
                    for b in range(DEC_B):
                        wait(dve, sm_ds, h, 2 + b // 4)
                        V.scalar_tensor_tensor(out=Ss[:, b, :], in0=Ss[:, b, :], scalar=egl[:, NT + b:NT + b + 1], in1=big[:, 6 + b // 4, b % 4 * P:(b % 4 + 1) * P], op0=ALU.mult, op1=ALU.add).then_inc(sm_state.sem, 1)

                def add_out(h, t):
                    wait(dve, o1_ready, h, t + 2)
                    V.tensor_tensor(o[:, t, :], o[:, t, :], big[:, 2 + t % 2, P:2 * P], ALU.add).then_inc(o_ready.sem, 1)

                def read(h, t):
                    wait(dve, ws_done, h, t + 1)
                    if t:
                        wait(dve, oo_done, h, t)
                    V.tensor_tensor(vn[:, :], uw[:, t, 0, :], big[:, 0, 0:P], ALU.subtract).then_inc(vn_ready.sem, 1)

                def state(h, t):
                    wait(dve, ds_done, h, t + 1)
                    if t == 0:
                        wait(dve, state_zero, h, 1)
                    V.scalar_tensor_tensor(out=S[:, :], in0=S[:, :], scalar=egl[:, t:t + 1], in1=big[:, 0, P:2 * P], op0=ALU.mult, op1=ALU.add).then_inc(s_ready.sem, 1)
                    if t:
                        add_out(h, t - 1)
                    if t == NT - 1:
                        add_out(h, t)

                def out_norms(h, _k):
                    wait(dve, o_squares, h, TILES)
                    V.tensor_scalar(osq[:, 1, :], osq[:, 0, :], 1.0 / HD, EPS, ALU.mult, ALU.add).then_inc(o_norms.sem, 1)
                    wait(dve, o_norms, h, 1)
                    V.reciprocal(osq[:, 2, :], osq[:, 1, :]).then_inc(o_norms.sem, 1)
                    wait(dve, o_rooted, h, 1)
                    V.tensor_tensor(o[:, :, :], o[:, :, :], osq[:, 3, :].unsqueeze(2).to_broadcast([P, TILES, P]), ALU.mult).then_inc(o_scaled.sem, 1)

                def out(h, g):
                    lo, hi = QUADS[g]
                    wait(dve, o_turned, h, g + 1)
                    if g == 0:
                        wait(dve, zb_silu, h, 1)
                    V.scalar_tensor_tensor(out=mixB[:, lo * P:hi * P], in0=big[:, OUT_BANKS[g], 0:(hi - lo) * P], scalar=K["gnw"][:, 0:1], in1=zb[:, lo * P:hi * P], op0=ALU.mult, op1=ALU.mult).then_inc(mixb_ready.sem, 1)

                over_heads(dve, {
                    "N_rows": rows, "N_conv": conv, "A_bias": bias, "A_max": biggest, "A_values": values, "A_scale": scale, "A_turn_o": turn_o,
                    "D_gates": gates, "N_sum": sums, "N_norms": head_norms, "N_unit": unit, "D_decay": decay, "D_gram": gram, "D_first": first, "D_level": level,
                    "D_sample_new": sample_new, "D_sample_out": sample_out, "D_read": read, "D_state": state, "P_norms": out_norms, "P_out": out})


def kept_tensors(nc, ctx):
    shapes = {
        "kT": ([P, KV, SEQ], F32), "vN": ([P, NT, KV, P], F32), "mask": ([P, NT * (NT + 1) // 2 * P], BF16),
        "alibi": ([P, SEQ], F32), "gates": ([P, H, GATES, TILES], F32), "cum": ([P, 2, P], F32),
        "dmT": ([P, 2, P], F32), "dmN": ([P, 2, P], F32), "level": ([P, LEVELS, P], F32),
        "segcol": ([P, DEC_B], F32), "gnw": ([P, 1], F32), "identb": ([P, P], BF16),
    }
    return {n: ctx.enter_context(nc.sbuf_tensor("keep_" + n, s, dt)) for n, (s, dt) in shapes.items()}


def attend_samples(nc, io, scratch, keep, ident):
    with ExitStack() as ctx:
        def sbt(name, shape, dt=F32):
            return ctx.enter_context(nc.sbuf_tensor(name, shape, dt))

        def sem(name):
            return ctx.enter_context(nc.semaphore(name))

        proj, mix = scratch["proj"], scratch["mix"]
        PAIRS = DEC_B // 2
        UNITS = KV * PAIRS
        SLICES = ((0, P), (P, P), (2 * P, DEC_T))
        qs = sbt("qs", [P, KV, DEC_B, GROUP, DEC_T])
        zs = sbt("zs", [P, H, P])
        kn = sbt("kn", [P, DEC_B, 2, KV * P])
        kT = sbt("kTs", [P, KV, DEC_B, LS])
        vn = sbt("vns", [P, DEC_B, 2, KV * P])
        vnew = sbt("vnew", [DEC_T, DEC_B, KV * P])
        smask = sbt("smask", [P, LS], BF16)
        rsel = sbt("rsel", [P, PAIRS, P], BF16)
        row = sbt("row", [P, LS], mybir.dt.int32)
        rowf = sbt("rowf", [P, LS])
        col = sbt("col", [P, 4])
        pcol = sbt("pcol", [P, 1], mybir.dt.int32)
        bval = sbt("bval", [P, 3, DEC_B])
        alibi = sbt("alibis", [P, KV, LS])
        lg = [sbt(f"lgs{i}", [P, LS]) for i in range(2)]
        pT = [sbt(f"pT{i}", [P, 3, P]) for i in range(2)]
        am = sbt("ams", [P, UNITS, 4])
        oN = [sbt(f"oNs{i}", [P, P]) for i in range(2)]
        mixS = sbt("mixS", [P, H, P])
        bank = [ctx.enter_context(nc.psum_tensor(f"sb{i}", [P, 512], F32)) for i in range(8)]

        cache_loaded, q_loaded, z_loaded, v_loaded, tabled, stepped, silued = map(
            sem, ["cache_loaded", "qs_loaded", "zs_loaded", "v_loaded", "s_tabled", "s_stepped", "s_silued"])
        turned, moved, lg_done, lg_ready, bias_ready, exp_ready = map(
            sem, ["s_turned", "s_moved", "s_lg_done", "s_lg_ready", "s_bias_ready", "s_exp_ready"])
        p_turned, p_ready, pv_done, inv_ready, on_ready, on_turned, mixed, stored = map(
            sem, ["s_p_turned", "s_p_ready", "s_pv_done", "s_inv_ready", "s_on_ready", "s_on_turned", "s_mixed", "s_stored"])

        with nc.Block() as block:
            @block.sync
            def _(sp):
                sp.dma_start(kn[:, :, :, :], io["cache_k"].rearrange("a b (n p) k d -> p (a b) n (k d)", p=P)).then_inc(cache_loaded, 16)
                for k in range(KV):
                    for b in range(DEC_B):
                        at = SEQ + b * DEC_T
                        rows = slice(C_Q + k * GROUP * P, C_Q + (k + 1) * GROUP * P)
                        sp.dma_start(qs[:, k, b, :, :], proj[rows, at:at + DEC_T].rearrange("(g d) t -> d g t", d=P)).then_inc(q_loaded, 16)
                    sp.dma_start(kT[:, k, :, PAST:], proj[C_K + k * P:C_K + (k + 1) * P, SEQ:].rearrange("d (b t) -> d b t", b=DEC_B)).then_inc(q_loaded, 16)
                sp.dma_start(smask[:, :], scratch["sample_mask"]).then_inc(q_loaded, 16)
                sp.dma_start(vn[:, :, :, :], io["cache_v"].rearrange("a b (n p) k d -> p (a b) n (k d)", p=P)).then_inc(v_loaded, 16)
                sp.dma_start(vnew[:, :, :], io["new_v_sample"].rearrange("a b t k d -> t (a b) (k d)")).then_inc(v_loaded, 16)
                sp.dma_start(zs[:, :, :], proj[C_Z:C_QI, SEQ:].rearrange("(h d) t -> d h t", d=P)).then_inc(z_loaded, 16)
                sp.wait_ge(mixed, UNITS)
                sp.dma_start(mix[0:H * P, SEQ:].rearrange("(h d) t -> d h t", d=P), mixS[:, :, :]).then_inc(stored, 16)
                sp.wait_ge(stored, 16)

            @block.gpsimd
            def _(pool):
                n = [0]

                def chain(instruction):
                    n[0] += 1
                    instruction.then_inc(tabled, 1)
                    pool.wait_ge(tabled, n[0])

                chain(pool.memset(rsel[:, :, :], 0.0))
                chain(pool.affine_select(out=rsel[:, :, :], in_=rsel[:, :, :], compare_op=ALU.not_equal, fill=1.0, base=0,
                                         pattern=[[-2 * DEC_T, PAIRS], [-DEC_T, 2], [0, GROUP], [-1, DEC_T]], channel_multiplier=1))
                chain(pool.iota(row[:, :], pattern=[[-1, LS]], base=PAST, channel_multiplier=0))
                chain(pool.iota(pcol[:, :], pattern=[[0, 1]], base=0, channel_multiplier=1))
                for b in range(DEC_B):
                    chain(pool.memset(bval[:, 0, b:b + 1], float(DEC_T * b)))
                    chain(pool.memset(bval[:, 1, b:b + 1], 2.0 ** (-8.0 * (b % GROUP + 1) / H) / SCALE))

            @block.tensor
            def _(pe):
                pe.wait_ge(cache_loaded, 16)
                for k in range(KV):
                    for pair in range(PAIRS):
                        i = k * PAIRS + pair
                        if i >= 4:
                            pe.wait_ge(moved, i - 3)
                        for j in range(4):
                            last = pe.transpose(bank[i % 4][:, j * P:(j + 1) * P], kn[:, 2 * pair + j // 2, j % 2, k * P:(k + 1) * P], ident[:, :])
                        last.then_inc(turned, 1)
                pe.wait_ge(q_loaded, 16 * (KV * (DEC_B + 1) + 1))
                pe.wait_ge(tabled, 2)
                pe.wait_ge(moved, UNITS)

                def logits(i):
                    k, pair = divmod(i, PAIRS)
                    if i >= 2:
                        pe.wait_ge(lg_ready, i - 1)
                    o = bank[i % 2]
                    pe.matmul(o[:, 0:LS], rsel[:, pair, :], smask[:, :], start=True, stop=False, skip_group_check=True)
                    for j in range(2):
                        b = 2 * pair + j
                        last = pe.matmul(o[j * 64:(j + 1) * 64, 0:LS], qs[:, k, b, :, :].rearrange("p g t -> p (g t)"), kT[:, k, b, :],
                                         start=False, stop=True, skip_group_check=True)
                    last.then_inc(lg_done, 1)

                def turn_out(i):
                    pe.wait_ge(on_ready, i + 1)
                    if i >= 2:
                        pe.wait_ge(mixed, i - 1)
                    pe.transpose(bank[6 + i % 2][:, 0:P], oN[i % 2][:, :], ident[:, :]).then_inc(on_turned, 1)

                logits(0)
                for i in range(UNITS):
                    k, pair = divmod(i, PAIRS)
                    if i + 1 < UNITS:
                        logits(i + 1)
                    pe.wait_ge(exp_ready, i + 1)
                    if i >= 2:
                        pe.wait_ge(p_ready, i - 1)
                    for n, (c, w) in enumerate(SLICES):
                        last = pe.transpose(bank[2 + i % 2][0:w, n * P:(n + 1) * P], lg[i % 2][:, c:c + w], ident[:, :])
                    last.then_inc(p_turned, 1)
                    if i:
                        turn_out(i - 1)
                    pe.wait_ge(p_ready, i + 1)
                    if i == 0:
                        pe.wait_ge(v_loaded, 32)
                    if i >= 2:
                        pe.wait_ge(on_ready, i - 1)
                    for j in range(2):
                        b = 2 * pair + j
                        for n, (c, w) in enumerate(SLICES):
                            v = vn[:, b, n, k * P:(k + 1) * P] if n < 2 else vnew[:, b, k * P:(k + 1) * P]
                            last = pe.matmul(bank[4 + i % 2][j * 64:(j + 1) * 64, 0:P], pT[i % 2][0:w, n, j * 64:(j + 1) * 64], v,
                                             start=(n == 0), stop=(n == 2))
                    last.then_inc(pv_done, 1)
                turn_out(UNITS - 1)

            @block.scalar
            def _(act):
                for i in range(UNITS):
                    k, pair = divmod(i, PAIRS)
                    act.wait_ge(turned, i + 1)
                    nc.scalar.activation(kT[:, k, 2 * pair:2 * pair + 2, 0:PAST], bank[i % 4][:, :].rearrange("d (b s) -> d b s", b=2), ACT.Copy).then_inc(moved, 1)
                act.wait_ge(z_loaded, 16)
                nc.scalar.activation(zs[:, :, :], zs[:, :, :], ACT.Silu).then_inc(silued, 1)
                for i in range(UNITS):
                    act.wait_ge(bias_ready, i + 1)
                    nc.scalar.activation(lg[i % 2][:, :], lg[i % 2][:, :], ACT.Exp, scale=SCALE, bias=am[:, i, 1:2], accum_out=am[:, i, 2:3]).then_inc(exp_ready, 1)
                    act.wait_ge(p_turned, i + 1)
                    if i >= 2:
                        act.wait_ge(pv_done, i - 1)
                    nc.scalar.activation(pT[i % 2][:, 0:2, :], bank[2 + i % 2][:, 0:2 * P].rearrange("p (n c) -> p n c", n=2), ACT.Copy)
                    nc.scalar.activation(pT[i % 2][0:DEC_T, 2, :], bank[2 + i % 2][0:DEC_T, 2 * P:3 * P], ACT.Copy).then_inc(p_ready, 1)

            @block.vector
            def _(dve):
                n = [0]

                def chain(instruction):
                    n[0] += 1
                    instruction.then_inc(stepped, 1)
                    dve.wait_ge(stepped, n[0])

                V = nc.vector
                dve.wait_ge(tabled, 4 + 2 * DEC_B)
                chain(V.tensor_tensor(bval[:, 2, :], bval[:, 0, :], keep["segcol"][:, :], ALU.mult))
                chain(V.tensor_reduce(col[:, 0:1], bval[:, 2, :], AX_X, ALU.add))
                chain(V.tensor_tensor(bval[:, 2, :], bval[:, 1, :], keep["segcol"][:, :], ALU.mult))
                chain(V.tensor_reduce(col[:, 2:3], bval[:, 2, :], AX_X, ALU.add))
                chain(V.tensor_copy(col[:, 3:4], pcol[:, :]))
                chain(V.tensor_tensor(col[:, 1:2], col[:, 3:4], col[:, 0:1], ALU.subtract))
                chain(V.tensor_copy(rowf[:, :], row[:, :]))
                chain(V.tensor_scalar(rowf[:, :], rowf[:, :], col[:, 1:2], None, ALU.add))
                chain(V.scalar_tensor_tensor(out=rowf[:, :], in0=rowf[:, :], scalar=-1.0, in1=rowf[:, :], op0=ALU.mult, op1=ALU.min))
                for k in range(KV):
                    chain(V.tensor_scalar(alibi[:, k, :], rowf[:, :], col[:, 2:3], 2.0 ** (-8.0 * k * GROUP / H), ALU.mult, ALU.mult))

                def add(i):
                    dve.wait_ge(lg_done, i + 1)
                    if i >= 2:
                        dve.wait_ge(p_turned, i - 1)
                    V.tensor_tensor(lg[i % 2][:, :], bank[i % 2][:, 0:LS], alibi[:, i // PAIRS, :], ALU.add).then_inc(lg_ready, 1)
                    dve.wait_ge(lg_ready, i + 1)
                    chain(V.tensor_reduce(am[:, i, 0:1], lg[i % 2][:, :], AX_X, ALU.max))
                    V.tensor_scalar(am[:, i, 1:2], am[:, i, 0:1], -SCALE, None, ALU.mult).then_inc(bias_ready, 1)

                def gate(i):
                    k, pair = divmod(i, PAIRS)
                    dve.wait_ge(on_turned, i + 1)
                    out = mixS[:, k * GROUP:(k + 1) * GROUP, 2 * DEC_T * pair:2 * DEC_T * (pair + 1)].rearrange("d g (b t) -> d b g t", b=2)
                    z = zs[:, k * GROUP:(k + 1) * GROUP, 2 * DEC_T * pair:2 * DEC_T * (pair + 1)].rearrange("d g (b t) -> d b g t", b=2)
                    V.tensor_tensor(out, bank[6 + i % 2][:, 0:P].rearrange("d (b g t) -> d b g t", b=2, g=GROUP), z, ALU.mult).then_inc(mixed, 1)

                add(0)
                dve.wait_ge(silued, 1)
                for i in range(UNITS):
                    if i + 1 < UNITS:
                        add(i + 1)
                    if i:
                        gate(i - 1)
                    dve.wait_ge(exp_ready, i + 1)
                    V.reciprocal(am[:, i, 3:4], am[:, i, 2:3]).then_inc(inv_ready, 1)
                    dve.wait_ge(inv_ready, i + 1)
                    dve.wait_ge(pv_done, i + 1)
                    V.tensor_scalar(oN[i % 2][:, :], bank[4 + i % 2][:, 0:P], am[:, i, 3:4], None, ALU.mult).then_inc(on_ready, 1)
                gate(UNITS - 1)


THIRD_TILES = 3
NW = 512


def project_out(nc, io, scratch):
    with ExitStack() as ctx:
        def sbt(name, shape, dt=F32):
            return ctx.enter_context(nc.sbuf_tensor(name, shape, dt))

        def sem(name):
            return ctx.enter_context(nc.semaphore(name))

        mix = scratch["mix"]
        THIRDS = TILES // THIRD_TILES
        CB = D // NW
        QUARTERS = KT // CK
        CH = 4
        TT = THIRD_TILES * P
        raw = [sbt(f"oraw{i}", [P, CK, NW]) for i in range(2)]
        wH = [sbt(f"owH{i}", [P, CK, NW], F32R) for i in range(2)]
        wL = [sbt(f"owL{i}", [P, CK, NW], F32R) for i in range(2)]
        mraw = [sbt(f"mraw{i}", [P, KT // 4, TT]) for i in range(2)]
        mH = sbt("mH", [P, KT, TT], F32R)
        mL = sbt("mL", [P, KT, TT], F32R)
        x = [sbt(f"ox{i}", [P, THIRD_TILES, NW]) for i in range(2)]
        yv = sbt("yv", [P, THIRD_TILES, D])
        fw = sbt("fw", [P, D])
        squares = sbt("osquares", [P, D])
        stat = sbt("ostat", [P, THIRD_TILES, 4])
        bank = [ctx.enter_context(nc.psum_tensor(f"ob{i}", [P, NW], F32)) for i in range(2 * THIRD_TILES)]

        w_loaded = [sem(f"ow_loaded{i}") for i in range(2)]
        x_loaded = [sem(f"ox_loaded{i}") for i in range(2)]
        m_loaded = [sem(f"m_loaded{i}") for i in range(2)]
        fw_loaded = sem("fw_loaded")
        high_ready, low_ready, mhigh_ready, mlow_ready, chunk_used = map(sem, ["ohigh_ready", "olow_ready", "mhigh_ready", "mlow_ready", "ochunk_used"])
        block_done, added, squared, stepped, rooted, scaled, weighted, stored = map(
            sem, ["block_done", "added", "osquared", "ostepped", "orooted", "oscaled", "oweighted", "ystored"])
        w_view = io["w_out"].rearrange("a (k p) n -> (a p) k n", p=P)
        xp = io["x_prompt"].rearrange("b (t p) d -> p (b t) d", p=P)
        xs = io["x_sample"].rearrange("b t d -> (b t) d")
        yp = io["y_prompt"].rearrange("b (t p) d -> p (b t) d", p=P)
        ys = io["y_sample"].rearrange("b t d -> (b t) d")
        units = [(r, c) for r in range(THIRDS) for c in range(CB)]

        def quarter(j):
            return slice(j % QUARTERS * CK, (j % QUARTERS + 1) * CK)

        def split_before(n):
            r, ch = (n + 2) // (CB * CH), (n + 2) % (CB * CH)
            if n < CH:
                return [n] if n >= 0 else []
            return [r * QUARTERS + ch] if 0 < r < THIRDS and ch < QUARTERS else []

        with nc.Block() as block:
            @block.sync
            def _(sp):
                sp.dma_start(fw[:, :], io["final_norm_w"].rearrange("(a d) -> a d", a=1).to_broadcast([P, D])).then_inc(fw_loaded, 16)
                n = 0

                def load_mix(j):
                    r, q = j // QUARTERS, j % QUARTERS
                    if j >= 2:
                        sp.wait_ge(mlow_ready, j - 1)
                    rows = slice(q * CK * P, (q + 1) * CK * P)
                    sp.dma_start(mraw[j % 2][:, :, :], mix[rows, r * TT:(r + 1) * TT].rearrange("(k p) t -> p k t", p=P)).then_inc(m_loaded[j % 2], 16)

                for i, (r, c) in enumerate(units):
                    for ch in range(CH):
                        if n < 2:
                            load_mix(n)
                        if n >= 2:
                            sp.wait_ge(low_ready, n - 1)
                        sp.dma_start(raw[n % 2][:, :, :], w_view[:, ch * CK:(ch + 1) * CK, c * NW:(c + 1) * NW]).then_inc(w_loaded[n % 2], 16)
                        for j in split_before(n - 1):
                            if j + 2 < THIRDS * QUARTERS:
                                load_mix(j + 2)
                        n += 1
                    if i >= 2:
                        sp.wait_ge(added, THIRD_TILES * (i - 1))
                    cols = slice(c * NW, (c + 1) * NW)
                    if r < THIRDS - 1:
                        sp.dma_start(x[i % 2][:, :, :], xp[:, r * THIRD_TILES:(r + 1) * THIRD_TILES, cols]).then_inc(x_loaded[i % 2], 16)
                    else:
                        sp.dma_start(x[i % 2][:, 0:THIRD_TILES - 1, :], xp[:, r * THIRD_TILES:NT, cols]).then_inc(x_loaded[i % 2], 16)
                        sp.dma_start(x[i % 2][:, THIRD_TILES - 1, :], xs[:, cols]).then_inc(x_loaded[i % 2], 16)

            @block.gpsimd
            def _(pool):
                n = 0
                for i, (r, c) in enumerate(units):
                    for ch in range(CH):
                        pool.wait_ge(high_ready, n + 1)
                        pool.tensor_tensor(wL[n % 2][:, :, :], raw[n % 2][:, :, :], wH[n % 2][:, :, :].bitcast(F32), ALU.subtract).then_inc(low_ready, 1)
                        n += 1

            @block.scalar
            def _(act):
                n = 0

                def root(k):
                    act.wait_ge(stepped, 2 * (k + 1))
                    t = k % THIRD_TILES
                    nc.scalar.activation(stat[:, t, 3:4], stat[:, t, 2:3], ACT.Sqrt).then_inc(rooted, 1)

                def store(k):
                    act.wait_ge(weighted, k + 1)
                    act.dma_start(yp[:, k, :] if k < NT else ys, yv[:, k % THIRD_TILES, :]).then_inc(stored, 16)

                def high(n):
                    act.wait_ge(w_loaded[n % 2], 16 * (n // 2 + 1))
                    if n >= 2:
                        act.wait_ge(chunk_used, n - 1)
                    nc.scalar.activation(wH[n % 2][:, :, :], raw[n % 2][:, :, :], ACT.Copy).then_inc(high_ready, 1)

                for i, (r, c) in enumerate(units):
                    for ch in range(CH):
                        for j in split_before(n):
                            act.wait_ge(m_loaded[j % 2], 16 * (j // 2 + 1))
                            if n >= CH:
                                act.wait_ge(chunk_used, n - 1)
                            nc.scalar.activation(mH[:, quarter(j), :], mraw[j % 2][:, :, :], ACT.Copy).then_inc(mhigh_ready, 1)
                        high(n)
                        behind = n - r * CB * CH
                        if r and 1 <= behind <= THIRD_TILES:
                            root((r - 1) * THIRD_TILES + behind - 1)
                        if r and 2 <= behind <= THIRD_TILES + 1:
                            store((r - 1) * THIRD_TILES + behind - 2)
                        n += 1
                for k in range(TILES - THIRD_TILES, TILES):
                    root(k)
                    store(k)
                act.wait_ge(stored, 16 * TILES)

            @block.tensor
            def _(pe):
                n = 0
                for i, (r, c) in enumerate(units):
                    for ch in range(CH):
                        if c == 0:
                            pe.wait_ge(mlow_ready, r * QUARTERS + ch + 1)
                        pe.wait_ge(low_ready, n + 1)
                        for t in range(THIRD_TILES):
                            o = bank[i % 2 * THIRD_TILES + t][:, :]
                            if ch == 0 and i >= 2:
                                pe.wait_ge(added, THIRD_TILES * (i - 2) + t + 1)
                            for k in range(CK):
                                kk = ch * CK + k
                                a = slice(t * P, (t + 1) * P)
                                first, end = kk == 0, kk == KT - 1
                                pe.matmul(o, mL[:, kk, a], wH[n % 2][:, k, :], start=first, stop=False)
                                pe.matmul(o, mH[:, kk, a], wL[n % 2][:, k, :], start=False, stop=False)
                                last = pe.matmul(o, mH[:, kk, a], wH[n % 2][:, k, :], start=False, stop=end)
                        last.then_inc(chunk_used, 1)
                        n += 1

            @block.vector
            def _(dve):
                dve.wait_ge(fw_loaded, 16)
                V = nc.vector

                def split_low(n):
                    for j in split_before(n):
                        dve.wait_ge(mhigh_ready, j + 1)
                        V.tensor_tensor(mL[:, quarter(j), :], mraw[j % 2][:, :, :], mH[:, quarter(j), :].bitcast(F32), ALU.subtract).then_inc(mlow_ready, 1)

                for n in range(CH):
                    split_low(n)
                for i, (r, c) in enumerate(units):
                    if c == CB - 1:
                        for n in range(CH * i + 2, CH * i + 5):
                            split_low(n)
                    dve.wait_ge(x_loaded[i % 2], 16 * (i // 2 + 1) if r < THIRDS - 1 else 16 * (CB * (THIRDS - 1) // 2 + 2 * (i // 2 - CB * (THIRDS - 1) // 2 + 1)))
                    if r and c == 0:
                        dve.wait_ge(stored, 16 * THIRD_TILES * r)
                    for t in range(THIRD_TILES):
                        dve.wait_ge(chunk_used, CH * (i + 1))
                        V.tensor_tensor(yv[:, t, c * NW:(c + 1) * NW], bank[i % 2 * THIRD_TILES + t][:, :], x[i % 2][:, t, :], ALU.add).then_inc(added, 1)
                    if c == CB - 1:
                        split_low(CH * i + 5)
                        for t in range(THIRD_TILES):
                            k = r * THIRD_TILES + t
                            dve.wait_ge(added, THIRD_TILES * (i + 1))
                            V.tensor_tensor_reduce(out=squares[:, :], in0=yv[:, t, :], in1=yv[:, t, :], scale=1.0, scalar=0.0, op0=ALU.mult, op1=ALU.add, accum_out=stat[:, t, 0:1]).then_inc(squared, 1)
                            dve.wait_ge(squared, k + 1)
                            V.tensor_scalar(stat[:, t, 1:2], stat[:, t, 0:1], 1.0 / D, EPS, ALU.mult, ALU.add).then_inc(stepped, 1)
                            dve.wait_ge(stepped, 2 * k + 1)
                            V.reciprocal(stat[:, t, 2:3], stat[:, t, 1:2]).then_inc(stepped, 1)
                        for t in range(THIRD_TILES):
                            k = r * THIRD_TILES + t
                            dve.wait_ge(rooted, k + 1)
                            V.scalar_tensor_tensor(out=yv[:, t, :], in0=yv[:, t, :], scalar=stat[:, t, 3:4], in1=fw[:, :], op0=ALU.mult, op1=ALU.mult).then_inc(weighted, 1)


INPUTS = ["x_prompt", "x_sample", "cache_k", "cache_v", "cache_idx_k", "state_conv", "state_delta", "norm_w", "w_in",
          "conv_w", "a_log", "dt_bias", "gnorm_w", "w_out", "final_norm_w"]
OUTPUTS = [("y_prompt", (1, SEQ, D)), ("y_sample", (DEC_B, DEC_T, D)),
           ("new_k_prompt", (1, 1, SEQ, KV, HD)), ("new_v_prompt", (1, 1, SEQ, KV, HD)), ("new_idx_k_prompt", (1, 1, SEQ, ID)),
           ("new_conv_prompt", (1, 1, 3, 3 * H * HD)), ("new_delta_prompt", (1, 1, H, HD, HD)),
           ("new_k_sample", (1, DEC_B, DEC_T, KV, HD)), ("new_v_sample", (1, DEC_B, DEC_T, KV, HD)),
           ("new_idx_k_sample", (1, DEC_B, DEC_T, ID)), ("new_conv_sample", (1, DEC_B, 3, 3 * H * HD)),
           ("new_delta_sample", (1, DEC_B, H, HD, HD))]


def build(nc, io):
    scratch = {
        "proj": nc.dram_tensor("proj_scratch", (PROJ, TOK), F32, kind="Internal").ap(),
        "mask": nc.dram_tensor("mask_scratch", (NT, P, SEQ), BF16, kind="Internal").ap(),
        "sample_mask": nc.dram_tensor("sample_mask_scratch", (P, LS), BF16, kind="Internal").ap(),
        "mix": nc.dram_tensor("mix_scratch", (2 * H * P, TOK), F32, kind="Internal").ap(),
    }
    with ExitStack() as ctx:
        ident = ctx.enter_context(nc.sbuf_tensor("ident", [P, P], F32))
        with ExitStack() as inner:
            hH = inner.enter_context(nc.sbuf_tensor("hH", [P, KT, TOK], F32R))
            hL = inner.enter_context(nc.sbuf_tensor("hL", [P, KT, TOK], F32R))
            done_with = normalise_inputs(nc, io, hH, hL, ident)
            done_with = project_and_select(nc, io, scratch, hH, hL, ident, done_with)
        with ExitStack() as inner:
            keep = kept_tensors(nc, inner)
            prepare_heads(nc, io, scratch, keep, ident, done_with)
            run_heads(nc, io, scratch, keep, ident)
            attend_samples(nc, io, scratch, keep, ident)
        project_out(nc, io, scratch)


def kernel(**inputs):
    import numpy as np
    from concourse import bacc
    from concourse.bass_utils import run_bass_kernel_spmd

    nc = bacc.Bacc("TRN2", target_bir_lowering=False, num_devices=1)
    arrays, io = {}, {}
    for name in INPUTS:
        a = np.ascontiguousarray(inputs[name])
        arrays["in_" + name] = a
        io[name] = nc.dram_tensor("in_" + name, a.shape, mybir.dt.from_np(a.dtype), kind="ExternalInput").ap()
    for name, shape in OUTPUTS:
        io[name] = nc.dram_tensor("out_" + name, shape, F32, kind="ExternalOutput").ap()
    build(nc, io)
    result = run_bass_kernel_spmd(nc, [arrays], core_ids=[0])
    return tuple(result.results[0]["out_" + name] for name, _ in OUTPUTS)
```
